# Optimizing a Trainium2 kernel written in Bass

```python
import jax, jax.numpy as jnp
from jax import lax
import numpy as np

D_MODEL = 1024
BATCH = 1
SEQ = 512
DEPTH = 1
DEC_BATCH = 8
DEC_SEQ = 4
PAST_LEN = 2048
PAGE_SIZE = 128

HEAD_DIM = 64
N_SB_HEADS = 4
DIL_GROUPS = ((128, 1), (512, 4), (2048, 16))
N_DIL_GROUPS = 3
HEADS_PER_DIL_GROUP = 2
N_DIL_HEADS = N_DIL_GROUPS * HEADS_PER_DIL_GROUP
N_FOX_HEADS = 6
N_HEADS = N_SB_HEADS + N_DIL_HEADS + N_FOX_HEADS
N_KV_HEADS = N_SB_HEADS + N_FOX_HEADS
MIX_WIDTH = N_HEADS * HEAD_DIM
N_BRANCHES = 3
N_IN = 3 * MIX_WIDTH + N_FOX_HEADS + N_BRANCHES * D_MODEL
ATTN_SCALE = HEAD_DIM ** -0.5
ALIBI_MAX_EXP = 8.0
Q_BLOCK = 128
N_GROUPS = 4
EXPERTS_PER_GROUP = 4
N_EXPERTS = N_GROUPS * EXPERTS_PER_GROUP
TOP_K_FINE = 2
D_EXPERT = 256
N_MOD = 6
EPS = 1e-6

kernel_name = 'hybrid_sb_dilated_fox_hmoe_step'

def rms_norm(x, g):
    x32 = x.astype(jnp.float32)
    y = x32 * lax.rsqrt(jnp.mean(x32 * x32, axis=-1, keepdims=True) + EPS)
    return (y * g.astype(jnp.float32)).astype(x.dtype)

def alibi_slopes():
    expo = -ALIBI_MAX_EXP * np.arange(1, N_DIL_HEADS + 1) / N_DIL_HEADS
    return jnp.asarray(np.power(2.0, expo), dtype=jnp.float32).reshape(N_DIL_GROUPS, HEADS_PER_DIL_GROUP)

def split_heads(t):
    b, s = t.shape[:2]
    t_sb = t[:, :, :N_SB_HEADS]
    t_dil = t[:, :, N_SB_HEADS:N_SB_HEADS + N_DIL_HEADS].reshape(b, s, N_DIL_GROUPS, HEADS_PER_DIL_GROUP, HEAD_DIM)
    t_fox = t[:, :, N_SB_HEADS + N_DIL_HEADS:]
    return t_sb, t_dil, t_fox

def project_in(h, w_in, b_f):
    b, s, _ = h.shape
    z = h @ w_in
    qkv = z[..., :3 * MIX_WIDTH].reshape(b, s, 3, N_HEADS, HEAD_DIM)
    f_logit = z[..., 3 * MIX_WIDTH:3 * MIX_WIDTH + N_FOX_HEADS].astype(jnp.float32) + b_f.astype(jnp.float32)
    logf = jax.nn.log_sigmoid(f_logit)
    gates = jax.nn.sigmoid(z[..., 3 * MIX_WIDTH + N_FOX_HEADS:].astype(jnp.float32)).astype(h.dtype)
    gates = gates.reshape(b, s, N_BRANCHES, D_MODEL)
    return qkv[:, :, 0], qkv[:, :, 1], qkv[:, :, 2], logf, gates

def block_rows(t, start):
    return lax.dynamic_slice_in_dim(t, start, Q_BLOCK, axis=1)

def sweep_query_blocks(block_fn, seq_len):
    starts = jnp.arange(seq_len // Q_BLOCK, dtype=jnp.int32) * Q_BLOCK
    out = lax.map(block_fn, starts)
    out = jnp.moveaxis(out, 0, 1)
    return out.reshape(out.shape[0], seq_len, *out.shape[3:])

def stick_breaking_attention(q, k, v, q_pos, k_pos):
    z = jnp.einsum('bthd,bshd->bhts', q, k).astype(jnp.float32) * ATTN_SCALE
    causal = k_pos[None, :] < q_pos[:, None]
    log_stay = jnp.where(causal, jax.nn.log_sigmoid(-z), 0.0)
    log_after = lax.cumsum(log_stay, axis=3, reverse=True) - log_stay
    log_w = jnp.where(causal, jax.nn.log_sigmoid(z) + log_after, -jnp.inf)
    w = jnp.exp(log_w)
    return jnp.einsum('bhts,bshd->bthd', w.astype(v.dtype), v)

def forgetting_attention(q, k, v, cum_q, cum_k, q_pos, k_pos):
    s = jnp.einsum('bthd,bshd->bhts', q, k).astype(jnp.float32) * ATTN_SCALE
    s = s + jnp.moveaxis(cum_q, 2, 1)[..., :, None] - jnp.moveaxis(cum_k, 2, 1)[..., None, :]
    causal = k_pos[None, :] <= q_pos[:, None]
    p = jax.nn.softmax(jnp.where(causal, s, -jnp.inf), axis=-1)
    return jnp.einsum('bhts,bshd->bthd', p.astype(v.dtype), v)

def dilated_group_attention(q, k_ctx, v_ctx, q_idx, window, dilation, slopes):
    n_keys = window // dilation + 1
    dist = jnp.arange(n_keys, dtype=jnp.int32) * dilation
    idx = q_idx[:, None] - dist[None, :]
    valid = idx >= 0
    idx = jnp.clip(idx, 0, k_ctx.shape[1] - 1)
    kg = k_ctx[:, idx]
    vg = v_ctx[:, idx]
    s = jnp.einsum('bthd,btkhd->bhtk', q, kg).astype(jnp.float32) * ATTN_SCALE
    s = s - slopes[:, None, None] * dist.astype(jnp.float32)[None, None, :]
    s = jnp.where(valid, s, -jnp.inf)
    lse = jax.nn.logsumexp(s, axis=-1)
    p = jnp.exp(s - lse[..., None])
    o = jnp.einsum('bhtk,btkhd->bthd', p.astype(v_ctx.dtype), vg)
    return o, jnp.moveaxis(lse, 1, 2)

def merge_dilation_groups(outs, lses):
    wts = jax.nn.softmax(jnp.stack(lses), axis=0)
    return jnp.sum(wts[..., None].astype(outs[0].dtype) * jnp.stack(outs), axis=0)

def mix_prompt(q, k, v, logf, slopes):
    b, s = q.shape[:2]
    pos = jnp.arange(s, dtype=jnp.int32)
    q_sb, q_dil, q_fox = split_heads(q)
    k_sb, k_dil, k_fox = split_heads(k)
    v_sb, v_dil, v_fox = split_heads(v)
    cum = jnp.cumsum(logf, axis=1)

    def sb_block(start):
        qp = start + jnp.arange(Q_BLOCK, dtype=jnp.int32)
        return stick_breaking_attention(block_rows(q_sb, start), k_sb, v_sb, qp, pos)

    def fox_block(start):
        qp = start + jnp.arange(Q_BLOCK, dtype=jnp.int32)
        return forgetting_attention(block_rows(q_fox, start), k_fox, v_fox, block_rows(cum, start), cum, qp, pos)

    def dil_block(start):
        qp = start + jnp.arange(Q_BLOCK, dtype=jnp.int32)
        qb = block_rows(q_dil, start)
        outs, lses = [], []
        for g, (window, dilation) in enumerate(DIL_GROUPS):
            o, lse = dilated_group_attention(qb[:, :, g], k_dil[:, :, g], v_dil[:, :, g], qp, window, dilation, slopes[g])
            outs.append(o)
            lses.append(lse)
        return merge_dilation_groups(outs, lses)

    o_sb = sweep_query_blocks(sb_block, s)
    o_dil = sweep_query_blocks(dil_block, s)
    o_fox = sweep_query_blocks(fox_block, s)
    kv_rows = jnp.stack([jnp.concatenate([k_sb, k_fox], axis=2), jnp.concatenate([v_sb, v_fox], axis=2)], axis=2)
    bufs = tuple(jnp.stack([k_dil[:, :, g], v_dil[:, :, g]], axis=2)[:, s - min(window, s):]
                 for g, (window, _) in enumerate(DIL_GROUPS))
    return (o_sb, o_dil, o_fox), (kv_rows, logf.astype(q.dtype)) + bufs

def mix_sample(q, k, v, logf, kv_past, logf_past, bufs, slopes):
    t = q.shape[1]
    p = kv_past.shape[1]
    q_pos = p + jnp.arange(t, dtype=jnp.int32)
    k_pos = jnp.arange(p + t, dtype=jnp.int32)
    q_sb, q_dil, q_fox = split_heads(q)
    k_sb, k_dil, k_fox = split_heads(k)
    v_sb, v_dil, v_fox = split_heads(v)
    k_sb_all = jnp.concatenate([kv_past[:, :, 0, :N_SB_HEADS], k_sb], axis=1)
    v_sb_all = jnp.concatenate([kv_past[:, :, 1, :N_SB_HEADS], v_sb], axis=1)
    k_fox_all = jnp.concatenate([kv_past[:, :, 0, N_SB_HEADS:], k_fox], axis=1)
    v_fox_all = jnp.concatenate([kv_past[:, :, 1, N_SB_HEADS:], v_fox], axis=1)
    cum = jnp.cumsum(jnp.concatenate([logf_past.astype(jnp.float32), logf], axis=1), axis=1)
    o_sb = stick_breaking_attention(q_sb, k_sb_all, v_sb_all, q_pos, k_pos)
    o_fox = forgetting_attention(q_fox, k_fox_all, v_fox_all, cum[:, p:], cum, q_pos, k_pos)
    outs, lses, new_bufs = [], [], []
    for g, (window, dilation) in enumerate(DIL_GROUPS):
        buf = bufs[g]
        wb = buf.shape[1]
        ctx = jnp.concatenate([buf, jnp.stack([k_dil[:, :, g], v_dil[:, :, g]], axis=2)], axis=1)
        o, lse = dilated_group_attention(q_dil[:, :, g], ctx[:, :, 0], ctx[:, :, 1],
                                         wb + jnp.arange(t, dtype=jnp.int32), window, dilation, slopes[g])
        outs.append(o)
        lses.append(lse)
        new_bufs.append(ctx[:, t:])
    o_dil = merge_dilation_groups(outs, lses)
    kv_rows = jnp.stack([jnp.concatenate([k_sb, k_fox], axis=2), jnp.concatenate([v_sb, v_fox], axis=2)], axis=2)
    return (o_sb, o_dil, o_fox), (kv_rows, logf.astype(q.dtype)) + tuple(new_bufs)

def hier_moe(h, w_rg, b_rg, w_re, b_re, w1, w3, w2):
    b, s, d = h.shape
    x = h.reshape(b * s, d)
    n = x.shape[0]
    g_logits = (x @ w_rg).astype(jnp.float32) + b_rg.astype(jnp.float32)
    g_prob = jax.nn.softmax(g_logits, axis=-1)
    _, g_idx = lax.top_k(g_logits, 1)
    g_gate = jnp.take_along_axis(g_prob, g_idx, axis=-1)
    e_logits = ((x @ w_re).astype(jnp.float32) + b_re.astype(jnp.float32)).reshape(n, N_GROUPS, EXPERTS_PER_GROUP)
    sel = jnp.broadcast_to(g_idx[:, :, None], (n, 1, EXPERTS_PER_GROUP))
    e_logits = jnp.take_along_axis(e_logits, sel, axis=1)[:, 0]
    e_val, e_idx = lax.top_k(e_logits, TOP_K_FINE)
    e_gate = jax.nn.softmax(e_val, axis=-1) * g_gate
    expert = g_idx * EXPERTS_PER_GROUP + e_idx
    combine = jnp.sum(jax.nn.one_hot(expert, N_EXPERTS, dtype=jnp.float32) * e_gate[..., None], axis=1)
    hid = jax.nn.silu(jnp.einsum('nd,edf->nef', x, w1)) * jnp.einsum('nd,edf->nef', x, w3)
    hid = hid * combine[:, :, None].astype(hid.dtype)
    return jnp.einsum('nef,efd->nd', hid, w2).reshape(b, s, d)

def trunk_layer(x, c, lw, mix_fn):
    b, t, d = x.shape
    mod = (jax.nn.silu(c) @ lw['w_mod'] + lw['b_mod']).reshape(b, N_MOD, 1, d)
    shift1, scale1, gate1 = mod[:, 0], mod[:, 1], mod[:, 2]
    shift2, scale2, gate2 = mod[:, 3], mod[:, 4], mod[:, 5]
    h = rms_norm(x, lw['norm1']) * (1 + scale1) + shift1
    q, k, v, logf, gates = project_in(h, lw['w_in'], lw['b_f'])
    (o_sb, o_dil, o_fox), state = mix_fn(q, k, v, logf)
    merged = (gates[:, :, 0] * (o_sb.reshape(b, t, -1) @ lw['w_br_sb'])
              + gates[:, :, 1] * (o_dil.reshape(b, t, -1) @ lw['w_br_dil'])
              + gates[:, :, 2] * (o_fox.reshape(b, t, -1) @ lw['w_br_fox']))
    x = x + gate1 * (merged @ lw['w_o'])
    h2 = rms_norm(x, lw['norm2']) * (1 + scale2) + shift2
    x = x + gate2 * hier_moe(h2, lw['w_rg'], lw['b_rg'], lw['w_re'], lw['b_re'], lw['w1'], lw['w3'], lw['w2'])
    return x, state

def setup_inputs(seed: int = 0) -> dict:
    key = jax.random.key(seed)
    ks = jax.random.split(key, 32)
    f32 = jnp.float32
    D = D_MODEL
    n_pages = PAST_LEN // PAGE_SIZE
    n_used = DEC_BATCH * n_pages
    n_pool = n_used + max(1, n_used // 4)

    def nrm(k, shape, scale=1.0):
        return jax.random.normal(k, shape, f32) * scale

    dil_w = [min(w, PAST_LEN) for (w, _) in DIL_GROUPS]
    return {
        'x_prompt': nrm(ks[0], (BATCH, SEQ, D)),
        'x_sample': nrm(ks[1], (DEC_BATCH, DEC_SEQ, D)),
        'cache_kv': nrm(ks[2], (n_pool, DEPTH, PAGE_SIZE, 2, N_KV_HEADS, HEAD_DIM)),
        'cache_fox_logf': jax.nn.log_sigmoid(nrm(ks[3], (n_pool, DEPTH, PAGE_SIZE, N_FOX_HEADS))),
        'cache_dil1': nrm(ks[4], (DEC_BATCH, DEPTH, dil_w[0], 2, HEADS_PER_DIL_GROUP, HEAD_DIM)),
        'cache_dil2': nrm(ks[5], (DEC_BATCH, DEPTH, dil_w[1], 2, HEADS_PER_DIL_GROUP, HEAD_DIM)),
        'cache_dil3': nrm(ks[6], (DEC_BATCH, DEPTH, dil_w[2], 2, HEADS_PER_DIL_GROUP, HEAD_DIM)),
        'page_table': jax.random.permutation(ks[7], n_pool)[:n_used].reshape(DEC_BATCH, n_pages).astype(jnp.int32),
        'c_prompt': nrm(ks[8], (BATCH, D)),
        'c_sample': nrm(ks[9], (DEC_BATCH, D)),
        'norm1': 1.0 + nrm(ks[10], (DEPTH, D), 0.1),
        'norm2': 1.0 + nrm(ks[11], (DEPTH, D), 0.1),
        'w_mod': nrm(ks[12], (DEPTH, D, N_MOD * D), 0.5 * D ** -0.5),
        'b_mod': nrm(ks[13], (DEPTH, N_MOD * D), 0.02),
        'w_in': nrm(ks[14], (DEPTH, D, N_IN), D ** -0.5),
        'b_f': nrm(ks[15], (DEPTH, N_FOX_HEADS), 0.1),
        'w_br_sb': nrm(ks[16], (DEPTH, N_SB_HEADS * HEAD_DIM, D), (N_SB_HEADS * HEAD_DIM) ** -0.5),
        'w_br_dil': nrm(ks[17], (DEPTH, HEADS_PER_DIL_GROUP * HEAD_DIM, D), (HEADS_PER_DIL_GROUP * HEAD_DIM) ** -0.5),
        'w_br_fox': nrm(ks[18], (DEPTH, N_FOX_HEADS * HEAD_DIM, D), (N_FOX_HEADS * HEAD_DIM) ** -0.5),
        'w_o': nrm(ks[19], (DEPTH, D, D), D ** -0.5),
        'w_rg': nrm(ks[20], (DEPTH, D, N_GROUPS), D ** -0.5),
        'b_rg': nrm(ks[21], (DEPTH, N_GROUPS), 0.01),
        'w_re': nrm(ks[22], (DEPTH, D, N_EXPERTS), D ** -0.5),
        'b_re': nrm(ks[23], (DEPTH, N_EXPERTS), 0.01),
        'w1': nrm(ks[24], (DEPTH, N_EXPERTS, D, D_EXPERT), D ** -0.5),
        'w3': nrm(ks[25], (DEPTH, N_EXPERTS, D, D_EXPERT), D ** -0.5),
        'w2': nrm(ks[26], (DEPTH, N_EXPERTS, D_EXPERT, D), D_EXPERT ** -0.5),
        'norm_f': 1.0 + nrm(ks[27], (D,), 0.1),
    }

def stack_layers(states, i):
    return jnp.stack([st[i] for st in states], axis=1)

def reference(x_prompt, x_sample, cache_kv, cache_fox_logf, cache_dil1, cache_dil2, cache_dil3, page_table,
              c_prompt, c_sample, norm1, norm2, w_mod, b_mod, w_in, b_f, w_br_sb, w_br_dil, w_br_fox, w_o,
              w_rg, b_rg, w_re, b_re, w1, w3, w2, norm_f):
    slopes = alibi_slopes()
    dil_caches = (cache_dil1, cache_dil2, cache_dil3)
    n_seq = page_table.shape[0]
    xp, xs = x_prompt, x_sample
    p_states, s_states = [], []
    for l in range(DEPTH):
        lw = {'norm1': norm1[l], 'norm2': norm2[l], 'w_mod': w_mod[l], 'b_mod': b_mod[l], 'w_in': w_in[l],
              'b_f': b_f[l], 'w_br_sb': w_br_sb[l], 'w_br_dil': w_br_dil[l], 'w_br_fox': w_br_fox[l],
              'w_o': w_o[l], 'w_rg': w_rg[l], 'b_rg': b_rg[l], 'w_re': w_re[l], 'b_re': b_re[l],
              'w1': w1[l], 'w3': w3[l], 'w2': w2[l]}
        kv_past = cache_kv[page_table, l]
        kv_past = kv_past.reshape(n_seq, -1, *kv_past.shape[3:])
        lf_past = cache_fox_logf[page_table, l].reshape(n_seq, -1, N_FOX_HEADS)
        bufs = tuple(cd[:, l] for cd in dil_caches)
        xp, sp = trunk_layer(xp, c_prompt, lw, lambda q, k, v, lf: mix_prompt(q, k, v, lf, slopes))
        xs, ss = trunk_layer(xs, c_sample, lw,
                             lambda q, k, v, lf: mix_sample(q, k, v, lf, kv_past, lf_past, bufs, slopes))
        p_states.append(sp)
        s_states.append(ss)
    y_prompt = rms_norm(xp, norm_f)
    y_sample = rms_norm(xs, norm_f)
    return (y_prompt, y_sample,
            stack_layers(p_states, 0), stack_layers(p_states, 1), stack_layers(p_states, 2),
            stack_layers(p_states, 3), stack_layers(p_states, 4),
            stack_layers(s_states, 0), stack_layers(s_states, 1), stack_layers(s_states, 2),
            stack_layers(s_states, 3), stack_layers(s_states, 4))


_drawn_inputs = setup_inputs


def setup_inputs(seed=0):
    import zlib

    import numpy as np

    out = dict(_drawn_inputs(seed))
    spreads = {}
    factors = {'cache_fox_logf': 18.263, 'b_f': 3.415, 'b_rg': 64.0, 'b_re': 64.0}
    for name, (base, spread) in spreads.items():
        noise = np.random.default_rng([zlib.crc32(name.encode()), seed]).standard_normal(out[name].shape)
        drawn = base * np.exp(spread * noise) if base else spread * noise
        out[name] = __import__('jax').numpy.asarray(drawn.astype(out[name].dtype))
    for name, factor in factors.items():
        out[name] = (out[name] * factor).astype(out[name].dtype)
    return out
```

```python
import numpy as np
import concourse.bass as bass
from concourse import mybir
from contextlib import ExitStack

F32 = mybir.dt.float32
I32 = mybir.dt.int32
ALU = mybir.AluOpType
ACT = mybir.ActivationFunctionType
AX = mybir.AxisListType.X

P = 128
D = 1024
KD = D // P
SEQ = 512
NB = 8
NT = 4
TOK = SEQ + NB * NT
PAGES = 16
HD = 64
SCALE = HD ** -0.5
EPS = 1e-6
NEG = -1e30
MIX = 1024
QTILES = SEQ // P
NFOX = 6
NEXP = 16
DE = 256
PAIR_TILES = (0, 1, 5, 6, 7)
SLOPES = [[2.0 ** (-8.0 * (2 * g + h + 1) / 6) for h in range(2)] for g in range(3)]
DILATION = (1, 4, 16)
DIL_COLS = (256, 512, 512)


def const_table():
    parts, at = {}, 0
    r = np.arange(P)[:, None].astype(np.float64)
    c = np.arange(P)[None, :].astype(np.float64)
    tabs = {
        "ident": (r == c) * 1.0,
        "ones": np.ones((P, P)),
        "later_key": (r > c) * 1.0,
        "later_page": ((r > c) & (r // PAGES == c // PAGES)) * 1.0,
        "causal_add": np.where(c > r, NEG, 0.0),
        "strict_mul": (r < c) * 1.0,
    }
    for hh in range(2):
        for g in range(3):
            n = DIL_COLS[g]
            dist = r - (np.arange(n)[None, :] - (n - P))
            ok = (dist >= 0) & (dist % DILATION[g] == 0)
            if g == 0:
                ok &= dist <= 128
            tabs[f"dil{g}{hh}"] = np.where(ok, -SLOPES[g][hh] * dist, NEG)
    sd = np.zeros((P, 3, NT, 2))
    for g in range(3):
        for t in range(NT):
            for hh in range(2):
                dist = (128 + t - r[:, 0]) if g == 0 else DILATION[g] * (128 - r[:, 0])
                sd[:, g, t, hh] = np.where(dist <= 128 * DILATION[g], -SLOPES[g][hh] * dist, NEG)
    tabs["dil_past"] = sd.reshape(P, 24)
    nb = np.zeros((P, 64))
    sm = np.zeros((P, 16))
    for s in range(NT):
        for t in range(NT):
            for h in range(4):
                sm[s, 4 * h + t] = float(s < t)
            for h in range(NFOX):
                nb[s, 16 + 4 * h + t] = 0.0 if s <= t else NEG
            for g in range(3):
                for hh in range(2):
                    ok = (s <= t) if g == 0 else (s == t)
                    nb[s, 40 + 8 * g + 2 * t + hh] = -SLOPES[g][hh] * (t - s) if ok else NEG
    tabs["new_add"] = nb
    tabs["new_strict"] = sm
    sel = np.zeros((P, NFOX, P))
    for h in range(NFOX):
        sel[h, h] = 1.0
    tabs["pick_head"] = sel.reshape(P, NFOX * P)
    pe = np.zeros((P, NEXP, P))
    for e in range(NEXP):
        pe[e, e] = 1.0
    tabs["pick_expert"] = pe.reshape(P, NEXP * P)
    tabs["count4"] = np.tile(np.arange(4.0), (P, 5))
    for n, t in tabs.items():
        parts[n] = (at, at + t.shape[1])
        at += t.shape[1]
    return parts, np.concatenate([t for t in tabs.values()], axis=1).astype(np.float32)


SMALL = ("ident", "ones", "later_key", "later_page", "causal_add", "strict_mul", "dil_past", "new_add",
         "new_strict", "count4")


class Chain:

    def __init__(self, eng, sem):
        self.eng, self.sem, self.n, self.turn = eng, sem, 0, 0

    def __call__(self, ins):
        ins.then_inc(self.sem, 1)
        self.n += 1
        self.eng.wait_ge(self.sem, self.turn + self.n)

    def enter(self, i, per):
        self.turn, self.at, self.per = i * per, self.n, per

    def leave(self, turns):
        assert self.n - self.at == self.per, (self.n - self.at, self.per)
        self.turn, self.n = 0, self.at + turns * self.per



ARENA = 24128


def trunk_kernel(nc, I, O):
    parts, _ = const_table()
    ctx = ExitStack()
    with ctx:
        def sb(name, shape, dt=F32):
            return ctx.enter_context(nc.sbuf_tensor(name, shape, dt))

        sems = {}

        def sem(name):
            if name not in sems:
                sems[name] = ctx.enter_context(nc.semaphore(name))
            return sems[name]

        xT = sb("xT", [P, KD, TOK])
        hT = sb("hT", [P, KD, TOK])
        oT = sb("oT", [P, 6, TOK])
        modT = sb("modT", [P, 48, 9])
        vecT = sb("vecT", [P, 72])
        gainA = sb("gainA", [P, KD, 9])
        rstd = sb("rstd", [P, TOK])
        small = sb("small", [P, sum(parts[n][1] - parts[n][0] for n in SMALL)])
        wring = sb("wring", [P, 3, 4096])
        wr_sb = sb("wr_sb", [P, KD, 20])
        br_sb = sb("br_sb", [P, 20])
        qbd = sb("qbd", [P, NB, 64])
        wnew = sb("wnew", [NT, NB, 64])
        mnew = sb("mnew", [NT, NB, 32])
        spnew = sb("spnew", [NT, NB, 16])
        fox_past = sb("fox_past", [P, P, NFOX])
        ptab = sb("ptab", [1, P], I32)
        pidx = sb("pidx", [P, 1], I32)
        wf_sb = sb("wf_sb", [P, KD, NFOX])
        bf_sb = sb("bf_sb", [NFOX, 1])
        eps_sb = sb("eps_sb", [P, 1])
        ncn = sb("ncn", [NB * NT, NFOX])
        lfnew = sb("lfnew", [NT, NB, NFOX])
        arena = sb("arena", [P, ARENA])
        vs_d = nc.dram_tensor("v_sample_rows", [NB * NT, 1024], F32, kind="Internal").ap()
        nc_d = nc.dram_tensor("ncum_sample_rows", [NB * NT, NFOX], F32, kind="Internal").ap()

        cs = {}
        off = 0
        for n in SMALL:
            w = parts[n][1] - parts[n][0]
            cs[n] = small[:, off:off + w]
            off += w
        ident, ones, later_key, later_page = (cs[n] for n in ("ident", "ones", "later_key", "later_page"))

        def place(at, *shape):
            n = int(np.prod(shape))
            assert at + n <= ARENA, (at, shape)
            a = arena[:, at:at + n]
            if len(shape) == 2:
                a = a.rearrange("p (a b) -> p a b", b=shape[1])
            if len(shape) == 3:
                a = a.rearrange("p (a b c) -> p a b c", b=shape[1], c=shape[2])
            return a

        xin = place(0, 5, D)
        c_raw = place(5120, D)
        c_tmp = place(6144, D)
        rows72 = place(7168, P)
        cT = sb("cT", [P, KD, 9])
        lf_page = place(13056, P, NFOX)
        lf_scan = place(13824, NFOX, P)
        lf_one = place(14592, P)
        lf_tot = place(14720, 2, NFOX)
        zT = place(0, 24, TOK)
        vtok = place(13056, 5, 1024)
        ktok = place(18176, 2, 1024)
        dil_tab = place(20224, 2560)
        pick_head = place(22784, 768)
        ncumT = place(23552, TOK)
        logfT = place(14800, TOK)
        fscr = place(15400, 4, TOK)
        sc_sb = place(8704, 2, 1280)
        nck = place(11264, 2, SEQ)
        pTb = place(12288, 2, 256)
        rowst = place(12800, 4, 2)
        pTa = place(18176, 2, 1024)
        sb_sp = place(8704, 4, SEQ)
        sb_zm = place(10752, 4, SEQ)
        sb_tmp = place(18176, 4, SEQ)
        lf_tok = place(24096, 5, NFOX)
        kring = place(0, 4, 640)
        v_even = place(2560, PAGES, 640)
        v_odd = wring[:, :, :].rearrange("p a b -> p (a b)")[:, 0:PAGES * 640].rearrange("p (a b) -> p a b", b=640)
        vpast = (v_even, v_odd)
        kT2 = place(12800, 2, 640)
        dbuf = place(14080, 2, 2304)
        vncur = place(18688, 1024)
        base = 19712
        at = [base]

        def next_place(*shape):
            at[0] += int(np.prod(shape))
            return place(at[0] - int(np.prod(shape)), *shape)

        s_z = next_place(2, 256)
        s_sp = next_place(2, 256 + 16)
        s_w = next_place(2, 256 + 128)
        s_y = next_place(2, 256 + 64)
        s_f = next_place(2, 384)
        s_lng = s_f[0:NT, :, :].rearrange("p a b -> p (a b)")[:, 0:512].rearrange("p (b n) -> p b n", n=64)
        s_dl = next_place(2, 24)
        s_m = next_place(2, 32)
        s_r = next_place(2, 32)
        s_li = next_place(2, 32)
        s_dg = next_place(2, 32)
        s_mx = next_place(2, 1)
        s_rn = next_place(2, 32)
        s_wn = next_place(2, 64)
        qcur = next_place(2, 64)
        s_sn = next_place(2, 16)
        wbr = place(0, 6, 1024)
        merged = place(6144, KD, TOK)
        gsig = place(10496, 2, TOK)
        btmp = place(11584, 2, TOK)
        upd_s = place(12700, KD, NB * NT)
        wexp = place(0, 2, 6144)
        hid = place(12288, 4, TOK)
        gact = place(14464, 2, TOK)
        yT = place(15552, KD, TOK)
        pick_exp = place(19904, 2048)
        combT = place(21952, TOK)
        rt = place(22496, 1500)

        def rtv(at, n):
            return rt[:, at:at + 5 * n].rearrange("p (i n) -> p i n", n=n)

        r_lg, r_ge, r_oh, r_t = rtv(0, 20), rtv(100, 4), rtv(120, 4), rtv(140, 4)
        r_pr = rt[:, 160:240].rearrange("p (i e g) -> p i e g", e=4, g=4)
        r_es, r_oh1, r_oh2, r_ce = rtv(240, 4), rtv(260, 4), rtv(280, 4), rtv(300, 4)
        r_m, r_gg, r_m1, r_m2, r_w2, r_g1 = (rt[:, 320 + 5 * n:325 + 5 * n] for n in range(6))
        comb_all = rtv(1000, 16)

        combB = wring[:, :, :].rearrange("p a b -> p (a b)")[:, 0:NEXP * TOK].rearrange("p (a b) -> p a b", b=TOK)
        ystage = place(0, 2, 1024)

        psum = ctx.enter_context(nc.psum_tensor("psum", [P, 8, 512], F32))
        banks = [psum[:, i, :] for i in range(8)]
        T = nc.tensor
        V = nc.vector
        A = nc.scalar

        units = []
        for h in range(NFOX):
            for i in range(QTILES):
                units.append(dict(kind="fox", h=h, i=i, off=64 * (h % 2), tile=3 + h // 2, head=h, vcol=640 + 64 * h,
                                  subs=[(5 + h // 2, 0, 128 * (i + 1), 0)]))
        for hh in range(2):
            for i in range(QTILES):
                lo = max(0, i - 1)
                subs, col = [], 0
                for g in range(3):
                    k0 = lo if g == 0 else 0
                    n = 128 * (i + 1 - k0)
                    subs.append((2 + g, 128 * k0, n, col))
                    col += n
                units.append(dict(kind="dil", h=hh, i=i, off=64 * hh, tile=2, head=NFOX + hh, subs=subs))
        nsub = ntg = 0
        for u in units:
            u["cols"] = sum(s[2] for s in u["subs"])
            u["sub0"] = nsub
            nsub += len(u["subs"])
            u["nblk"] = u["cols"] // P
            u["tg0"] = ntg
            ntg += -(-u["nblk"] // 4)
            u["tg1"], u["sub1"] = ntg, nsub
            u["blk"] = []
            for g, (tile, k0, n, _) in enumerate(u["subs"]):
                for b in range(n // P):
                    vc = u["vcol"] if u["kind"] == "fox" else 256 + 128 * g + 64 * u["h"]
                    u["blk"].append((k0 // P + b, vc))
        NU = len(units)

        def pT(par, n):
            return pTa[:, par, 128 * n:128 * n + 128] if n < 8 else pTb[:, par, 128 * (n - 8):128 * (n - 8) + 128]

        def evs(tg):
            return tg // 2 + 1, (tg + 1) // 2

        block = ctx.enter_context(nc.Block())

        KST = (4 + 4 + 5 * NB, 4 + 5)
        VST = 4 * 3 + 5 + 5 * NB

        @block.sync
        def _(sp):
            a = 0
            w = parts["strict_mul"][1]
            sp.dma_start(small[:, 0:w], I["const"][:, 0:w]).then_inc(sem("ld_const"), 16)
            a = w
            for n in SMALL[6:]:
                lo, hi = parts[n]
                sp.dma_start(cs[n], I["const"][:, lo:hi]).then_inc(sem("ld_const"), 16)
            sp.dma_start(c_raw[0:1, :], I["c_prompt"]).then_inc(sem("ld_c"), 16)
            sp.dma_start(c_raw[1:9, :], I["c_sample"]).then_inc(sem("ld_c"), 16)
            sp.dma_start(rows72[0:48, :], I["b_mod"].rearrange("l (m p) -> (l m) p", p=P)).then_inc(sem("ld_c"), 16)
            for n, v in enumerate((I["norm1"].rearrange("l (m p) -> (l m) p", p=P),
                                   I["norm2"].rearrange("l (m p) -> (l m) p", p=P),
                                   I["norm_f"].rearrange("(m p) -> m p", p=P))):
                sp.dma_start(rows72[48 + 8 * n:56 + 8 * n, :], v).then_inc(sem("ld_c"), 16)
            sp.dma_start(ptab[:, :], I["page_table"].rearrange("(o b) n -> o (b n)", o=1)).then_inc(sem("ld_pt"), 16)
            sp.dma_start(pidx[:, :], I["page_table"].rearrange("b (n o) -> (b n) o", o=1)).then_inc(sem("ld_pi"), 16)
            sp.dma_start(xin[:, 0:4, :], I["x_prompt"][0].rearrange("(i p) d -> p i d", p=P)).then_inc(sem("ld_x"), 16)
            sp.dma_start(xin[0:32, 4, :], I["x_sample"].rearrange("b t d -> (b t) d")).then_inc(sem("ld_x"), 16)

            def chunk(c, slot, src, turn=None):
                sp.dma_start(wring[:, slot, :].rearrange("p (k n) -> p k n", k=KD),
                             src.rearrange("(k p) n -> p k n", p=P)).then_inc(sem(f"ld_w{slot}"), 16)

            wm, wi, wo = I["w_mod"][0], I["w_in"][0], I["w_o"][0]
            for c in range(6):
                if c >= 3:
                    sp.wait_ge(sem("w_used"), c - 2)
                chunk(c, c % 3, wm[:, 512 * c:512 * c + 512])
            sp.dma_start(wf_sb[:, :, :], wi[:, 3072:3078].rearrange("(k p) n -> p k n", p=P)).then_inc(sem("ld_f"), 16)
            sp.dma_start(bf_sb[:, :], I["b_f"].rearrange("l (n o) -> (l n) o", o=1)).then_inc(sem("ld_f"), 16)
            for n in range(6):
                if n < 3:
                    sp.wait_ge(sem("w_used"), 4 + n)
                else:
                    sp.wait_ge(sem("z_mm"), 4 * (n - 2))
                chunk(6 + n, n % 3, wi[:, 512 * n:512 * n + 512])
            for n in range(6):
                if n < 3:
                    sp.wait_ge(sem("z_mm"), 4 * (4 + n))
                else:
                    sp.wait_ge(sem("w_used"), 6 + n - 2)
                chunk(12 + n, n % 3, wm[:, 3072 + 512 * n:3584 + 512 * n])
            k = 0
            for hh in range(2):
                for g in range(3):
                    lo, hi = parts[f"dil{g}{hh}"]
                    sp.dma_start(dil_tab[:, k:k + hi - lo], I["const"][:, lo:hi]).then_inc(sem("ld_dt"), 16)
                    k += hi - lo
            lo, hi = parts["pick_head"]
            sp.dma_start(pick_head, I["const"][:, lo:hi]).then_inc(sem("ld_dt"), 16)
            for g in range(3):
                W = DILATION[g] * 128
                n = (W - NT) * 256
                for b in range(NB):
                    src = I[f"cache_dil{g + 1}"][b, 0].rearrange("w a h d -> (w a h d)")[1024:1024 + n]
                    dst = O[f"dil{g + 1}_sample"][b, 0].rearrange("w a h d -> (w a h d)")[0:n]
                    sp.dma_start(dst.rearrange("(s n) -> s n", s=16),
                                 src.rearrange("(s n) -> s n", s=16)).then_inc(sem("shift"), 16)
            sp.wait_ge(sem("pv_mm"), NU)
            sp.wait_ge(sem("o_ev"), 8)
            sp.wait_ge(sem("w_used"), 12)
            sp.wait_ge(sem("new_ready"), 1)
            sp.wait_ge(sem("ld_pt"), 16)
            sp.wait_ge(sem("st_kv"), 16 * VST)
            sp.wait_ge(sem("st_vs"), 16)
            sp.wait_ge(sem("st_lf"), 32)
            with sp.Fori(0, NB // 2) as i:
                for par in range(2):
                    sp.wait_ge(sem("seq_pv"), i * 2)
                    b = i * 2 + par
                    db = dbuf[:, par, :]
                    sp.dma_start(db[:, 0:256], I["cache_dil1"][bass.ds(b, 1), 0].rearrange("b w a h d -> w (b a h d)")
                                 ).then_inc(sem(f"ld_db{par}"), 16)
                    sp.dma_start(db[:, 256:1280], I["cache_dil2"][bass.ds(b, 1), 0].rearrange(
                        "b (i r) a h d -> i (b r a h d)", r=4)).then_inc(sem(f"ld_db{par}"), 16)
                    sp.dma_start(db[:, 1280:2304], I["cache_dil3"][bass.ds(b, 1), 0].rearrange(
                        "b (i r) a h d -> i (b r) (a h d)", r=16)[:, 0:4, :].rearrange("i r n -> i r n")
                        ).then_inc(sem(f"ld_db{par}"), 16)
                    for p in range(PAGES):
                        slot = p % 4
                        pid = sp.value_load(ptab[0:1, bass.ds(b * PAGES + p, 1)], min_val=0, max_val=159)
                        pg = I["cache_kv"][bass.ds(pid, 1), 0]
                        sp.wait_ge(sem("kT_mm"), i * 36 + (18 * par + p - 3 if p >= 4 else 13 + p if par else 0))
                        sp.dma_start(kring[:, slot, :], pg[:, :, 0].rearrange("o k h d -> k (o h d)")
                                     ).then_inc(sem(f"ld_k{slot}"), 16)
                        sp.dma_start(vpast[par][:, p, :], pg[:, :, 1].rearrange("o k h d -> k (o h d)")
                                     ).then_inc(sem(f"ld_v{par}"), 16)
            sp.wait_ge(sem("seq_out"), NB)
            for k in range(6):
                src = (I["w_br_sb"][0], I["w_br_sb"][0], I["w_br_dil"][0], I["w_br_fox"][0], I["w_br_fox"][0],
                       I["w_br_fox"][0])[k]
                r = (0, 128, 0, 0, 128, 256)[k]
                sp.dma_start(wbr[:, k, :], src[r:r + 128, :]).then_inc(sem("ld_br"), 16)
            c = 18
            for half in range(2):
                for b in range(3):
                    if c >= 21:
                        sp.wait_ge(sem("gate_mm"), 4 * (c - 20))
                    chunk(c, c % 3, wi[:, 3078 + 1024 * b + 512 * half:3078 + 1024 * b + 512 * half + 512])
                    c += 1
            for half in range(2):
                sp.wait_ge(sem("gate_mm"), 4 * (c - 20))
                chunk(c, c % 3, wo[:, 512 * half:512 * half + 512])
                c += 1
            sp.dma_start(wr_sb[:, :, 0:4], I["w_rg"][0].rearrange("(k p) n -> p k n", p=P)).then_inc(sem("ld_r"), 16)
            sp.dma_start(wr_sb[:, :, 4:20], I["w_re"][0].rearrange("(k p) n -> p k n", p=P)).then_inc(sem("ld_r"), 16)
            sp.dma_start(br_sb[:, 0:4], I["b_rg"].to_broadcast([P, 4])).then_inc(sem("ld_r"), 16)
            sp.dma_start(br_sb[:, 4:20], I["b_re"].to_broadcast([P, 16])).then_inc(sem("ld_r"), 16)
            sp.wait_ge(sem("xo_mm"), 8)
            lo, hi = parts["pick_expert"]
            sp.dma_start(pick_exp, I["const"][:, lo:hi]).then_inc(sem("ld_pe"), 16)

            def expert(e, slot):
                for n, name in enumerate(("w1", "w3")):
                    sp.dma_start(wexp[:, slot, 2048 * n:2048 * n + 2048].rearrange("p (k f) -> p k f", k=KD),
                                 I[name][0][bass.ds(e, 1)].rearrange("o (k p) f -> p (o k) f", p=P)
                                 ).then_inc(sem(f"ld_e{slot}"), 16)
                sp.dma_start(wexp[:, slot, 4096:6144].rearrange("p (k f) -> p k f", k=2),
                             I["w2"][0][bass.ds(e, 1)].rearrange("o (k p) f -> p (o k) f", p=P)
                             ).then_inc(sem(f"ld_e{slot}"), 16)

            expert(0, 0)
            expert(1, 1)
            with sp.Fori(0, NEXP // 2 - 1) as i:
                for u in range(2):
                    sp.wait_ge(sem("y_mm"), i * 16 + (8 + 8 * u))
                    expert(i * 2 + (2 + u), u)
            sp.wait_ge(sem("shift"), 16 * 24)
            sp.wait_ge(sem("st_kv"), 16 * VST)
            sp.wait_ge(sem("st_lf"), 32)
            for s in range(2):
                sp.wait_ge(sem(f"st_k{s}"), 16 * KST[s])
            sp.wait_ge(sem("st_y0"), 16 * 3)
            sp.wait_ge(sem("st_y1"), 16 * 2)


        def kv_stores(i):
            out = []
            for kv in range(2):
                if i < 4:
                    rows = O["kv_prompt"][0, 0, 128 * i:128 * i + 128, kv]
                    out += [(kv, 0, 256, rows[:, 0:4]), (kv, 640, 384, rows[:, 4:10])]
                    for g in range(3):
                        if g == 0 and i < 3:
                            continue
                        lo = 0 if g == 0 else 128 * i
                        out.append((kv, 256 + 128 * g, 128, O[f"dil{g + 1}_prompt"][0, 0, lo:lo + 128, kv]))
            return out

        def group_out(eng, n, tg, copy, done):
            u = units[n]
            b0 = 4 * (tg - u["tg0"])
            k = min(4, u["nblk"] - b0)
            eng.wait_ge(sem("tg_mm"), tg + 1)
            if n >= 2:
                eng.wait_ge(sem("pv_mm"), n - 1)
            dst = pTa[:, n % 2, 128 * b0:128 * (b0 + k)] if b0 < 8 else pTb[:, n % 2, 0:128 * k]
            copy(dst, banks[2 + tg % 2][:, 0:128 * k]).then_inc(sem(done), 1)

        def keys_out(eng, i, par, p, copy):
            pr = p % 2
            eng.wait_ge(sem("kT_mm"), i * 36 + (18 * par + p + 1))
            if p >= 2:
                eng.wait_ge(sem("k_scored"), i * 34 + (17 * par + p - 1))
            elif p == 0:
                eng.wait_ge(sem("k_scored"), i * 34 + 17 * par)
            else:
                eng.wait_ge(sem("seq_s"), i * 2 + par)
            n = 512 if p == 17 else 640
            src = psum[:, 2 * pr:2 * pr + 2, :].rearrange("p a b -> p (a b)")[:, 0:n]
            copy(kT2[:, pr, 0:n], src).then_inc(sem(f"kT_ev{pr}"), 1)

        @block.gpsimd
        def _(pool):
            pool.wait_ge(sem("ld_pi"), 16)
            pool.indirect_dma_start(
                out=lf_page.rearrange("p a b -> p (a b)"), out_offset=None,
                in_=I["cache_fox_logf"].rearrange("n l k h -> n (l k h)"),
                in_offset=bass.IndirectOffsetOnAxis(ap=pidx[:, 0:1], axis=0)).then_inc(sem("ld_lf"), 16)
            pool.wait_ge(sem("lf_rows"), 1)
            pool.dma_start(O["logf_prompt"][0, 0].rearrange("(i p) h -> p i h", p=P),
                           lf_tok[:, 0:4, :]).then_inc(sem("st_lf"), 16)
            pool.dma_start(O["logf_sample"].rearrange("b l t h -> (b l t) h"), lf_tok[0:32, 4, :]
                           ).then_inc(sem("st_lf"), 16)
            pool.dma_start(nc_d, ncn[0:32, :]).then_inc(sem("st_nc"), 16)
            pool.wait_ge(sem("st_nc"), 16)
            pool.dma_start(lfnew[0:NT, :, :], nc_d.rearrange("(b t) h -> t b h", t=NT)).then_inc(sem("ld_nc"), 16)
            for i in range(5):
                pool.wait_ge(sem("kt_ev"), 2 * i + 2)
                pool.wait_ge(sem("vt_ev"), 2 * i + 2)
                src = (ktok[:, i % 2, :], vtok[:, i, :])
                for kv, lo, n, dst in kv_stores(i):
                    s = "st_kv" if kv else f"st_k{i % 2}"
                    pool.dma_start(dst.rearrange("t h d -> t (h d)"), src[kv][:, lo:lo + n]).then_inc(sem(s), 16)
                if i == 4:
                    for kv in range(2):
                        s = "st_kv" if kv else f"st_k{i % 2}"
                        r = O["kv_sample"][:, 0, :, kv].rearrange("b t h d -> b t (h d)")
                        for b in range(NB):
                            rows = src[kv][4 * b:4 * b + 4, :]
                            pool.dma_start(r[b, :, 0:256], rows[:, 0:256]).then_inc(sem(s), 16)
                            pool.dma_start(r[b, :, 256:640], rows[:, 640:1024]).then_inc(sem(s), 16)
                            for g in range(3):
                                W = DILATION[g] * 128
                                dst = O[f"dil{g + 1}_sample"][b, 0, W - NT:W, kv].rearrange("t h d -> t (h d)")
                                pool.dma_start(dst, rows[:, 256 + 128 * g:384 + 128 * g]).then_inc(sem(s), 16)
                    pool.dma_start(vs_d, src[1][0:32, :]).then_inc(sem("st_vs"), 16)
            for n, u in enumerate(units):
                pool.wait_ge(sem("rs_ready"), n + 1)
                s = sc_sb[:, n % 2, 0:u["cols"]]
                nc.gpsimd.tensor_scalar(s, s, rowst[:, 3, n % 2:n % 2 + 1], None, ALU.mult).then_inc(sem("nrm"), 1)
            pool.wait_ge(sem("st_vs"), 16)
            pool.wait_ge(sem("pv_mm"), NU)
            link = Chain(pool, sem("pool_own"))
            for pad in (s_sp[:, :, 256:272], s_w[:, :, 256:384]):
                nc.gpsimd.memset(pad, 0.0)
            link(nc.gpsimd.memset(s_y[:, :, 256:320], 0.0))
            with pool.Fori(0, NB // 2) as i:
                link.enter(i, 6)
                for par in range(2):
                    pool.wait_ge(sem("seq_pv"), i * 2 + par)
                    pool.dma_start(vncur[0:NT, :], vs_d[bass.ds(i * 2 * NT + par * NT, NT), :]).then_inc(sem("ld_vn"), 16)
                    pool.wait_ge(sem("sp_ready"), i * 2 + (par + 1))
                    sp_, w, y = s_sp[:, par, :], s_w[:, par, :], s_y[:, par, :]
                    link(nc.gpsimd.tensor_tensor(w[:, 0:256], sp_[:, 0:256], sp_[:, 16:272], ALU.add))
                    link(nc.gpsimd.tensor_tensor(y[:, 0:256], w[:, 0:256], w[:, 32:288], ALU.add))
                    link(nc.gpsimd.tensor_tensor(w[:, 0:256], y[:, 0:256], y[:, 64:320], ALU.add))
                    nc.gpsimd.tensor_tensor(y[:, 0:256], w[:, 0:256], w[:, 128:384], ALU.add
                                            ).then_inc(sem("y_ready"), 1)
                link.leave(NB // 2)

        @block.tensor
        def _(pe):
            def mm(out, lhsT, rhs, start=True, stop=True, **k):
                return T.matmul(out, lhsT, rhs, start=start, stop=stop, **k)

            pe.wait_ge(sem("ld_const"), 16 * 5)
            pe.wait_ge(sem("ld_c"), 16 * 6)
            pe.wait_ge(sem("c_silu"), 1)
            for k in range(KD):
                T.transpose(banks[7][:, 9 * k:9 * k + 9], c_tmp[0:9, 128 * k:128 * k + 128], ident[0:9, 0:9])
            T.transpose(banks[7][:, 128:200], rows72[0:72, :], ident[0:72, 0:72]).then_inc(sem("c_t"), 1)
            pe.wait_ge(sem("ld_x"), 32)
            for k in range(KD):
                if k >= 4:
                    pe.wait_ge(sem("x_evD" if k % 2 else "x_evA"), (k - 4) // 2 + 1)
                for i in range(4):
                    last = T.transpose(banks[k % 4][:, 128 * i:128 * i + 128], xin[:, i, 128 * k:128 * k + 128], ident)
                last.then_inc(sem("x_t"), 1)
            for k in range(KD):
                last = T.transpose(banks[4][:, 32 * k:32 * k + 32], xin[0:32, 4, 128 * k:128 * k + 128],
                                   ident[0:32, 0:32])
            last.then_inc(sem("x_t"), 1)

            def mod_chunk(u):
                for j in range(4):
                    for k in range(KD):
                        last = mm(banks[u][:, 9 * j:9 * j + 9], wring[:, u, 512 * k + 128 * j:512 * k + 128 * j + 128],
                                  cT[:, k, :], k == 0, k == KD - 1)
                return last

            pe.wait_ge(sem("cT_ready"), 1)
            pe.wait_ge(sem("x_evA"), 4)
            pe.wait_ge(sem("x_evD"), 4)
            for c in range(6):
                if c >= 3:
                    pe.wait_ge(sem("mod_ev"), c - 2)
                pe.wait_ge(sem(f"ld_w{c % 3}"), 16 * (c // 3 + 1))
                mod_chunk(c % 3).then_inc(sem("w_used"), 1)

            def norm_sums(n):
                pe.wait_ge(sem("sq"), n + 1)
                for k in range(KD):
                    mm(banks[5], ones, hT[:, k, 0:SEQ], k == 0, k == KD - 1)
                    last = mm(banks[6][:, 0:32], ones, hT[:, k, SEQ:TOK], k == 0, k == KD - 1)
                last.then_inc(sem("ss"), 1)

            norm_sums(0)

            pe.wait_ge(sem("h_ready"), 1)
            pe.wait_ge(sem("mod_ev"), 6)
            with pe.Fori(0, 2) as i:
                for u in range(3):
                    pe.wait_ge(sem(f"ld_w{u}"), i * 16 + 48)
                    for j in range(4):
                        n = 4 * u + j
                        pe.wait_ge(sem("z_ev"), i * 12 + max(0, n - 1))
                        for k in range(KD):
                            w = wring[:, u, 512 * k + 128 * j:512 * k + 128 * j + 128]
                            mm(banks[n % 2], w, hT[:, k, 0:SEQ], k == 0, k == KD - 1)
                            last = mm(banks[2 + n % 2][:, 0:32], w, hT[:, k, SEQ:TOK], k == 0, k == KD - 1)
                        last.then_inc(sem("z_mm"), 1)

            pe.wait_ge(sem("ld_f"), 32)
            for k in range(KD):
                mm(banks[4][0:NFOX, :], wf_sb[:, k, :], hT[:, k, 0:SEQ], k == 0, k == KD - 1)
                last = mm(banks[5][0:NFOX, 0:32], wf_sb[:, k, :], hT[:, k, SEQ:TOK], k == 0, k == KD - 1)
            last.then_inc(sem("f_mm"), 1)
            pe.wait_ge(sem("lf_tot"), 1)
            mm(banks[7][:, 0:NFOX], later_page, lf_tot[:, 0, :]).then_inc(sem("lf_late"), 1)

            pe.wait_ge(sem("z_ev"), 24)
            with pe.Fori(0, 2) as i:
                for u in range(3):
                    pe.wait_ge(sem("mod_ev"), i * 3 + 6)
                    pe.wait_ge(sem(f"ld_w{u}"), i * 16 + 80)
                    mod_chunk(u).then_inc(sem("w_used"), 1)

            pe.wait_ge(sem("lf_after"), 1)
            pe.wait_ge(sem("mod_ev"), 12)
            for h in range(NFOX):
                dst = banks[0][:, 128 * h:128 * h + 128] if h < 4 else banks[1][:, 128 * (h - 4):128 * (h - 3)]
                last = T.transpose(dst, lf_scan[:, h, :], ident)
            last.then_inc(sem("lf_tr"), 1)
            pe.wait_ge(sem("lf_rowT"), 1)
            for i in range(4):
                T.transpose(banks[6][:, 6 * i:6 * i + 6], logfT[0:6, 128 * i:128 * i + 128], ident[0:6, 0:6])
            T.transpose(banks[6][0:32, 24:30], logfT[0:6, SEQ:TOK], ident[0:6, 0:6])
            T.transpose(banks[6][0:32, 32:38], ncumT[0:6, SEQ:TOK], ident[0:6, 0:6]).then_inc(sem("lf_rowt"), 1)

            pe.wait_ge(sem("lf_past"), 1)
            for i in range(5):
                n = P if i < 4 else 32
                for g in range(4):
                    if i:
                        pe.wait_ge(sem("kt_ev" if g < 2 else "vt_ev"), 2 * (i - 1) + g % 2 + 1)
                    for j in range(4):
                        last = T.transpose(banks[g][0:n, 128 * j:128 * j + 128],
                                           zT[:, 8 + 4 * g + j, 128 * i:128 * i + n], ident)
                    last.then_inc(sem("kv_t"), 1)

            pe.wait_ge(sem("kt_ev"), 10)
            pe.wait_ge(sem("vt_ev"), 10)
            pe.wait_ge(sem("lf_rows"), 1)

            def sb_scores(h):
                for kt in range(4):
                    if h:
                        pe.wait_ge(sem("sbz_read"), 4 * (h - 1) + kt + 1)
                    o = 64 * (h % 2)
                    mm(banks[kt][:, 128 * kt:SEQ], zT[o:o + 64, 8 + h // 2, 128 * kt:128 * kt + 128],
                       zT[o:o + 64, h // 2, 128 * kt:SEQ]).then_inc(sem("sbz_mm"), 1)

            sb_scores(0)
            for h in range(4):
                if h < 3:
                    sb_scores(h + 1)
                pe.wait_ge(sem("sbsp"), h + 1)
                for n, kt in enumerate((3, 2, 1, 0)):
                    if 4 * h + n >= 2:
                        pe.wait_ge(sem("sba_read"), 4 * h + n - 1)
                    bk = banks[4 + n % 2]
                    last = mm(bk[:, 128 * kt:SEQ], later_key, sb_sp[:, kt, 128 * kt:SEQ], True, kt == 3)
                    for k2 in range(kt + 1, 4):
                        last = mm(bk[:, 128 * k2:SEQ], ones, sb_sp[:, k2, 128 * k2:SEQ], False, k2 == 3)
                    last.then_inc(sem("sba_mm"), 1)
                pe.wait_ge(sem("sbw"), h + 1)
                if h >= 2:
                    pe.wait_ge(sem("sbo_ev"), h - 1)
                o = 64 * (h % 2)
                for kt in range(4):
                    last = mm(banks[6 + h % 2][o:o + 64, 128 * kt:SEQ], vtok[:, kt, 64 * h:64 * h + 64],
                              sb_zm[:, kt, 128 * kt:SEQ], kt == 0, kt == 3)
                last.then_inc(sem("sbo_mm"), 1)

            pe.wait_ge(sem("sbo_ev"), 4)
            pe.wait_ge(sem("sba_read"), 16)
            pe.wait_ge(sem("sbz_read"), 16)
            pe.wait_ge(sem("ld_dt"), 16 * 7)

            def fox_rows(h):
                if h >= 2:
                    pe.wait_ge(sem("nck_ev"), h - 1)
                mm(banks[6 + h % 2], pick_head[0:NFOX, 128 * h:128 * h + 128], ncumT[0:NFOX, 0:SEQ]
                   ).then_inc(sem("nck_mm"), 1)

            def scores(n):
                u = units[n]
                o, i = u["off"], u["i"]
                for s, (tile, k0, cols, _) in enumerate(u["subs"]):
                    c = u["sub0"] + s
                    if c >= 2:
                        pe.wait_ge(sem("sc_ev"), c - 1)
                    mm(banks[c % 2][:, 0:cols], zT[o:o + 64, tile, 128 * i:128 * i + 128],
                       zT[o:o + 64, 8 + tile, k0:k0 + cols]).then_inc(sem("sc_mm"), 1)

            def turn_weights(n):
                u = units[n]
                pe.wait_ge(sem("nrm"), n + 1)
                for tg in range(u["tg0"], u["tg1"]):
                    if tg >= 2:
                        d, a = evs(tg - 2)
                        pe.wait_ge(sem("tg_evA" if tg % 2 else "tg_evD"), a if tg % 2 else d)
                    b0 = 4 * (tg - u["tg0"])
                    for b in range(b0, min(b0 + 4, u["nblk"])):
                        last = T.transpose(banks[2 + tg % 2][:, 128 * (b - b0):128 * (b - b0) + 128],
                                           sc_sb[:, n % 2, 128 * b:128 * b + 128], ident)
                    last.then_inc(sem("tg_mm"), 1)

            def weigh(n):
                u = units[n]
                d, a = evs(u["tg1"] - 1)
                pe.wait_ge(sem("tg_evD"), d)
                if a:
                    pe.wait_ge(sem("tg_evA"), a)
                if u["i"] == 0 and u["head"] >= 2:
                    pe.wait_ge(sem("o_ev"), u["head"] - 1)
                o, i = u["off"], u["i"]
                for b, (kt, vc) in enumerate(u["blk"]):
                    last = mm(banks[4 + u["head"] % 2][o:o + 64, 128 * i:128 * i + 128], vtok[:, kt, vc:vc + 64],
                              pT(n % 2, b), b == 0, b == u["nblk"] - 1)
                last.then_inc(sem("pv_mm"), 1)

            fox_rows(0)
            scores(0)
            for n in range(NU):
                if n % 4 == 0 and n // 4 + 1 < NFOX:
                    fox_rows(n // 4 + 1)
                if n + 1 < NU:
                    scores(n + 1)
                turn_weights(n)
                if n:
                    weigh(n - 1)
            weigh(NU - 1)

            pe.wait_ge(sem("qbd_ready"), 1)
            pe.wait_ge(sem("sc_ev"), nsub)
            for b in range(NB):
                for j in range(8):
                    tile = PAIR_TILES[j] if j < 5 else j - 3
                    last = mm(banks[0][0:NT, 64 * b + 8 * j:64 * b + 8 * j + 8],
                              zT[:, 8 + tile, SEQ + NT * b:SEQ + NT * b + NT], qbd[:, b, 8 * j:8 * j + 8])
            last.then_inc(sem("new_mm"), 1)
            pe.wait_ge(sem("spn_ready"), 1)
            mm(banks[1][0:NT, 0:128], later_key[0:NT, 0:NT], spnew[:, :, :].rearrange("p b n -> p (b n)")
               ).then_inc(sem("new_a"), 1)

            pe.wait_ge(sem("new_ready"), 1)
            pe.wait_ge(sem("o_ev"), 8)
            pe.wait_ge(sem("nck_ev"), NFOX)

            def turn_keys(i, par, p):
                pr = p % 2
                pe.wait_ge(sem(f"kT_ev{pr}"), i * 18 + (par * 9 + p // 2))
                if p < PAGES:
                    slot = p % 4
                    pe.wait_ge(sem(f"ld_k{slot}"), i * 128 + 16 * (par * 4 + p // 4 + 1))
                    srcs = [kring[:, slot, 128 * j:128 * j + 128] for j in range(5)]
                else:
                    if p == PAGES:
                        pe.wait_ge(sem(f"ld_db{par}"), i * 48 + 48)
                    starts = (0, 256, 512, 768, 1024) if p == PAGES else (1280, 1536, 1792, 2048)
                    srcs = [dbuf[:, par, s:s + 128] for s in starts]
                for j, s in enumerate(srcs):
                    dst = banks[2 * pr][:, 128 * j:128 * j + 128] if j < 4 else banks[2 * pr + 1][:, 0:128]
                    last = T.transpose(dst, s, ident)
                last.then_inc(sem("kT_mm"), 1)

            def score_keys(i, par, p):
                pr = p % 2
                pe.wait_ge(sem(f"kT_ev{pr}"), i * 18 + (par * 9 + p // 2 + 1))
                if p < PAGES:
                    bk, c0 = banks[4 + p // 8], 40 * (p % 8)
                    jobs = [(j, c0 + 8 * j, 8 * j, 8) for j in range(5)]
                elif p == PAGES:
                    bk = banks[5]
                    jobs = [(0, 320, 40, 8)] + [(1 + t, 328 + 2 * t, 48 + 2 * t, 2) for t in range(NT)]
                else:
                    bk = banks[5]
                    jobs = [(t, 336 + 2 * t, 56 + 2 * t, 2) for t in range(NT)]
                for j, c, q, n in jobs:
                    last = mm(bk[:, c:c + n], kT2[:, pr, 128 * j:128 * j + 128], qcur[:, par, q:q + n])
                return last

            def column_max(i, par):
                pe.wait_ge(sem("m_ready"), i * 2 + (par + 1))
                T.transpose(banks[6][0:32, 256:384], s_m[:, par, :], ident).then_inc(sem("m_t"), 1)

            def column_max_back(i, par):
                pe.wait_ge(sem("dg_ready"), i * 2 + (par + 1))
                mm(banks[6][:, 384:416], ones[0:32, :], s_dg[0:32, par, :]).then_inc(sem("m_b"), 1)

            def sticks(i, par):
                pe.wait_ge(sem("y_ready"), i * 2 + (par + 1))
                a = banks[7][:, 64:320]
                mm(a, later_key, s_sp[:, par, 0:256], True, False)
                mm(a, ones, s_y[:, par, 16:272], False, False)
                mm(a.rearrange("p (a b) -> p a b", b=16), ones[0:NT, :],
                   s_sn[0:NT, par, :].unsqueeze(1).to_broadcast([NT, PAGES, 16]), False, True).then_inc(sem("a_mm"), 1)

            def sums(i, par):
                pe.wait_ge(sem("r_ready"), i * 2 + (par + 1))
                mm(banks[6][:, 416:448], ones, s_r[:, par, :], True, False)
                mm(banks[6][:, 416:448], ones[0:NT, :], s_rn[0:NT, par, :], False, True).then_inc(sem("l_mm"), 1)

            def weigh_values(i, par):
                pe.wait_ge(sem("w_ready"), i * 2 + (par + 1))
                pe.wait_ge(sem(f"ld_v{par}"), i * 256 + 256)
                pe.wait_ge(sem("ld_vn"), i * 32 + 16 * (par + 1))
                first = True
                for p in range(PAGES):
                    for j in range(5):
                        w = s_w[:, par, 16 * p + 8 * j:16 * p + 8 * j + 8] if j < 2 else \
                            s_f[:, par, 24 * p + 8 * (j - 2):24 * p + 8 * (j - 2) + 8]
                        mm(banks[7][:, 8 * j:8 * j + 8], vpast[par][:, p, 128 * j:128 * j + 128], w,
                           first, False, skip_group_check=True)
                        first = False
                mm(banks[7][:, 40:48], dbuf[:, par, 128:256], s_dl[:, par, 0:8], False, False, skip_group_check=True)
                for g in (1, 2):
                    for t in range(NT):
                        at = 1024 * (g - 1) + 256 + 256 * t + 128
                        mm(banks[7][:, 40 + 2 * t:42 + 2 * t], dbuf[:, par, at:at + 128],
                           s_dl[:, par, 8 * g + 2 * t:8 * g + 2 * t + 2], False, False, skip_group_check=True)
                for j in range(8):
                    tile = PAIR_TILES[j] if j < 5 else j - 3
                    c = 8 * j if j < 5 else 40
                    last = mm(banks[7][:, c:c + 8], vncur[0:NT, 128 * tile:128 * tile + 128],
                              s_wn[0:NT, par, 8 * j:8 * j + 8], False, j == 7, skip_group_check=True)
                last.then_inc(sem("seq_pv"), 1)

            def read_keys(i, par, between):
                pe.wait_ge(sem("qcur"), i * 2 + (par + 1))
                pe.wait_ge(sem("s_read"), i * 2 + par)
                for p in range(18):
                    turn_keys(i, par, p)
                    if p:
                        score_keys(i, par, p - 1).then_inc(sem("k_scored"), 1)
                    for step in between.get(p, ()):
                        step(i, 0)
                score_keys(i, par, 17).then_inc(sem("seq_s"), 1)

            with pe.Fori(0, NB // 2) as i:
                read_keys(i, 0, {})
                pe.wait_ge(sem("seq_out"), i * 2)
                read_keys(i, 1, {3: (column_max,), 6: (column_max_back, sticks), 12: (sums,)})
                weigh_values(i, 0)
                pe.wait_ge(sem("seq_out"), i * 2 + 1)
                column_max(i, 1)
                column_max_back(i, 1)
                sticks(i, 1)
                sums(i, 1)
                weigh_values(i, 1)

            pe.wait_ge(sem("seq_out"), NB)
            pe.wait_ge(sem("s_read"), NB)
            pe.wait_ge(sem("ld_br"), 16 * 6)
            n, c = 0, 18
            for half in range(2):
                for b in range(3):
                    pe.wait_ge(sem(f"ld_w{c % 3}"), 16 * (c // 3 + 1))
                    for j in range(4):
                        m = 4 * half + j
                        if n >= 2:
                            pe.wait_ge(sem("gate_ev"), n - 1)
                            pe.wait_ge(sem("br_ev"), n - 1)
                        kts = ((0, 1), (2,), (3, 4, 5))[b]
                        for k in kts:
                            w = wbr[:, k, 128 * m:128 * m + 128]
                            mm(banks[4 + n % 2], w, oT[:, k, 0:SEQ], k == kts[0], k == kts[-1])
                            mm(banks[6 + n % 2][:, 0:32], w, oT[:, k, SEQ:TOK], k == kts[0], k == kts[-1])
                        for k in range(KD):
                            w = wring[:, c % 3, 512 * k + 128 * j:512 * k + 128 * j + 128]
                            mm(banks[n % 2], w, hT[:, k, 0:SEQ], k == 0, k == KD - 1)
                            last = mm(banks[2 + n % 2][:, 0:32], w, hT[:, k, SEQ:TOK], k == 0, k == KD - 1)
                        last.then_inc(sem("gate_mm"), 1)
                        n += 1
                    c += 1

            for half in range(2):
                pe.wait_ge(sem(f"ld_w{c % 3}"), 16 * (c // 3 + 1))
                pe.wait_ge(sem("br_ev"), 24)
                for j in range(4):
                    m = 4 * half + j
                    if m >= 2:
                        pe.wait_ge(sem("xo_ev"), m - 1)
                    for k in range(KD):
                        w = wring[:, c % 3, 512 * k + 128 * j:512 * k + 128 * j + 128]
                        mm(banks[m % 2], w, merged[:, k, 0:SEQ], k == 0, k == KD - 1)
                        last = mm(banks[2 + m % 2][:, 0:32], w, merged[:, k, SEQ:TOK], k == 0, k == KD - 1)
                    last.then_inc(sem("xo_mm"), 1)
                c += 1
            norm_sums(1)

            pe.wait_ge(sem("h_ready"), 2)
            pe.wait_ge(sem("xo_ev"), 8)
            pe.wait_ge(sem("ld_r"), 64)
            for i in range(5):
                n = P if i < 4 else 32
                for k in range(KD):
                    last = mm(banks[0][0:n, 20 * i:20 * i + 20], hT[:, k, 128 * i:128 * i + n], wr_sb[:, k, :],
                              k == 0, k == KD - 1)
            last.then_inc(sem("rt_mm"), 1)
            pe.wait_ge(sem("comb_ready"), 1)
            for i in range(5):
                n = P if i < 4 else 32
                dst = banks[1][0:16, 128 * i:128 * i + 128] if i < 4 else banks[2][0:16, 0:32]
                last = T.transpose(dst, comb_all[0:n, i, :], ident[0:n, 0:n])
            last.then_inc(sem("comb_t"), 1)
            pe.wait_ge(sem("combT_ready"), 1)
            pe.wait_ge(sem("ld_pe"), 16)
            for e in range(NEXP):
                if e >= 2:
                    pe.wait_ge(sem("combB_ev"), e - 1)
                pick = pick_exp[0:NEXP, 128 * e:128 * e + 128]
                mm(banks[5][:, 32 * e:32 * e + 32], pick, combT[0:NEXP, SEQ:TOK])
                mm(banks[3 + e % 2], pick, combT[0:NEXP, 0:SEQ]).then_inc(sem("combB_mm"), 1)

            pe.wait_ge(sem("combB_ev"), 16)
            pe.wait_ge(sem("combBs_ev"), 1)

            def expert(i, u):
                pe.wait_ge(sem(f"ld_e{u}"), i * 48 + 48)
                pe.wait_ge(sem("hid_ev"), i * 2 + u)
                for f in range(2):
                    for w13 in range(2):
                        bk = banks[2 * f + w13]
                        for k in range(KD):
                            at = 2048 * w13 + 256 * k + 128 * f
                            w = wexp[:, u, at:at + 128]
                            mm(bk, w, hT[:, k, 0:SEQ], k == 0, k == KD - 1)
                            last = mm(banks[4][:, 64 * f + 32 * w13:64 * f + 32 * w13 + 32], w, hT[:, k, SEQ:TOK],
                                      k == 0, k == KD - 1)
                    last.then_inc(sem(f"hid_mm{f}"), 1)
                pe.wait_ge(sem("hid_ev"), i * 2 + u + 1)
                for m in range(KD):
                    n = i * 16 + 8 * u
                    pe.wait_ge(sem("y_ev"), n + max(0, m - 1) if m or u else n)
                    if m == 0:
                        pe.wait_ge(sem("ys_ev"), i * 2 + u)
                    for f in range(2):
                        w = wexp[:, u, 4096 + 1024 * f + 128 * m:4096 + 1024 * f + 128 * m + 128]
                        mm(banks[5][:, 32 * m:32 * m + 32], w, hid[:, 2 * u + f, SEQ:TOK], f == 0, f == 1)
                        last = mm(banks[6 + m % 2], w, hid[:, 2 * u + f, 0:SEQ], f == 0, f == 1)
                    last.then_inc(sem("y_mm"), 1)

            with pe.Fori(0, NEXP // 2) as i:
                expert(i, 0)
                expert(i, 1)
            norm_sums(2)
            pe.wait_ge(sem("h_ready"), 3)
            for i in range(5):
                n = P if i < 4 else 32
                for g in range(2):
                    if i:
                        pe.wait_ge(sem("yo_evA" if g else "yo_evD"), i)
                    for j in range(4):
                        last = T.transpose(banks[g][0:n, 128 * j:128 * j + 128],
                                           hT[:, 4 * g + j, 128 * i:128 * i + n], ident)
                    last.then_inc(sem("yo_t"), 1)

        @block.scalar
        def _(act):
            link = Chain(act, sem("act_own"))

            def f(out, in_, fn, **k):
                return A.activation(out, in_, fn, **k)

            act.wait_ge(sem("ld_c"), 16 * 6)
            f(c_tmp[0:9, :], c_raw[0:9, :], ACT.Exp, scale=-1.0).then_inc(sem("c_e"), 1)
            for k in range(0, KD, 2):
                act.wait_ge(sem("x_t"), k + 1)
                A.copy(xT[:, k, 0:SEQ], banks[k % 4]).then_inc(sem("x_evA"), 1)

            def norm_root(n):
                f(hT[:, :, :], xT[:, :, :], ACT.Square).then_inc(sem("sq"), 1)
                act.wait_ge(sem("ss"), n + 1)
                f(rstd[:, 0:SEQ], banks[5], ACT.Ln, scale=1.0 / D, bias=eps_sb[:, 0:1])
                link(f(rstd[:, SEQ:TOK], banks[6][:, 0:32], ACT.Ln, scale=1.0 / D, bias=eps_sb[:, 0:1]))
                f(rstd[:, :], rstd[:, :], ACT.Exp, scale=-0.5).then_inc(sem("rs"), 1)

            act.wait_ge(sem("x_evD"), 4)
            act.wait_ge(sem("xs_ev"), 1)
            act.wait_ge(sem("x_evA"), 4)
            norm_root(0)

            with act.Fori(0, 2) as i:
                for n in range(12):
                    act.wait_ge(sem("z_mm"), i * 12 + (n + 1))
                    A.copy(zT[:, bass.ds(i * 12 + n, 1), 0:SEQ].rearrange("p o n -> p (o n)"), banks[n % 2])
                    A.copy(zT[:, bass.ds(i * 12 + n, 1), SEQ:TOK].rearrange("p o n -> p (o n)"),
                           banks[2 + n % 2][:, 0:32]).then_inc(sem("z_ev"), 1)

            act.wait_ge(sem("f_abs"), 1)
            link(f(fscr[0:NFOX, 2, :], fscr[0:NFOX, 1, :], ACT.Exp))
            f(fscr[0:NFOX, 3, :], fscr[0:NFOX, 2, :], ACT.Ln, bias=1.0).then_inc(sem("f_ln"), 1)

            kst = [0, 0]
            per = [len([x for x in kv_stores(i) if x[0] == 0]) for i in range(4)]
            for i in range(5):
                if i >= 2:
                    kst[i % 2] += per[i - 2]
                    act.wait_ge(sem(f"st_k{i % 2}"), 16 * kst[i % 2])
                n = P if i < 4 else 32
                for g in range(2):
                    act.wait_ge(sem("kv_t"), 4 * i + g + 1)
                    A.copy(ktok[0:n, i % 2, 512 * g:512 * g + 512], banks[g][0:n, :]).then_inc(sem("kt_ev"), 1)

            for h in range(4):
                for kt in range(4):
                    c = slice(128 * kt, SEQ)
                    act.wait_ge(sem("sb_abs"), 4 * h + kt + 1)
                    link(f(sb_tmp[:, kt, c], sb_tmp[:, kt, c], ACT.Exp))
                    f(sb_tmp[:, kt, c], sb_tmp[:, kt, c], ACT.Ln, bias=1.0).then_inc(sem("sb_ln"), 1)
                for n, kt in enumerate((3, 2, 1, 0)):
                    c = slice(128 * kt, SEQ)
                    act.wait_ge(sem("sba_read"), 4 * h + n + 1)
                    f(sb_zm[:, kt, c], sb_zm[:, kt, c], ACT.Exp).then_inc(sem("sb_exp"), 1)
                act.wait_ge(sem("sbo_mm"), h + 1)
                o = 64 * (h % 2)
                A.copy(oT[o:o + 64, h // 2, 0:SEQ], banks[6 + h % 2][o:o + 64, :]).then_inc(sem("sbo_ev"), 1)

            def fox_rows(h):
                act.wait_ge(sem("nck_mm"), h + 1)
                if h >= 2:
                    act.wait_ge(sem("sc_ev"), 4 * (h - 1))
                A.copy(nck[:, h % 2, :], banks[6 + h % 2]).then_inc(sem("nck_ev"), 1)

            def weights(n):
                act.wait_ge(sem("mx_ready"), n + 1)
                s = sc_sb[:, n % 2, 0:units[n]["cols"]]
                f(s, s, ACT.Exp, bias=rowst[:, 1, n % 2:n % 2 + 1],
                  accum_out=rowst[:, 2, n % 2:n % 2 + 1]).then_inc(sem("ex"), 1)

            fox_rows(0)
            weights(0)
            for n, u in enumerate(units):
                if n % 4 == 0 and n // 4 + 1 < NFOX:
                    fox_rows(n // 4 + 1)
                if n + 1 < NU:
                    weights(n + 1)
                for tg in range(u["tg0"], u["tg1"]):
                    if tg % 2:
                        group_out(act, n, tg, A.copy, "tg_evA")
                done = [n - 1] if n < NU - 1 else [n - 1, n]
                for m in done:
                    if m >= 0 and units[m]["i"] == 3:
                        v = units[m]
                        act.wait_ge(sem("pv_mm"), m + 1)
                        A.copy(oT[v["off"]:v["off"] + 64, v["tile"], 0:SEQ],
                               banks[4 + v["head"] % 2][v["off"]:v["off"] + 64, :]).then_inc(sem("o_ev"), 1)

            act.wait_ge(sem("new_abs"), 1)
            link(f(s_lng[0:NT, :, 0:16], s_lng[0:NT, :, 0:16], ACT.Exp))
            f(s_lng[0:NT, :, 0:16], s_lng[0:NT, :, 0:16], ACT.Ln, bias=1.0).then_inc(sem("new_ln"), 1)
            act.wait_ge(sem("new_t"), 1)
            f(wnew[:, :, 0:16], wnew[:, :, 0:16], ACT.Exp).then_inc(sem("new_exp"), 1)

            def stick_logs(i, par):
                act.wait_ge(sem("z_abs"), i * 2 + (par + 1))
                link(f(s_y[:, par, 0:256], s_y[:, par, 0:256], ACT.Exp))
                f(s_y[:, par, 0:256], s_y[:, par, 0:256], ACT.Ln, bias=1.0).then_inc(sem("z_ln"), 1)

            def softmax_weights(i, par):
                act.wait_ge(sem("f_sub"), i * 2 + (par + 1))
                f(s_f[:, par, :], s_f[:, par, :], ACT.Exp)
                f(s_dl[:, par, :], s_dl[:, par, :], ACT.Exp)
                f(s_wn[0:NT, par, 16:64], s_wn[0:NT, par, 16:64], ACT.Exp).then_inc(sem("f_exp"), 1)

            def stick_weights(i, par):
                act.wait_ge(sem("t_ready"), i * 2 + (par + 1))
                f(s_w[:, par, 0:256], s_z[:, par, :], ACT.Exp).then_inc(sem("w_ready"), 1)

            with act.Fori(0, NB // 2) as i:
                link.enter(i, 2)
                for p in range(1, 18, 2):
                    keys_out(act, i, 0, p, A.copy)
                for p in range(1, 18, 2):
                    keys_out(act, i, 1, p, A.copy)
                    if p == 1:
                        stick_logs(i, 0)
                    if p == 9:
                        softmax_weights(i, 0)
                    if p == 11:
                        stick_weights(i, 0)
                stick_logs(i, 1)
                softmax_weights(i, 1)
                stick_weights(i, 1)
                link.leave(NB // 2)

            for n in range(24):
                act.wait_ge(sem("gate_mm"), n + 1)
                if n >= 2:
                    act.wait_ge(sem("br_ev"), n - 1)
                f(gsig[:, n % 2, 0:SEQ], banks[n % 2], ACT.Sigmoid)
                f(gsig[:, n % 2, SEQ:TOK], banks[2 + n % 2][:, 0:32], ACT.Sigmoid).then_inc(sem("gate_ev"), 1)

            act.wait_ge(sem("xo_ev"), 8)
            norm_root(1)
            act.wait_ge(sem("rt_sub"), 1)
            f(r_ge, r_ge, ACT.Exp).then_inc(sem("rt_exp"), 1)
            act.wait_ge(sem("rt_d"), 1)
            f(r_w2, r_w2, ACT.Exp).then_inc(sem("rt_dexp"), 1)
            for e in range(NEXP):
                act.wait_ge(sem("combB_mm"), e + 1)
                A.copy(combB[:, e, 0:SEQ], banks[3 + e % 2]).then_inc(sem("combB_ev"), 1)

            with act.Fori(0, NEXP // 2) as i:
                for u in range(2):
                    for ft in range(2):
                        act.wait_ge(sem(f"hid_mm{ft}"), i * 2 + (u + 1))
                        act.wait_ge(sem("hid_ev"), i * 2 + u)
                        last = f(gact[:, ft, 0:SEQ], banks[2 * ft], ACT.Silu)
                        if ft == 1:
                            for f2 in range(2):
                                last = f(gact[:, f2, SEQ:TOK], banks[4][:, 64 * f2:64 * f2 + 32], ACT.Silu)
                        last.then_inc(sem(f"gact{ft}"), 1)

            act.wait_ge(sem("x2_ev"), 1)
            norm_root(2)
            for i in range(5):
                n = P if i < 4 else 32
                act.wait_ge(sem("yo_t"), 2 * i + 2)
                if i >= 2:
                    act.wait_ge(sem(f"st_y{i % 2}"), 16 * (i // 2))
                A.copy(ystage[0:n, i % 2, 512:1024], banks[1][0:n, :]).then_inc(sem("yo_evA"), 1)
                act.wait_ge(sem("yo_evA"), i + 1)
                act.wait_ge(sem("yo_evD"), i + 1)
                if i < 4:
                    dst = O["y_prompt"][0, 128 * i:128 * i + 128, :]
                else:
                    dst = O["y_sample"].rearrange("b t d -> (b t) d")
                act.dma_start(dst, ystage[0:n, i % 2, :]).then_inc(sem(f"st_y{i % 2}"), 16)

        @block.vector
        def _(dve):
            link = Chain(dve, sem("dve_own"))

            def tt(out, a, b, op):
                return V.tensor_tensor(out, a, b, op)

            def ts(out, a, s1, s2, op0, op1=None):
                if op1 is None:
                    return V.tensor_scalar(out, a, s1, None, op0)
                return V.tensor_scalar(out, a, s1, s2, op0, op1)

            def stt(out, a, s, b, op0, op1):
                return V.scalar_tensor_tensor(out=out, in0=a, scalar=s, in1=b, op0=op0, op1=op1)

            V.memset(eps_sb[:, :], EPS)
            V.memset(lf_one, 1.0)
            link(V.memset(qbd[:, :, :], 0.0))
            dve.wait_ge(sem("c_e"), 1)
            link(ts(c_tmp[0:9, :], c_tmp[0:9, :], 1.0, None, ALU.add))
            link(V.reciprocal(c_tmp[0:9, :], c_tmp[0:9, :]))
            tt(c_tmp[0:9, :], c_tmp[0:9, :], c_raw[0:9, :], ALU.mult).then_inc(sem("c_silu"), 1)
            dve.wait_ge(sem("c_t"), 1)
            V.tensor_copy(vecT[:, :], banks[7][:, 128:200])
            V.tensor_copy(cT[:, :, :], banks[7][:, 0:72].rearrange("p (k n) -> p k n", n=9)).then_inc(sem("cT_ready"), 1)
            dve.wait_ge(sem("cT_ready"), 1)
            for k in range(1, KD, 2):
                dve.wait_ge(sem("x_t"), k + 1)
                V.tensor_copy(xT[:, k, 0:SEQ], banks[k % 4]).then_inc(sem("x_evD"), 1)
            dve.wait_ge(sem("x_t"), KD + 1)
            V.tensor_copy(xT[:, :, SEQ:TOK], banks[4][:, 0:256].rearrange("p (k n) -> p k n", n=32)
                          ).then_inc(sem("xs_ev"), 1)

            dve.wait_ge(sem("ld_lf"), 16)
            for h in range(NFOX):
                last = V.tensor_tensor_scan(lf_scan[:, h, :], lf_one, lf_page[:, :, h], 0.0, ALU.mult, ALU.add)
            link(last)
            V.tensor_copy(lf_tot[:, 0, :], lf_scan[:, :, P - 1]).then_inc(sem("lf_tot"), 1)
            dve.wait_ge(sem("lf_tot"), 1)

            def mod_out(bank, j):
                bm = vecT[:, j].unsqueeze(2).to_broadcast([P, 4, 9])
                return tt(modT[:, j, :], banks[bank][:, 0:36].rearrange("p (j n) -> p j n", n=9), bm, ALU.add)


            def gain(n, shift, norm):
                bn = vecT[:, norm:norm + 8].unsqueeze(2).to_broadcast([P, KD, 9])
                stt(gainA[:, :, :], modT[:, shift + 8:shift + 16, :], 1.0, bn, ALU.add, ALU.mult
                    ).then_inc(sem("gain"), 1)
                dve.wait_ge(sem("gain"), n + 1)

            def modulate(n, shift):
                dve.wait_ge(sem("rs"), n + 1)
                link(tt(hT[:, :, :], xT[:, :, :], rstd[:, :].unsqueeze(1).to_broadcast([P, KD, TOK]), ALU.mult))
                for k in range(KD):
                    ts(hT[:, k, 0:SEQ], hT[:, k, 0:SEQ], gainA[:, k, 0:1], modT[:, shift + k, 0:1], ALU.mult, ALU.add)
                hs = hT[:, :, SEQ:TOK].rearrange("p k (b t) -> p k b t", t=NT)
                link(tt(hs, hs, gainA[:, :, 1:9].unsqueeze(3).to_broadcast([P, KD, NB, NT]), ALU.mult))
                tt(hs, hs, modT[:, shift:shift + 8, 1:9].unsqueeze(3).to_broadcast([P, KD, NB, NT]), ALU.add
                   ).then_inc(sem("h_ready"), 1)

            for c in range(6):
                dve.wait_ge(sem("w_used"), c + 1)
                mod_out(c % 3, slice(4 * c, 4 * c + 4)).then_inc(sem("mod_ev"), 1)
            dve.wait_ge(sem("mod_ev"), 6)
            gain(0, 0, 48)
            modulate(0, 0)

            dve.wait_ge(sem("f_mm"), 1)
            dve.wait_ge(sem("ld_f"), 32)
            y, ya, yl = fscr[0:NFOX, 0, :], fscr[0:NFOX, 1, :], fscr[0:NFOX, 3, :]
            ts(y[:, 0:SEQ], banks[4][0:NFOX, :], bf_sb[:, 0:1], None, ALU.add)
            link(ts(y[:, SEQ:TOK], banks[5][0:NFOX, 0:32], bf_sb[:, 0:1], None, ALU.add))
            stt(ya, y, -1.0, y, ALU.mult, ALU.min).then_inc(sem("f_abs"), 1)
            dve.wait_ge(sem("f_ln"), 1)
            link(stt(logfT[0:NFOX, :], y, 0.0, yl, ALU.min, ALU.subtract))
            link(V.memset(ya, 1.0))
            V.tensor_tensor_scan(ncumT[0:NFOX, 0:SEQ], ya[:, 0:SEQ], logfT[0:NFOX, 0:SEQ], 0.0, ALU.mult, ALU.subtract)
            lfs = logfT[0:NFOX, SEQ:TOK].rearrange("p (b t) -> p b t", t=NT)
            ncs = ncumT[0:NFOX, SEQ:TOK].rearrange("p (b t) -> p b t", t=NT)
            last = link(ts(ncs[:, :, 0], lfs[:, :, 0], -1.0, None, ALU.mult))
            for t in range(1, NT):
                last = tt(ncs[:, :, t], ncs[:, :, t - 1], lfs[:, :, t], ALU.subtract)
                if t < NT - 1:
                    link(last)
            last.then_inc(sem("lf_rowT"), 1)
            dve.wait_ge(sem("lf_rowT"), 1)

            dve.wait_ge(sem("lf_late"), 1)
            link(tt(lf_tot[:, 1, :], lf_tot[:, 0, :], banks[7][:, 0:NFOX], ALU.add))
            for h in range(NFOX):
                last = ts(lf_scan[:, h, :], lf_scan[:, h, :], -1.0, lf_tot[:, 1, h:h + 1], ALU.mult, ALU.add)
            last.then_inc(sem("lf_after"), 1)

            with dve.Fori(0, 2) as i:
                for u in range(3):
                    dve.wait_ge(sem("w_used"), i * 3 + (7 + u))
                    bm = vecT[:, bass.ds(i * 12 + (24 + 4 * u), 4)].unsqueeze(2).to_broadcast([P, 4, 9])
                    tt(modT[:, bass.ds(i * 12 + (24 + 4 * u), 4), :],
                       banks[u][:, 0:36].rearrange("p (j n) -> p j n", n=9), bm, ALU.add).then_inc(sem("mod_ev"), 1)
            dve.wait_ge(sem("lf_tr"), 1)
            V.tensor_copy(fox_past[:, :, 0:4].rearrange("p a h -> p h a"),
                          banks[0].rearrange("p (h a) -> p h a", h=4))
            V.tensor_copy(fox_past[:, :, 4:6].rearrange("p a h -> p h a"),
                          banks[1][:, 0:256].rearrange("p (h a) -> p h a", h=2)).then_inc(sem("lf_past"), 1)
            dve.wait_ge(sem("lf_rowt"), 1)
            V.tensor_copy(lf_tok[:, 0:4, :], banks[6][:, 0:24].rearrange("p (i h) -> p i h", h=6))
            V.tensor_copy(lf_tok[0:32, 4, :], banks[6][0:32, 24:30])
            V.tensor_copy(ncn[:, :], banks[6][0:32, 32:38]).then_inc(sem("lf_rows"), 1)

            dve.wait_ge(sem("z_ev"), 24)
            for j, tile in enumerate(PAIR_TILES):
                for hh in range(2):
                    r = slice(64 * hh, 64 * hh + 64)
                    V.tensor_copy(qbd[r, :, 8 * j + 4 * hh:8 * j + 4 * hh + 4],
                                  zT[r, tile, SEQ:TOK].rearrange("p (b t) -> p b t", t=NT))
            for g in range(3):
                for hh in range(2):
                    r = slice(64 * hh, 64 * hh + 64)
                    last = V.tensor_copy(qbd[r, :, 40 + 8 * g + hh:48 + 8 * g:2],
                                         zT[r, 2 + g, SEQ:TOK].rearrange("p (b t) -> p b t", t=NT))
            last.then_inc(sem("qbd_ready"), 1)

            for i in range(5):
                n = P if i < 4 else 32
                for g in range(2):
                    dve.wait_ge(sem("kv_t"), 4 * i + g + 3)
                    V.tensor_copy(vtok[0:n, i, 512 * g:512 * g + 512], banks[2 + g][0:n, :]
                                  ).then_inc(sem("vt_ev"), 1)

            dve.wait_ge(sem("st_k0"), 16 * KST[0])
            dve.wait_ge(sem("st_k1"), 16 * KST[1])
            for h in range(4):
                for kt in range(4):
                    c, dg = slice(128 * kt, SEQ), slice(128 * kt, 128 * kt + 128)
                    dve.wait_ge(sem("sbz_mm"), 4 * h + kt + 1)
                    if h:
                        dve.wait_ge(sem("sbo_mm"), h)
                    ts(sb_zm[:, kt, c], banks[kt][:, c], SCALE, None, ALU.mult).then_inc(sem("sbz_read"), 1)
                    dve.wait_ge(sem("sbz_read"), 4 * h + kt + 1)
                    stt(sb_tmp[:, kt, c], sb_zm[:, kt, c], -1.0, sb_zm[:, kt, c], ALU.mult, ALU.min
                        ).then_inc(sem("sb_abs"), 1)
                for kt in range(4):
                    c, dg = slice(128 * kt, SEQ), slice(128 * kt, 128 * kt + 128)
                    dve.wait_ge(sem("sb_ln"), 4 * h + kt + 1)
                    link(stt(sb_sp[:, kt, c], sb_zm[:, kt, c], 0.0, sb_tmp[:, kt, c], ALU.max, ALU.add))
                    link(tt(sb_zm[:, kt, c], sb_zm[:, kt, c], sb_sp[:, kt, c], ALU.subtract))
                    last = tt(sb_sp[:, kt, dg], sb_sp[:, kt, dg], cs["strict_mul"], ALU.mult)
                last.then_inc(sem("sbsp"), 1)
                for n, kt in enumerate((3, 2, 1, 0)):
                    c = slice(128 * kt, SEQ)
                    dve.wait_ge(sem("sba_mm"), 4 * h + n + 1)
                    tt(sb_zm[:, kt, c], sb_zm[:, kt, c], banks[4 + n % 2][:, c], ALU.subtract
                       ).then_inc(sem("sba_read"), 1)
                for n, kt in enumerate((3, 2, 1, 0)):
                    dg = slice(128 * kt, 128 * kt + 128)
                    dve.wait_ge(sem("sb_exp"), 4 * h + n + 1)
                    last = tt(sb_zm[:, kt, dg], sb_zm[:, kt, dg], cs["strict_mul"], ALU.mult)
                last.then_inc(sem("sbw"), 1)

            dve.wait_ge(sem("ld_dt"), 16 * 7)
            dve.wait_ge(sem("sbo_mm"), 4)
            tab_at = {}
            k = 0
            for hh in range(2):
                for g in range(3):
                    tab_at[g, hh] = (k, DIL_COLS[g])
                    k += DIL_COLS[g]

            def logits(n):
                u = units[n]
                sc = sc_sb[:, n % 2, :]
                if n >= 2:
                    dve.wait_ge(sem("tg_mm"), units[n - 2]["tg1"])
                for s, (tile, k0, cols, at) in enumerate(u["subs"]):
                    c = u["sub0"] + s
                    dve.wait_ge(sem("sc_mm"), c + 1)
                    if u["kind"] == "fox":
                        dve.wait_ge(sem("nck_ev"), u["h"] + 1)
                        bias = nck[:, u["h"] % 2, 0:cols]
                    else:
                        t0, tn = tab_at[s, u["h"]]
                        bias = dil_tab[:, t0 + tn - cols:t0 + tn]
                    stt(sc[:, at:at + cols], banks[c % 2][:, 0:cols], SCALE, bias, ALU.mult, ALU.add
                        ).then_inc(sem("sc_ev"), 1)
                dve.wait_ge(sem("sc_ev"), u["sub1"])
                n_ = u["cols"]
                if u["kind"] == "fox":
                    link(tt(sc[:, n_ - 128:n_], sc[:, n_ - 128:n_], cs["causal_add"], ALU.add))
                V.tensor_reduce(rowst[:, 1, n % 2:n % 2 + 1], sc[:, 0:n_], AX, ALU.max, negate=True
                                ).then_inc(sem("mx_ready"), 1)

            logits(0)
            for n, u in enumerate(units):
                if n + 1 < NU:
                    logits(n + 1)
                dve.wait_ge(sem("ex"), n + 1)
                if n >= 2:
                    dve.wait_ge(sem("nrm"), n - 1)
                V.reciprocal(rowst[:, 3, n % 2:n % 2 + 1], rowst[:, 2, n % 2:n % 2 + 1]).then_inc(sem("rs_ready"), 1)
                for tg in range(u["tg0"], u["tg1"]):
                    if tg % 2 == 0:
                        group_out(dve, n, tg, V.tensor_copy, "tg_evD")

            dve.wait_ge(sem("new_mm"), 1)
            dve.wait_ge(sem("ld_nc"), 16)
            dve.wait_ge(sem("pv_mm"), NU)
            nv = banks[0][0:NT, :].rearrange("p (b n) -> p b n", n=64)
            link(ts(wnew[:, :, 0:16], nv[:, :, 0:16], SCALE, None, ALU.mult))
            stt(s_lng[0:NT, :, 0:16], wnew[:, :, 0:16], -1.0, wnew[:, :, 0:16], ALU.mult, ALU.min
                ).then_inc(sem("new_abs"), 1)
            link(stt(wnew[:, :, 16:64], nv[:, :, 16:64], SCALE,
                     cs["new_add"][0:NT, 16:64].unsqueeze(1).to_broadcast([NT, NB, 48]), ALU.mult, ALU.add))
            fx = wnew[:, :, 16:40].rearrange("p b (h t) -> p b h t", t=NT)
            link(tt(fx, fx, lfnew[:, :, :].unsqueeze(3).to_broadcast([NT, NB, NFOX, NT]), ALU.add))
            V.tensor_copy(mnew[:, :, 0:24], wnew[:, :, 16:40])
            V.tensor_reduce(mnew[:, :, 24:32], wnew[:, :, 40:64].rearrange("p b (g c) -> p b c g", g=3), AX, ALU.max)
            dve.wait_ge(sem("new_ln"), 1)
            link(stt(spnew[:, :, :], wnew[:, :, 0:16], 0.0, s_lng[0:NT, :, 0:16], ALU.max, ALU.add))
            link(tt(wnew[:, :, 0:16], wnew[:, :, 0:16], spnew[:, :, :], ALU.subtract))
            strict = cs["new_strict"][0:NT, :].unsqueeze(1).to_broadcast([NT, NB, 16])
            tt(spnew[:, :, :], spnew[:, :, :], strict, ALU.mult).then_inc(sem("spn_ready"), 1)
            dve.wait_ge(sem("new_a"), 1)
            tt(wnew[:, :, 0:16], wnew[:, :, 0:16], banks[1][0:NT, 0:128].rearrange("p (b n) -> p b n", n=16),
               ALU.subtract).then_inc(sem("new_t"), 1)
            dve.wait_ge(sem("new_exp"), 1)
            tt(wnew[:, :, 0:16], wnew[:, :, 0:16], strict, ALU.mult).then_inc(sem("new_ready"), 1)
            dve.wait_ge(sem("new_ready"), 1)

            def take(i, par):
                b = i * 2 + par
                V.tensor_copy(qcur[:, par, :], qbd[:, bass.ds(b, 1), :].rearrange("p o n -> p (o n)")
                              ).then_inc(sem("qcur"), 1)
                V.tensor_copy(s_sn[0:NT, par, :], spnew[:, bass.ds(b, 1), :].rearrange("p o n -> p (o n)"))
                link(V.tensor_copy(s_wn[0:NT, par, :], wnew[:, bass.ds(b, 1), :].rearrange("p o n -> p (o n)")))

            def read_scores(i, par):
                dve.wait_ge(sem("seq_s"), i * 2 + (par + 1))
                for half in range(2):
                    v = banks[4 + half][:, 0:320].rearrange("p (a n) -> p a n", n=40)
                    ts(s_z[:, par, 128 * half:128 * half + 128].rearrange("p (a n) -> p a n", n=16),
                       v[:, :, 0:16], SCALE, None, ALU.mult)
                    after = fox_past[:, bass.ds(i * 32 + (16 * par + 8 * half), 8), :]
                    stt(s_f[:, par, 192 * half:192 * half + 192].rearrange("p (a h t) -> p a h t", h=NFOX, t=NT),
                        v[:, :, 16:40].rearrange("p a (h t) -> p a h t", t=NT), SCALE,
                        after.unsqueeze(3).to_broadcast([P, 8, NFOX, NT]), ALU.mult, ALU.add)
                stt(s_dl[:, par, :], banks[5][:, 320:344], SCALE, cs["dil_past"], ALU.mult, ALU.add
                    ).then_inc(sem("s_read"), 1)
                dve.wait_ge(sem("s_read"), i * 2 + (par + 1))
                stt(s_y[:, par, 0:256], s_z[:, par, :], -1.0, s_z[:, par, :], ALU.mult, ALU.min).then_inc(sem("z_abs"), 1)
                V.tensor_reduce(s_m[:, par, 0:24], s_f[:, par, :].rearrange("p (a c) -> p c a", c=24), AX, ALU.max)
                link(V.tensor_reduce(s_m[:, par, 24:32], s_dl[:, par, :].rearrange("p (g c) -> p c g", g=3),
                                     AX, ALU.max))
                tt(s_m[0:NT, par, :], s_m[0:NT, par, :],
                   mnew[:, bass.ds(i * 2 + par, 1), :].rearrange("p o n -> p (o n)"), ALU.max
                   ).then_inc(sem("m_ready"), 1)

            def softplus(i, par):
                dve.wait_ge(sem("z_ln"), i * 2 + (par + 1))
                stt(s_sp[:, par, 0:256], s_z[:, par, :], 0.0, s_y[:, par, 0:256], ALU.max, ALU.add
                    ).then_inc(sem("sp_ready"), 1)
                dve.wait_ge(sem("sp_ready"), i * 2 + (par + 1))
                link(tt(s_z[:, par, :], s_z[:, par, :], s_sp[:, par, 0:256], ALU.subtract))

            def top(i, par):
                dve.wait_ge(sem("m_t"), i * 2 + (par + 1))
                link(V.tensor_reduce(s_mx[0:32, par, :], banks[6][0:32, 256:384], AX, ALU.max))
                ts(s_dg[0:32, par, :], ident[0:32, 0:32], s_mx[0:32, par, 0:1], None, ALU.mult
                   ).then_inc(sem("dg_ready"), 1)

            def less_top(i, par):
                dve.wait_ge(sem("m_b"), i * 2 + (par + 1))
                f = s_f[:, par, :].rearrange("p (a c) -> p a c", c=24)
                tt(f, f, banks[6][:, 384:408].unsqueeze(1).to_broadcast([P, PAGES, 24]), ALU.subtract)
                d = s_dl[:, par, :].rearrange("p (g c) -> p g c", g=3)
                tt(d, d, banks[6][:, 408:416].unsqueeze(1).to_broadcast([P, 3, 8]), ALU.subtract)
                w = s_wn[0:NT, par, :]
                tt(w[:, 16:40], w[:, 16:40], banks[6][0:NT, 384:408], ALU.subtract)
                w = w[:, 40:64].rearrange("p (g c) -> p g c", g=3)
                tt(w, w, banks[6][0:NT, 408:416].unsqueeze(1).to_broadcast([NT, 3, 8]), ALU.subtract
                   ).then_inc(sem("f_sub"), 1)

            def row_sums(i, par):
                dve.wait_ge(sem("f_exp"), i * 2 + (par + 1))
                V.tensor_reduce(s_r[:, par, 0:24], s_f[:, par, :].rearrange("p (a c) -> p c a", c=24), AX, ALU.add)
                V.tensor_reduce(s_r[:, par, 24:32], s_dl[:, par, :].rearrange("p (g c) -> p c g", g=3), AX, ALU.add)
                V.tensor_copy(s_rn[0:NT, par, 0:24], s_wn[0:NT, par, 16:40])
                V.tensor_reduce(s_rn[0:NT, par, 24:32], s_wn[0:NT, par, 40:64].rearrange("p (g c) -> p c g", g=3),
                                AX, ALU.add).then_inc(sem("r_ready"), 1)

            def less_sticks(i, par):
                dve.wait_ge(sem("a_mm"), i * 2 + (par + 1))
                tt(s_z[:, par, :], s_z[:, par, :], banks[7][:, 64:320], ALU.subtract).then_inc(sem("t_ready"), 1)

            def inverse(i, par):
                dve.wait_ge(sem("l_mm"), i * 2 + (par + 1))
                link(V.reciprocal(s_li[:, par, :], banks[6][:, 416:448]))

            def write_out(i, par):
                dve.wait_ge(sem("seq_pv"), i * 2 + (par + 1))
                c = bass.ds(i * 8 + (SEQ + 4 * par), NT)
                for hh in range(2):
                    r = slice(64 * hh, 64 * hh + 64)
                    pair = banks[7][r, 0:40].rearrange("p (j n) -> p j n", n=8)[:, :, 4 * hh:4 * hh + 4]
                    V.tensor_copy(oT[r, 0:2, c], pair[:, 0:2])
                    li = s_li[r, par, 0:24].rearrange("p (j n) -> p j n", n=8)[:, :, 4 * hh:4 * hh + 4]
                    tt(oT[r, 3:6, c], pair[:, 2:5], li, ALU.mult)
                    last = tt(oT[r, 2, c], banks[7][r, 40 + hh:48:2], s_li[r, par, 24 + hh:32:2], ALU.mult)
                last.then_inc(sem("seq_out"), 1)

            with dve.Fori(0, NB // 2) as i:
                link.enter(i, 10)
                take(i, 0)
                take(i, 1)
                for p in range(0, 18, 2):
                    keys_out(dve, i, 0, p, V.tensor_copy)
                read_scores(i, 0)
                steps = {2: (softplus,), 4: (top,), 8: (less_top,), 10: (row_sums, less_sticks), 14: (inverse,)}
                for p in range(0, 18, 2):
                    keys_out(dve, i, 1, p, V.tensor_copy)
                    for step in steps.get(p, ()):
                        step(i, 0)
                read_scores(i, 1)
                softplus(i, 1)
                write_out(i, 0)
                for step in (top, less_top, row_sums, less_sticks, inverse, write_out):
                    step(i, 1)
                link.leave(NB // 2)

            for n in range(24):
                half, b, j = n // 12, (n // 4) % 3, n % 4
                m = 4 * half + j
                dve.wait_ge(sem("gate_ev"), n + 1)
                for c, bk in ((slice(0, SEQ), banks[4 + n % 2]), (slice(SEQ, TOK), banks[6 + n % 2][:, 0:32])):
                    out = merged[:, m, c] if b == 0 else btmp[:, n % 2, c]
                    last = tt(out, gsig[:, n % 2, c], bk, ALU.mult)
                    if b:
                        link(last)
                        last = tt(merged[:, m, c], merged[:, m, c], btmp[:, n % 2, c], ALU.add)
                last.then_inc(sem("br_ev"), 1)

            def add_gated(m, gate, main, smp, src_sb):
                stt(xT[:, m, 0:SEQ], main, modT[:, gate + m, 0:1], xT[:, m, 0:SEQ], ALU.mult, ALU.add)
                g = modT[:, gate + m, 1:9].unsqueeze(2).to_broadcast([P, NB, NT])
                link(tt(upd_s[:, m, :].rearrange("p (b t) -> p b t", t=NT),
                        smp.rearrange("p (b t) -> p b t", t=NT), g, ALU.mult))
                return tt(xT[:, m, SEQ:TOK], xT[:, m, SEQ:TOK], upd_s[:, m, :], ALU.add)

            for m in range(KD):
                dve.wait_ge(sem("xo_mm"), m + 1)
                add_gated(m, 16, banks[m % 2], banks[2 + m % 2][:, 0:32], False).then_inc(sem("xo_ev"), 1)
            dve.wait_ge(sem("xo_ev"), 8)
            gain(1, 24, 56)
            modulate(1, 24)

            dve.wait_ge(sem("ld_r"), 64)
            link(V.memset(r_lg, 0.0))
            dve.wait_ge(sem("rt_mm"), 1)
            tt(r_lg[:, 0:4, :], banks[0][:, 0:80].rearrange("p (i n) -> p i n", n=20),
               br_sb[:, :].unsqueeze(1).to_broadcast([P, 4, 20]), ALU.add)
            link(tt(r_lg[0:32, 4, :], banks[0][0:32, 80:100], br_sb[0:32, :], ALU.add))

            def wide(a):
                return a.unsqueeze(2).to_broadcast([P, 5, 4])

            count4 = cs["count4"].rearrange("p (i n) -> p i n", n=4)

            def first_max(val, mx, oh):
                link(V.tensor_reduce(mx, val, AX, ALU.max))
                link(tt(r_t, val, wide(mx), ALU.is_ge))
                link(stt(r_t, r_t, -100.0, count4, ALU.mult, ALU.add))
                link(V.tensor_reduce(r_g1, r_t, AX, ALU.min))
                link(tt(oh, r_t, wide(r_g1), ALU.is_equal))

            gl = r_lg[:, :, 0:4]
            first_max(gl, r_m, r_oh)
            tt(r_ge, gl, wide(r_m), ALU.subtract).then_inc(sem("rt_sub"), 1)
            ohe = r_oh.unsqueeze(2).to_broadcast([P, 5, 4, 4])
            link(tt(r_pr, r_lg[:, :, 4:20].rearrange("p i (g e) -> p i e g", g=4), ohe, ALU.mult))
            link(V.tensor_reduce(r_es, r_pr, AX, ALU.add))
            first_max(r_es, r_m1, r_oh1)
            link(stt(r_es, r_oh1, NEG, r_es, ALU.mult, ALU.add))
            first_max(r_es, r_m2, r_oh2)
            tt(r_w2, r_m2, r_m1, ALU.subtract).then_inc(sem("rt_d"), 1)
            dve.wait_ge(sem("rt_exp"), 1)
            link(V.tensor_reduce(r_gg, r_ge, AX, ALU.add))
            dve.wait_ge(sem("rt_dexp"), 1)
            link(stt(r_gg, r_w2, 1.0, r_gg, ALU.add, ALU.mult))
            link(V.reciprocal(r_g1, r_gg))
            link(tt(r_w2, r_w2, r_g1, ALU.mult))
            link(tt(r_oh1, r_oh1, wide(r_g1), ALU.mult))
            link(tt(r_oh2, r_oh2, wide(r_w2), ALU.mult))
            link(tt(r_ce, r_oh1, r_oh2, ALU.add))
            tt(comb_all.rearrange("p i (g e) -> p i g e", g=4), r_oh.unsqueeze(3).to_broadcast([P, 5, 4, 4]),
               r_ce.unsqueeze(2).to_broadcast([P, 5, 4, 4]), ALU.mult).then_inc(sem("comb_ready"), 1)
            dve.wait_ge(sem("comb_t"), 1)
            V.tensor_copy(combT[0:16, 0:SEQ], banks[1][0:16, :])
            V.tensor_copy(combT[0:16, SEQ:TOK], banks[2][0:16, 0:32]).then_inc(sem("combT_ready"), 1)
            link(V.memset(yT, 0.0))
            dve.wait_ge(sem("combB_mm"), 16)
            V.tensor_copy(combB[:, :, SEQ:TOK], banks[5].rearrange("p (e n) -> p e n", n=32)
                          ).then_inc(sem("combBs_ev"), 1)
            dve.wait_ge(sem("combBs_ev"), 1)
            dve.wait_ge(sem("combB_ev"), 16)

            with dve.Fori(0, NEXP // 2) as i:
                link.enter(i, 8)
                for u in range(2):
                    cb = combB[:, bass.ds(i * 2 + u, 1), :].rearrange("p o n -> p (o n)")
                    for ft in range(2):
                        dve.wait_ge(sem(f"gact{ft}"), i * 2 + (u + 1))
                        link(tt(gact[:, ft, 0:SEQ], gact[:, ft, 0:SEQ], cb[:, 0:SEQ], ALU.mult))
                        last = tt(hid[:, 2 * u + ft, 0:SEQ], gact[:, ft, 0:SEQ], banks[2 * ft + 1], ALU.mult)
                    for ft in range(2):
                        link(tt(gact[:, ft, SEQ:TOK], gact[:, ft, SEQ:TOK], cb[:, SEQ:TOK], ALU.mult))
                        last = tt(hid[:, 2 * u + ft, SEQ:TOK], gact[:, ft, SEQ:TOK],
                                  banks[4][:, 64 * ft + 32:64 * ft + 64], ALU.mult)
                    last.then_inc(sem("hid_ev"), 1)
                    for m in range(KD):
                        dve.wait_ge(sem("y_mm"), i * 16 + (8 * u + m + 1))
                        tt(yT[:, m, 0:SEQ], yT[:, m, 0:SEQ], banks[6 + m % 2], ALU.add).then_inc(sem("y_ev"), 1)
                    tt(yT[:, :, SEQ:TOK], yT[:, :, SEQ:TOK],
                       banks[5][:, 0:256].rearrange("p (m n) -> p m n", n=32), ALU.add).then_inc(sem("ys_ev"), 1)
                link.leave(NEXP // 2)
            dve.wait_ge(sem("ys_ev"), NEXP)
            dve.wait_ge(sem("y_ev"), 8 * NEXP)
            for m in range(KD):
                last = add_gated(m, 40, yT[:, m, 0:SEQ], yT[:, m, SEQ:TOK], True)
            last.then_inc(sem("x2_ev"), 1)
            dve.wait_ge(sem("x2_ev"), 1)

            dve.wait_ge(sem("rs"), 3)
            link(tt(hT[:, :, :], xT[:, :, :], rstd[:, :].unsqueeze(1).to_broadcast([P, KD, TOK]), ALU.mult))
            for k in range(KD):
                last = ts(hT[:, k, :], hT[:, k, :], vecT[:, 64 + k:65 + k], None, ALU.mult)
            last.then_inc(sem("h_ready"), 1)
            for i in range(5):
                n = P if i < 4 else 32
                dve.wait_ge(sem("yo_t"), 2 * i + 1)
                if i >= 2:
                    dve.wait_ge(sem(f"st_y{i % 2}"), 16 * (i // 2))
                V.tensor_copy(ystage[0:n, i % 2, 0:512], banks[0][0:n, :]).then_inc(sem("yo_evD"), 1)


_OUTS = [("y_prompt", (1, SEQ, D)), ("y_sample", (NB, NT, D)),
         ("kv_prompt", (1, 1, SEQ, 2, 10, HD)), ("logf_prompt", (1, 1, SEQ, NFOX)),
         ("dil1_prompt", (1, 1, 128, 2, 2, HD)), ("dil2_prompt", (1, 1, 512, 2, 2, HD)),
         ("dil3_prompt", (1, 1, 512, 2, 2, HD)),
         ("kv_sample", (NB, 1, NT, 2, 10, HD)), ("logf_sample", (NB, 1, NT, NFOX)),
         ("dil1_sample", (NB, 1, 128, 2, 2, HD)), ("dil2_sample", (NB, 1, 512, 2, 2, HD)),
         ("dil3_sample", (NB, 1, 2048, 2, 2, HD))]


def program(nc, arrays):
    ins = {n: nc.dram_tensor(f"in_{n}", a.shape, mybir.dt.from_np(a.dtype), kind="ExternalInput").ap()
           for n, a in arrays.items()}
    outs = {n: nc.dram_tensor(f"out_{n}", s, F32, kind="ExternalOutput").ap() for n, s in _OUTS}
    trunk_kernel(nc, ins, outs)


def kernel(**inputs):
    import concourse.bacc as _bacc
    from concourse.bass_utils import run_bass_kernel_spmd as _run

    nc = _bacc.Bacc("TRN2", target_bir_lowering=False, num_devices=1)
    arrays = {n: np.ascontiguousarray(a) for n, a in inputs.items()}
    arrays["const"] = const_table()[1]
    program(nc, arrays)
    r = _run(nc, [{f"in_{n}": a for n, a in arrays.items()}], core_ids=[0])
    return tuple(r.results[0][f"out_{n}"] for n, _ in _OUTS)
```

```python
import numpy as np
import concourse.bass as bass
from concourse import mybir
from contextlib import ExitStack

F32 = mybir.dt.float32
I32 = mybir.dt.int32
ALU = mybir.AluOpType
ACT = mybir.ActivationFunctionType
AX = mybir.AxisListType.X

P = 128
D = 1024
KD = D // P
SEQ = 512
NB = 8
NT = 4
TOK = SEQ + NB * NT
PAGES = 16
HD = 64
SCALE = HD ** -0.5
EPS = 1e-6
NEG = -1e30
MIX = 1024
QTILES = SEQ // P
NFOX = 6
NEXP = 16
DE = 256
PAIR_TILES = (0, 1, 5, 6, 7)
SLOPES = [[2.0 ** (-8.0 * (2 * g + h + 1) / 6) for h in range(2)] for g in range(3)]
DILATION = (1, 4, 16)
DIL_COLS = (256, 512, 512)
TOP = 2
CHUNKS = NEXP + (TOP * TOK - NEXP) // P
RING = 3
PAD_ROW = 4 * TOP * TOK


def const_table():
    parts, at = {}, 0
    r = np.arange(P)[:, None].astype(np.float64)
    c = np.arange(P)[None, :].astype(np.float64)
    tabs = {
        "ident": (r == c) * 1.0,
        "ones": np.ones((P, P)),
        "later_key": (r > c) * 1.0,
        "later_page": ((r > c) & (r // PAGES == c // PAGES)) * 1.0,
        "causal_add": np.where(c > r, NEG, 0.0),
        "strict_mul": (r < c) * 1.0,
    }
    for hh in range(2):
        for g in range(3):
            n = DIL_COLS[g]
            dist = r - (np.arange(n)[None, :] - (n - P))
            ok = (dist >= 0) & (dist % DILATION[g] == 0)
            if g == 0:
                ok &= dist <= 128
            tabs[f"dil{g}{hh}"] = np.where(ok, -SLOPES[g][hh] * dist, NEG)
    sd = np.zeros((P, 3, NT, 2))
    for g in range(3):
        for t in range(NT):
            for hh in range(2):
                dist = (128 + t - r[:, 0]) if g == 0 else DILATION[g] * (128 - r[:, 0])
                sd[:, g, t, hh] = np.where(dist <= 128 * DILATION[g], -SLOPES[g][hh] * dist, NEG)
    tabs["dil_past"] = sd.reshape(P, 24)
    nb = np.zeros((P, 64))
    sm = np.zeros((P, 16))
    for s in range(NT):
        for t in range(NT):
            for h in range(4):
                sm[s, 4 * h + t] = float(s < t)
            for h in range(NFOX):
                nb[s, 16 + 4 * h + t] = 0.0 if s <= t else NEG
            for g in range(3):
                for hh in range(2):
                    ok = (s <= t) if g == 0 else (s == t)
                    nb[s, 40 + 8 * g + 2 * t + hh] = -SLOPES[g][hh] * (t - s) if ok else NEG
    tabs["new_add"] = nb
    tabs["new_strict"] = sm
    sel = np.zeros((P, NFOX, P))
    for h in range(NFOX):
        sel[h, h] = 1.0
    tabs["pick_head"] = sel.reshape(P, NFOX * P)
    ids = np.zeros((P, 5 + CHUNKS))
    ids[:, 0:5] = r + 128 * np.arange(5)
    ids[:, 5:] = np.arange(CHUNKS)
    tabs["moe_ids"] = ids
    tabs["slot_pad"] = np.tile([0.0, PAD_ROW, 0.0, 0.0], (P, CHUNKS))
    tabs["fold4"] = (np.arange(P)[:, None] % 32 == np.arange(8)[None, :]) * 1.0
    tabs["count4"] = np.tile(np.arange(4.0), (P, 5))
    for n, t in tabs.items():
        parts[n] = (at, at + t.shape[1])
        at += t.shape[1]
    return parts, np.concatenate([t for t in tabs.values()], axis=1).astype(np.float32)


SMALL = ("ident", "ones", "later_key", "later_page", "causal_add", "strict_mul", "dil_past", "new_add",
         "new_strict", "fold4", "count4")


SERIES = {
    "forget_rows": ("lf_rowT", "lf_rowt", "lf_rows"),
    "past_steps": ("lf_tot", "lf_late", "lf_after", "lf_tr", "lf_past"),
    "own_keys": ("new_mm", "new_abs", "new_ln", "spn_ready", "new_a", "new_t", "new_exp", "new_ready"),
    "routing": ("rt_part", "lg_rows", "rt_mm", "comb_ready", "rank_mm", "dest_ready", "exp_id"),
    "rt_dve": ("rt_sub", "rt_d"),
    "rt_act": ("rt_exp", "rt_dexp"),
    "c_steps": ("c_e", "c_silu", "c_t", "cT_ready"),
    "f_steps": ("f_mm", "f_abs", "f_ln"),
}


class Chain:

    def __init__(self, eng, sem):
        self.eng, self.sem, self.n, self.turn = eng, sem, 0, 0

    def __call__(self, ins):
        ins.then_inc(self.sem, 1)
        self.n += 1
        self.eng.wait_ge(self.sem, self.turn + self.n)

    def enter(self, i, per):
        self.turn, self.at, self.per = i * per, self.n, per

    def leave(self, turns):
        assert self.n - self.at == self.per, (self.n - self.at, self.per)
        self.turn, self.n = 0, self.at + turns * self.per



ARENA = 24128


def trunk_kernel(nc, I, O):
    parts, _ = const_table()
    ctx = ExitStack()
    with ctx:
        def sb(name, shape, dt=F32):
            return ctx.enter_context(nc.sbuf_tensor(name, shape, dt))

        sems = {}

        def sem(name):
            if name not in sems:
                sems[name] = ctx.enter_context(nc.semaphore(name))
            return sems[name]

        def done_at(name):
            for series, names in SERIES.items():
                if name in names:
                    return sem(series), names.index(name) + 1

        xT = sb("xT", [P, KD, TOK])
        hT = sb("hT", [P, KD, TOK])
        oT = sb("oT", [P, 6, TOK])
        modT = sb("modT", [P, 48, 9])
        vecT = sb("vecT", [P, 72])
        gainA = sb("gainA", [P, KD, 9])
        rstd = sb("rstd", [P, TOK])
        small = sb("small", [P, sum(parts[n][1] - parts[n][0] for n in SMALL)])
        wring = sb("wring", [P, 3, 4096])
        wr_sb = sb("wr_sb", [P, KD, 32])
        br_sb = sb("br_sb", [P, 20])
        qbd = sb("qbd", [P, NB, 64])
        wnew = sb("wnew", [NT, NB, 64])
        mnew = sb("mnew", [NT, NB, 32])
        spnew = sb("spnew", [NT, NB, 16])
        fox_past = sb("fox_past", [P, P, NFOX])
        ptab = sb("ptab", [1, P], I32)
        pidx = sb("pidx", [P, 1], I32)
        wf_sb = sb("wf_sb", [P, KD, NFOX])
        bf_sb = sb("bf_sb", [NFOX, 1])
        eps_sb = sb("eps_sb", [P, 1])
        ncn = sb("ncn", [NB * NT, NFOX])
        lfnew = sb("lfnew", [NT, NB, NFOX])
        arena = sb("arena", [P, ARENA])
        vs_d = nc.dram_tensor("v_sample_rows", [NB * NT, 1024], F32, kind="Internal").ap()
        h_d = nc.dram_tensor("expert_in_rows", [TOK, D], F32, kind="Internal").ap()
        slots_d = nc.dram_tensor("expert_slots", [CHUNKS * P, 4], F32, kind="Internal").ap()
        y_d = nc.dram_tensor("expert_out_rows", [TOP * TOK, D], F32, kind="Internal").ap()
        nc_d = nc.dram_tensor("ncum_sample_rows", [NB * NT, NFOX], F32, kind="Internal").ap()

        cs = {}
        off = 0
        for n in SMALL:
            w = parts[n][1] - parts[n][0]
            cs[n] = small[:, off:off + w]
            off += w
        ident, ones, later_key, later_page = (cs[n] for n in ("ident", "ones", "later_key", "later_page"))

        def place(at, *shape):
            n = int(np.prod(shape))
            assert at + n <= ARENA, (at, shape)
            a = arena[:, at:at + n]
            if len(shape) == 2:
                a = a.rearrange("p (a b) -> p a b", b=shape[1])
            if len(shape) == 3:
                a = a.rearrange("p (a b c) -> p a b c", b=shape[1], c=shape[2])
            return a

        xin = place(0, 5, D)
        c_raw = place(5120, D)
        c_tmp = place(6144, D)
        rows72 = place(7168, P)
        mod_rows = place(18176, 3, 512)
        cT = place(19800, KD, 32)
        lf_page = place(13056, P, NFOX)
        lf_scan = place(13824, NFOX, P)
        lf_one = place(14592, P)
        lf_tot = place(14720, 2, NFOX)
        zT = place(0, 24, TOK)
        vtok = place(13056, 5, 1024)
        dil_tab = place(20224, 2560)
        pick_head = place(22784, 768)
        ncumT = place(23552, TOK)
        logfT = place(14800, TOK)
        fscr = place(15400, 4, TOK)
        flat_ring = wring[:, :, :].rearrange("p a b -> p (a b)")
        ktok = [place(18176, 1024), place(19200, 1024)] + \
            [flat_ring[:, a:a + 1024] for a in (10240, 11264, 2048)]
        sc_sb = flat_ring[:, 3072:3072 + 3 * 1280].rearrange("p (a b) -> p a b", a=3)
        nck = place(11264, 2, SEQ)
        pTb = place(12288, 2, 256)
        rowst = place(12800, 4, 3)
        pTa = place(8704, 2, 1024)
        sb_at = ((place(8704, 4, SEQ), place(10752, 4, SEQ), flat_ring[:, 0:2048].rearrange("p (a b) -> p a b", a=4)),
                 tuple(flat_ring[:, 4096 + 2048 * n:6144 + 2048 * n].rearrange("p (a b) -> p a b", a=4)
                       for n in range(3)))
        sb_sp, sb_zm, sb_tmp = zip(*sb_at)
        lf_tok = place(24096, 5, NFOX)
        kring = place(0, 4, 640)
        v_even = place(2560, PAGES, 640)
        v_odd = wring[:, :, :].rearrange("p a b -> p (a b)")[:, 0:PAGES * 640].rearrange("p (a b) -> p a b", b=640)
        vpast = (v_even, v_odd)
        kT5 = place(12800, 5, 512)
        dbuf = place(15360, 2, 2304)
        vncur = place(19968, 1024)
        rest = wring[:, :, :].rearrange("p a b -> p (a b)")[:, PAGES * 640:]
        row_a = rest[:, 0:512]
        row_b = rest[:, 512:1024]
        qcur = rest[:, 1024:1536].rearrange("p (a j n) -> p a j n", a=2, j=8)
        s_o = rest[:, 1536:1920]
        at = [20992]

        def next_place(*shape):
            at[0] += int(np.prod(shape))
            return place(at[0] - int(np.prod(shape)), *shape)

        s_z = next_place(256)
        s_sp = next_place(256 + 16)
        s_y = next_place(256 + 64)
        s_w = next_place(2, 256 + 128)
        s_f = next_place(2, 384)
        s_lng = s_f[0:NT, :, :].rearrange("p a b -> p (a b)")[:, 0:512].rearrange("p (b n) -> p b n", n=64)
        s_dl = next_place(2, 24)
        s_dx = next_place(4, 40)
        s_m = next_place(2, 32)
        s_r = next_place(2, 32)
        s_li = next_place(2, 32)
        s_dg = next_place(2, 32)
        s_mx = next_place(2, 1)
        s_rn = next_place(2, 32)
        s_wn = next_place(2, 64)
        s_sn = next_place(2, 16)
        wbr = place(0, 6, 1024)
        merged = place(6144, KD, TOK)
        gsig = place(10496, 2, TOK)
        btmp = place(11584, 2, TOK)
        upd_s = place(12700, KD, NB * NT)
        wdown = place(0, RING, 2048)
        xrow = place(6144, RING, D)
        xg = place(9216, RING, D)
        hidr = place(13056, RING, DE)
        sil = place(13824, RING, DE)
        hidT = place(14592, RING, DE)
        ychunk = place(15360, RING, D)
        slot_t = place(18432, CHUNKS + 2, 4)
        pay = place(18540, 10, 4)
        hrow = place(18580, 2, D)
        moe_ids = place(20632, 5 + CHUNKS)
        tok_now = place(20664, RING).bitcast(I32)
        row_now = place(20668, RING).bitcast(I32)
        dest_i = place(20708, 10).bitcast(I32)
        exp_id = place(20720, CHUNKS).bitcast(I32)
        gate_now = place(20744, RING)
        lg_rows = place(20760, TOK)
        carried = place(20748, 1)
        yrow = place(0, 5, 2 * D)
        rt = place(22496, 1500)

        def rtv(at, n):
            return rt[:, at:at + 5 * n].rearrange("p (i n) -> p i n", n=n)

        r_lg, r_ge, r_oh, r_t = rtv(0, 20), rtv(100, 4), rtv(120, 4), rtv(140, 4)
        r_pr = rt[:, 160:240].rearrange("p (i e g) -> p i e g", e=4, g=4)
        r_es, r_oh1, r_oh2, r_ce = rtv(240, 4), rtv(260, 4), rtv(280, 4), rtv(300, 4)
        r_m, r_gg, r_m1, r_m2, r_w2, r_g1 = (rt[:, 320 + 5 * n:325 + 5 * n] for n in range(6))
        r_a = rt[:, 400:560].rearrange("p (k i e) -> p k i e", k=TOP, e=NEXP)
        r_b, r_sb, r_sel = rtv(560, 16), rtv(640, 16), rtv(720, 16)
        r_n, r_end, r_st = (rt[:, 800 + 16 * n:816 + 16 * n] for n in range(3))
        r_dest = rt[:, 850:860].rearrange("p (i k) -> p i k", k=TOP)
        r_eid = rt[:, 860:860 + CHUNKS]
        r_tot = rt[:, 1290:1386].rearrange("p (i e) -> p i e", e=NEXP)
        r_cmp = rt[:, 900:900 + 16 * CHUNKS].rearrange("p (c e) -> p c e", e=NEXP)
        ystage = place(13056, 2, 1024)

        psum = ctx.enter_context(nc.psum_tensor("psum", [P, 8, 512], F32))
        banks = [psum[:, i, :] for i in range(8)]
        HALF = TOK // 2

        def halves(bank, rows=P):
            return psum[0:rows, bank:bank + 2, 0:HALF]

        def as_halves(a):
            return a.rearrange("p (a b) -> p a b", a=2)

        T = nc.tensor
        V = nc.vector
        A = nc.scalar

        units = []
        for h in range(NFOX):
            for i in range(QTILES):
                units.append(dict(kind="fox", h=h, i=i, off=64 * (h % 2), tile=3 + h // 2, head=h, vcol=640 + 64 * h,
                                  subs=[(5 + h // 2, 0, 128 * (i + 1), 0)]))
        for hh in range(2):
            for i in range(QTILES):
                lo = max(0, i - 1)
                subs, col = [], 0
                for g in range(3):
                    k0 = lo if g == 0 else 0
                    n = 128 * (i + 1 - k0)
                    subs.append((2 + g, 128 * k0, n, col))
                    col += n
                units.append(dict(kind="dil", h=hh, i=i, off=64 * hh, tile=2, head=NFOX + hh, subs=subs))
        nsub = ntg = 0
        for u in units:
            u["cols"] = sum(s[2] for s in u["subs"])
            u["sub0"] = nsub
            nsub += len(u["subs"])
            u["nblk"] = u["cols"] // P
            u["tg0"] = ntg
            ntg += -(-u["nblk"] // 4)
            u["tg1"], u["sub1"] = ntg, nsub
            u["blk"] = []
            for g, (tile, k0, n, _) in enumerate(u["subs"]):
                for b in range(n // P):
                    vc = u["vcol"] if u["kind"] == "fox" else 256 + 128 * g + 64 * u["h"]
                    u["blk"].append((k0 // P + b, vc))
        NU = len(units)

        def pT(par, n):
            return pTa[:, par, 128 * n:128 * n + 128] if n < 8 else pTb[:, par, 128 * (n - 8):128 * (n - 8) + 128]

        def evs(tg):
            return tg // 2 + 1, (tg + 1) // 2

        PV_STEPS = 6
        W_LOADS = [16 * len(range(s, 26, 3)) for s in range(3)]
        block = ctx.enter_context(nc.Block())

        KV_STORES = 4 * 4 + 1
        SAMPLE_STORES = 2 * 5 * NB

        @block.sync
        def _(sp):
            a = 0
            w = parts["strict_mul"][1]
            sp.dma_start(small[:, 0:w], I["const"][:, 0:w]).then_inc(sem("ld_const"), 16)
            a = w
            for n in SMALL[6:]:
                lo, hi = parts[n]
                sp.dma_start(cs[n], I["const"][:, lo:hi]).then_inc(sem("ld_const"), 16)
            sp.dma_start(c_raw[0:1, :], I["c_prompt"]).then_inc(sem("ld_c"), 16)
            sp.dma_start(c_raw[1:9, :], I["c_sample"]).then_inc(sem("ld_c"), 16)
            sp.dma_start(rows72[0:48, :], I["b_mod"].rearrange("l (m p) -> (l m) p", p=P)).then_inc(sem("ld_c"), 16)
            for n, v in enumerate((I["norm1"].rearrange("l (m p) -> (l m) p", p=P),
                                   I["norm2"].rearrange("l (m p) -> (l m) p", p=P),
                                   I["norm_f"].rearrange("(m p) -> m p", p=P))):
                sp.dma_start(rows72[48 + 8 * n:56 + 8 * n, :], v).then_inc(sem("ld_c"), 16)
            sp.dma_start(ptab[:, :], I["page_table"].rearrange("(o b) n -> o (b n)", o=1)).then_inc(sem("ld_pt"), 16)
            sp.dma_start(pidx[:, :], I["page_table"].rearrange("b (n o) -> (b n) o", o=1)).then_inc(sem("ld_pt"), 16)
            sp.dma_start(xin[:, 0:4, :], I["x_prompt"][0].rearrange("(i p) d -> p i d", p=P)).then_inc(sem("ld_x"), 16)
            sp.dma_start(xin[0:32, 4, :], I["x_sample"].rearrange("b t d -> (b t) d")).then_inc(sem("ld_x"), 16)

            lo, hi = parts["slot_pad"]
            sp.dma_start(slots_d.rearrange("(p c) n -> p (c n)", p=P), I["const"][:, lo:hi]
                         ).then_inc(sem("ld_const"), 16)

            def chunk(c, slot, src, turn=None):
                sp.dma_start(wring[:, slot, :].rearrange("p (k n) -> p k n", k=KD),
                             src.rearrange("(k p) n -> p k n", p=P)).then_inc(sem(f"ld_w{slot}"), 16)

            wm, wi, wo = I["w_mod"][0], I["w_in"][0], I["w_o"][0]
            for c in range(6):
                if c >= 3:
                    sp.wait_ge(sem("w_used"), c - 2)
                chunk(c, c % 3, wm[:, 512 * c:512 * c + 512])
            sp.dma_start(wf_sb[:, :, :], wi[:, 3072:3078].rearrange("(k p) n -> p k n", p=P)).then_inc(sem("ld_f"), 16)
            sp.dma_start(bf_sb[:, :], I["b_f"].rearrange("l (n o) -> (l n) o", o=1)).then_inc(sem("ld_f"), 16)
            for n in range(12):
                if n < 3:
                    sp.wait_ge(sem("w_used"), 4 + n)
                elif n % 2:
                    sp.wait_ge(sem("z_mm"), 4 * ((n - 3) // 2 + 1))
                else:
                    sp.wait_ge(sem("w_used"), 6 + (n - 3) // 2 + 1)
                c = n // 2
                chunk(6 + n, n % 3, wm[:, 3072 + 512 * c:3584 + 512 * c] if n % 2 else wi[:, 512 * c:512 * c + 512])
            k = 0
            for hh in range(2):
                for g in range(3):
                    lo, hi = parts[f"dil{g}{hh}"]
                    sp.dma_start(dil_tab[:, k:k + hi - lo], I["const"][:, lo:hi]).then_inc(sem("ld_dt"), 16)
                    k += hi - lo
            lo, hi = parts["pick_head"]
            sp.dma_start(pick_head, I["const"][:, lo:hi]).then_inc(sem("ld_dt"), 16)
            sp.wait_ge(sem("kt_ev"), 10)
            sp.wait_ge(sem("vt_ev"), 10)
            for kv, src in enumerate((ktok[4], vtok[:, 4, :])):
                r = O["kv_sample"][:, 0, :, kv].rearrange("b t h d -> b t (h d)")
                for b in range(NB):
                    rows = src[4 * b:4 * b + 4, :]
                    sp.dma_start(r[b, :, 0:256], rows[:, 0:256]).then_inc(sem("st_smp"), 16)
                    sp.dma_start(r[b, :, 256:640], rows[:, 640:1024]).then_inc(sem("st_smp"), 16)
                    for g in range(3):
                        W = DILATION[g] * 128
                        dst = O[f"dil{g + 1}_sample"][b, 0, W - NT:W, kv].rearrange("t h d -> t (h d)")
                        sp.dma_start(dst, rows[:, 256 + 128 * g:384 + 128 * g]).then_inc(sem("st_smp"), 16)
            for g in range(3):
                W = DILATION[g] * 128
                n = (W - NT) * 256
                for b in range(NB):
                    src = I[f"cache_dil{g + 1}"][b, 0].rearrange("w a h d -> (w a h d)")[1024:1024 + n]
                    dst = O[f"dil{g + 1}_sample"][b, 0].rearrange("w a h d -> (w a h d)")[0:n]
                    sp.dma_start(dst.rearrange("(s n) -> s n", s=16),
                                 src.rearrange("(s n) -> s n", s=16)).then_inc(sem("shift"), 16)
            sp.wait_ge(sem("pv_mm"), NU)
            sp.wait_ge(sem("o_ev"), 8)
            sp.wait_ge(sem("w_used"), 12)
            sp.wait_ge(*done_at("new_ready"))
            sp.wait_ge(sem("ld_pt"), 32)
            for stored in ("st_k", "st_v"):
                sp.wait_ge(sem(stored), 16 * KV_STORES)
            sp.wait_ge(sem("st_smp"), 16 * SAMPLE_STORES)
            sp.wait_ge(sem("st_vs"), 16)
            sp.wait_ge(sem("st_lf"), 32)
            def sequence(i, b0):
                par = b0 % 2
                b = i * 2 + b0
                db = dbuf[:, par, :]

                ids = {}

                def page(p, kv, dst, done, wait=()):
                    if p not in ids or wait:
                        ids[p] = sp.value_load(ptab[0:1, bass.ds(b * PAGES + p, 1)], min_val=0, max_val=159)
                    pg = I["cache_kv"][bass.ds(ids[p], 1), 0]
                    for w in wait:
                        sp.wait_ge(*w)
                    sp.dma_start(dst, pg[:, :, kv].rearrange("o k h d -> k (o h d)")).then_inc(sem(done), 16)

                def values(p):
                    free = ((sem("v_used"), i * 2 * PV_STEPS + (PV_STEPS * (b0 - 2) + min(p // 2, PV_STEPS - 1) + 1)),) \
                        if b0 >= 2 and p % 2 == 0 else ()
                    page(p, 1, vpast[par][:, p, :], f"ld_v{par}", free)

                def windows():
                    sp.dma_start(db[:, 0:256], I["cache_dil1"][bass.ds(b, 1), 0].rearrange(
                        "b w a h d -> w (b a h d)")).then_inc(sem(f"ld_db{par}"), 16)
                    sp.dma_start(db[:, 256:1280], I["cache_dil2"][bass.ds(b, 1), 0].rearrange(
                        "b (i r) a h d -> i (b r a h d)", r=4)).then_inc(sem(f"ld_db{par}"), 16)
                    sp.dma_start(db[:, 1280:2304], I["cache_dil3"][bass.ds(b, 1), 0].rearrange(
                        "b (i r) a h d -> i (b r) (a h d)", r=16)[:, 0:4, :].rearrange("i r n -> i r n")
                        ).then_inc(sem(f"ld_db{par}"), 16)

                early = 12 if b0 else 0
                for p in range(PAGES):
                    free = ((sem("kT_mm"), i * 36 + 18 * b0 + (p - 3 if p >= 4 else p - 5)),) if p >= 4 or b0 else ()
                    if p == 8 and b0 >= 2:
                        free += ((sem("v_used"), i * 2 * PV_STEPS + PV_STEPS * (b0 - 1)),)
                    page(p, 0, kring[:, p % 4, :], f"ld_k{p % 4}", free)
                    if p == 3:
                        for v in range(early):
                            values(v)
                    if p == 8:
                        windows()
                    if p >= early:
                        values(p)

            sequence(0, 0)
            sequence(0, 1)
            with sp.Fori(0, NB // 2 - 1) as i:
                sequence(i, 2)
                sequence(i, 3)
            sp.wait_ge(sem("kT_mm"), 18 * NB)
            sp.wait_ge(sem("seq_pv"), NB - 1)
            for k in range(6):
                src = (I["w_br_sb"][0], I["w_br_sb"][0], I["w_br_dil"][0], I["w_br_fox"][0], I["w_br_fox"][0],
                       I["w_br_fox"][0])[k]
                r = (0, 128, 0, 0, 128, 256)[k]
                sp.dma_start(wbr[:, k, :], src[r:r + 128, :]).then_inc(sem("ld_br"), 16)
            c = 18
            for half in range(2):
                for b in range(3):
                    if c >= 21:
                        sp.wait_ge(sem("gate_mm"), 4 * (c - 20))
                    elif c == 18:
                        sp.wait_ge(sem("seq_pv"), NB)
                    elif c == 20:
                        sp.wait_ge(sem("seq_out"), NB)
                    chunk(c, c % 3, wi[:, 3078 + 1024 * b + 512 * half:3078 + 1024 * b + 512 * half + 512])
                    c += 1
            for half in range(2):
                sp.wait_ge(sem("gate_mm"), 4 * (c - 20))
                chunk(c, c % 3, wo[:, 512 * half:512 * half + 512])
                c += 1
            sp.dma_start(wr_sb[:, :, 0:4], I["w_rg"][0].rearrange("(k p) n -> p k n", p=P)).then_inc(sem("ld_r"), 16)
            sp.dma_start(wr_sb[:, :, 4:20], I["w_re"][0].rearrange("(k p) n -> p k n", p=P)).then_inc(sem("ld_r"), 16)
            sp.dma_start(br_sb[:, 0:4], I["b_rg"].to_broadcast([P, 4])).then_inc(sem("ld_r"), 16)
            sp.dma_start(br_sb[:, 4:20], I["b_re"].to_broadcast([P, 16])).then_inc(sem("ld_r"), 16)
            sp.wait_ge(sem("xo_mm"), 8)
            lo, hi = parts["moe_ids"]
            sp.dma_start(moe_ids, I["const"][:, lo:hi]).then_inc(sem("ld_mi"), 16)
            for i in range(5):
                n = P if i < 4 else 32
                sp.wait_ge(sem("row_ev"), 2 * i + 2)
                sp.dma_start(h_d[128 * i:128 * i + n, :], hrow[0:n, i % 2, :]).then_inc(sem(f"st_h{i % 2}"), 16)
            sp.wait_ge(*done_at("exp_id"))

            def expert_weights(i, c0, slot):
                e = sp.value_load(exp_id[0:1, bass.ds(i * RING + c0, 1)], min_val=0, max_val=NEXP - 1)
                if c0 >= RING:
                    sp.wait_ge(sem("h_mm"), i * RING + (c0 - 2))
                w = wring[:, slot, :].rearrange("p (k f) -> p k f", f=2 * DE)
                for n, name in enumerate(("w1", "w3")):
                    sp.dma_start(w[:, :, DE * n:DE * n + DE],
                                 I[name][0][bass.ds(e, 1)].rearrange("o (k p) f -> p (o k) f", p=P)
                                 ).then_inc(sem(f"ld_w{slot}"), 16)
                if c0 >= RING:
                    sp.wait_ge(sem("y_mm"), i * 2 * RING + 2 * (c0 - 2))
                sp.dma_start(wdown[:, slot, :].rearrange("p (k f) -> p k f", k=2),
                             I["w2"][0][bass.ds(e, 1)].rearrange("o (k p) f -> p (o k) f", p=P)
                             ).then_inc(sem(f"ld_e{slot}"), 16)

            expert_weights(0, 0, 0)
            sp.wait_ge(sem("ld_g0"), 16)
            for c in range(1, RING):
                expert_weights(0, c, c)
            with sp.Fori(0, CHUNKS // RING - 1) as i:
                for u in range(RING):
                    expert_weights(i, RING + u, u)
            for s in range(RING):
                sp.wait_ge(sem(f"st_yc{s}"), 16 * (CHUNKS // RING))
            for i in range(5):
                n = P if i < 4 else 32
                if i >= RING:
                    sp.wait_ge(sem("ysum"), i - RING + 1)
                sp.dma_start(yrow[0:n, i, :], y_d[256 * i:256 * i + 2 * n, :].rearrange("(t k) d -> t (k d)", k=2)
                             ).then_inc(sem(f"ld_y{i % RING}"), 16)
            sp.wait_ge(sem("shift"), 16 * 24)
            for stored in ("st_k", "st_v"):
                sp.wait_ge(sem(stored), 16 * KV_STORES)
            sp.wait_ge(sem("st_smp"), 16 * SAMPLE_STORES)
            sp.wait_ge(sem("st_lf"), 32)
            sp.wait_ge(sem("st_y0"), 16 * 3)
            sp.wait_ge(sem("st_y1"), 16 * 2)


        def kv_stores(i):
            out = []
            for kv in range(2):
                if i < 4:
                    rows = O["kv_prompt"][0, 0, 128 * i:128 * i + 128, kv]
                    out += [(kv, 0, 256, rows[:, 0:4]), (kv, 640, 384, rows[:, 4:10])]
                    for g in range(3):
                        if g == 0 and i < 3:
                            continue
                        lo = 0 if g == 0 else 128 * i
                        out.append((kv, 256 + 128 * g, 128, O[f"dil{g + 1}_prompt"][0, 0, lo:lo + 128, kv]))
            return out

        def group_out(eng, n, tg, copy, done):
            u = units[n]
            b0 = 4 * (tg - u["tg0"])
            k = min(4, u["nblk"] - b0)
            eng.wait_ge(sem("tg_mm"), tg + 1)
            if n >= 2:
                eng.wait_ge(sem("pv_mm"), n - 1)
            dst = pTa[:, n % 2, 128 * b0:128 * (b0 + k)] if b0 < 8 else pTb[:, n % 2, 0:128 * k]
            copy(dst, banks[2 + tg % 2][:, 0:128 * k]).then_inc(sem(done), 1)

        def keys_out(eng, i, b0, p, copy):
            eng.wait_ge(sem("kT_mm"), i * 36 + (18 * b0 + p + 1))
            eng.wait_ge(sem("qk_mm"), i * 10 + (5 * b0 + p // 4))
            src = banks[p % 2]
            if p < PAGES:
                c = 128 * (p % 4)
                copy(kT5[:, 0:4, c:c + 128], src.rearrange("p (j n) -> p j n", j=4)
                     ).then_inc(sem("kT_evA" if p % 2 else "kT_evD"), 1)
            else:
                copy(kT5[:, p - PAGES, :], src).then_inc(sem("kT_evA" if p % 2 else "kT_evD"), 1)

        @block.gpsimd
        def _(pool):
            pool.wait_ge(sem("ld_pt"), 32)
            pool.indirect_dma_start(
                out=lf_page.rearrange("p a b -> p (a b)"), out_offset=None,
                in_=I["cache_fox_logf"].rearrange("n l k h -> n (l k h)"),
                in_offset=bass.IndirectOffsetOnAxis(ap=pidx[:, 0:1], axis=0)).then_inc(sem("ld_lf"), 16)
            pool.wait_ge(*done_at("lf_rows"))
            pool.dma_start(O["logf_prompt"][0, 0].rearrange("(i p) h -> p i h", p=P),
                           lf_tok[:, 0:4, :]).then_inc(sem("st_lf"), 16)
            pool.dma_start(O["logf_sample"].rearrange("b l t h -> (b l t) h"), lf_tok[0:32, 4, :]
                           ).then_inc(sem("st_lf"), 16)
            pool.dma_start(nc_d, ncn[0:32, :]).then_inc(sem("st_nc"), 16)
            pool.wait_ge(sem("st_nc"), 16)
            pool.dma_start(lfnew[0:NT, :, :], nc_d.rearrange("(b t) h -> t b h", t=NT)).then_inc(sem("ld_nc"), 16)
            for i in range(5):
                pool.wait_ge(sem("kt_ev"), 2 * i + 2)
                pool.wait_ge(sem("vt_ev"), 2 * i + 2)
                src = (ktok[i], vtok[:, i, :])
                for kv, lo, n, dst in kv_stores(i):
                    pool.dma_start(dst.rearrange("t h d -> t (h d)"), src[kv][:, lo:lo + n]
                                   ).then_inc(sem("st_v" if kv else "st_k"), 16)
            pool.dma_start(vs_d, vtok[0:32, 4, :]).then_inc(sem("st_vs"), 16)
            for n, u in enumerate(units):
                pool.wait_ge(sem("rs_ready"), n + 1)
                s = sc_sb[:, n % 3, 0:u["cols"]]
                nc.gpsimd.tensor_scalar(s, s, rowst[:, 3, n % 3:n % 3 + 1], None, ALU.mult).then_inc(sem("nrm"), 1)
            pool.wait_ge(sem("st_vs"), 16)
            pool.wait_ge(sem("pv_mm"), NU)
            link = Chain(pool, sem("pool_own"))
            for pad in (s_sp[:, 256:272], s_w[:, :, 256:384]):
                nc.gpsimd.memset(pad, 0.0)
            link(nc.gpsimd.memset(s_y[:, 256:320], 0.0))
            with pool.Fori(0, NB // 2) as i:
                link.enter(i, 6)
                for par in range(2):
                    pool.wait_ge(sem("seq_pv"), i * 2 + par)
                    pool.dma_start(vncur[0:NT, :], vs_d[bass.ds(i * 2 * NT + par * NT, NT), :]).then_inc(sem("ld_vn"), 16)
                    pool.wait_ge(sem("sp_ready"), i * 2 + (par + 1))
                    sp_, w, y = s_sp, s_w[:, par, :], s_y
                    link(nc.gpsimd.tensor_tensor(w[:, 0:256], sp_[:, 0:256], sp_[:, 16:272], ALU.add))
                    link(nc.gpsimd.tensor_tensor(y[:, 0:256], w[:, 0:256], w[:, 32:288], ALU.add))
                    link(nc.gpsimd.tensor_tensor(w[:, 0:256], y[:, 0:256], y[:, 64:320], ALU.add))
                    nc.gpsimd.tensor_tensor(y[:, 0:256], w[:, 0:256], w[:, 128:384], ALU.add
                                            ).then_inc(sem("y_ready"), 1)
                link.leave(NB // 2)

            pool.wait_ge(*done_at("dest_ready"))
            pool.wait_ge(sem("ld_const"), 16 * 7)
            for n in range(10):
                r = P if n < 8 else 32
                pool.indirect_dma_start(
                    out=slots_d, out_offset=bass.IndirectOffsetOnAxis(ap=dest_i[0:r, n:n + 1], axis=0),
                    in_=pay[0:r, n, :], in_offset=None).then_inc(sem("st_slot"), 16)
            pool.wait_ge(sem("st_slot"), 160)
            pool.dma_start(slot_t[:, 0:CHUNKS, :], slots_d.rearrange("(c p) n -> p c n", p=P)).then_inc(sem("ld_slot"), 16)
            pool.wait_ge(sem("st_h0"), 48)
            pool.wait_ge(sem("st_h1"), 32)

            before = link.n

            def carry(i, n):
                pool.wait_ge(sem("pool_own"), i * 2 * RING + (before + n))
                nc.gpsimd.tensor_tensor(carried[0:1, :], ones[0:1, 0:1], ones[0:1, 0:1], ALU.mult
                                        ).then_inc(sem("pool_own"), 1)

            def gather(i, c0, slot):
                pool.wait_ge(sem("tok_ready"), i * RING + (c0 + 1))
                carry(i, c0 if c0 < RING else 2 * c0 - RING)
                pool.indirect_dma_start(
                    out=xrow[:, slot, :], out_offset=None, in_=h_d,
                    in_offset=bass.IndirectOffsetOnAxis(ap=tok_now[:, slot:slot + 1], axis=0)
                    ).then_inc(sem(f"ld_g{slot}"), 16)

            def scatter(i, c0, slot):
                pool.wait_ge(sem("yc_evA"), i * RING + (c0 + 1))
                pool.wait_ge(sem("yc_evD"), i * RING + (c0 + 1))
                carry(i, 2 * c0 + RING + 1 if c0 < CHUNKS - RING else c0 + CHUNKS)
                pool.indirect_dma_start(
                    out=y_d, out_offset=bass.IndirectOffsetOnAxis(ap=row_now[:, slot:slot + 1], axis=0),
                    in_=ychunk[:, slot, :], in_offset=None, bounds_check=TOP * TOK - 1, oob_is_err=False
                    ).then_inc(sem(f"st_yc{slot}"), 16)

            for c in range(RING):
                gather(0, c, c)
            with pool.Fori(0, CHUNKS // RING - 1) as i:
                for u in range(RING):
                    gather(i, RING + u, u)
                    scatter(i, u, u)
            for u in range(RING):
                scatter(0, CHUNKS - RING + u, u)

        @block.tensor
        def _(pe):
            def mm(out, lhsT, rhs, start=True, stop=True, **k):
                return T.matmul(out, lhsT, rhs, start=start, stop=stop, **k)

            def mm_tokens(bank, lhsT, rhs, start, stop, rows=P):
                for s in range(2):
                    last = mm(psum[0:rows, bank + s, 0:HALF], lhsT, rhs[:, HALF * s:HALF * s + HALF], start, stop)
                return last

            pe.wait_ge(sem("ld_const"), 16 * 7)
            pe.wait_ge(sem("ld_c"), 16 * 6)
            pe.wait_ge(*done_at("c_silu"))
            for k in range(KD):
                T.transpose(banks[7][:, 9 * k:9 * k + 9], c_tmp[0:9, 128 * k:128 * k + 128], ident[0:9, 0:9])
            T.transpose(banks[7][:, 128:200], rows72[0:72, :], ident[0:72, 0:72]).then_inc(sem("c_steps"), 1)
            pe.wait_ge(sem("ld_x"), 32)
            for k in range(KD):
                if k >= 4:
                    pe.wait_ge(sem("x_evD" if k % 2 else "x_evA"), (k - 4) // 2 + 1)
                for i in range(4):
                    last = T.transpose(banks[k % 4][:, 128 * i:128 * i + 128], xin[:, i, 128 * k:128 * k + 128], ident)
                last.then_inc(sem("x_t"), 1)
            for k in range(KD):
                last = T.transpose(banks[4][:, 32 * k:32 * k + 32], xin[0:32, 4, 128 * k:128 * k + 128],
                                   ident[0:32, 0:32])
            last.then_inc(sem("x_t"), 1)

            def mod_chunk(u, bank):
                for r in range(2):
                    for q in range(4):
                        k = 2 * q + r
                        last = mm(banks[bank][32 * q:32 * q + 32, :], cT[:, k, :],
                                  wring[:, u, 512 * k:512 * k + 512], r == 0, r == 1, skip_group_check=True)
                last.then_inc(sem("w_used"), 1)

            def mod_turn(u, bank):
                for j in range(4):
                    last = T.transpose(banks[bank][:, 128 * j:128 * j + 128], mod_rows[:, u, 128 * j:128 * j + 128], ident)
                last.then_inc(sem("mod_t"), 1)

            pe.wait_ge(*done_at("cT_ready"))
            pe.wait_ge(sem("x_evA"), 4)
            pe.wait_ge(sem("x_evD"), 4)
            for c in range(6):
                if c >= 3:
                    pe.wait_ge(sem("mod_ev"), c - 2)
                pe.wait_ge(sem(f"ld_w{c % 3}"), 16 * (c // 3 + 1))
                mod_chunk(c % 3, c % 3)
                if c:
                    pe.wait_ge(sem("mod_rows"), c)
                    mod_turn((c - 1) % 3, (c - 1) % 3)
            pe.wait_ge(sem("mod_rows"), 6)
            mod_turn(2, 2)

            def norm_sums(n):
                for k in range(KD):
                    pe.wait_ge(sem("sq"), KD * n + k + 1)
                    last = mm_tokens(5, ones, hT[:, k, :], k == 0, k == KD - 1)
                last.then_inc(sem("ss"), 1)

            norm_sums(0)

            pe.wait_ge(sem("h_ready"), 2)
            pe.wait_ge(sem("mod_ev"), 6)
            def turn_modulation(i, u):
                pe.wait_ge(sem("mod_rows"), i * 3 + (7 + u))
                mod_turn(u, 4 + u)

            with pe.Fori(0, 2) as i:
                for v in range(6):
                    slot, u = v % 3, v // 2
                    pe.wait_ge(sem(f"ld_w{slot}"), i * 32 + (48 + 16 * (v // 3)))
                    if v % 2:
                        pe.wait_ge(sem("mod_ev"), i * 3 + (4 + u))
                        mod_chunk(slot, 4 + u)
                        continue
                    for j in range(4):
                        n = 4 * u + j
                        pe.wait_ge(sem("z_ev"), i * 12 + max(0, n - 1))
                        for k in range(KD):
                            w = wring[:, slot, 512 * k + 128 * j:512 * k + 128 * j + 128]
                            last = mm_tokens(2 * (n % 2), w, hT[:, k, :], k == 0, k == KD - 1)
                        last.then_inc(sem("z_mm"), 1)
                    if u:
                        turn_modulation(i, u - 1)
                turn_modulation(i, 2)

            pe.wait_ge(sem("ld_f"), 32)
            pe.wait_ge(sem("mod_ev"), 12)
            for k in range(KD):
                last = mm_tokens(4, wf_sb[:, k, :], hT[:, k, :], k == 0, k == KD - 1, NFOX)
            last.then_inc(sem("f_steps"), 1)
            pe.wait_ge(*done_at("lf_tot"))
            mm(banks[7][:, 0:NFOX], later_page, lf_tot[:, 0, :]).then_inc(sem("past_steps"), 1)

            pe.wait_ge(sem("z_ev"), 24)
            pe.wait_ge(*done_at("lf_after"))
            pe.wait_ge(sem("mod_ev"), 12)
            for h in range(NFOX):
                dst = banks[0][:, 128 * h:128 * h + 128] if h < 4 else banks[1][:, 128 * (h - 4):128 * (h - 3)]
                last = T.transpose(dst, lf_scan[:, h, :], ident)
            last.then_inc(sem("past_steps"), 1)
            pe.wait_ge(*done_at("lf_rowT"))
            for i in range(4):
                T.transpose(banks[6][:, 6 * i:6 * i + 6], logfT[0:6, 128 * i:128 * i + 128], ident[0:6, 0:6])
            T.transpose(banks[6][0:32, 24:30], logfT[0:6, SEQ:TOK], ident[0:6, 0:6])
            T.transpose(banks[6][0:32, 32:38], ncumT[0:6, SEQ:TOK], ident[0:6, 0:6]).then_inc(sem("forget_rows"), 1)

            pe.wait_ge(*done_at("lf_past"))
            for i in range(5):
                n = P if i < 4 else 32
                for g in range(4):
                    if i:
                        pe.wait_ge(sem("kt_ev" if g < 2 else "vt_ev"), 2 * (i - 1) + g % 2 + 1)
                    for j in range(4):
                        last = T.transpose(banks[g][0:n, 128 * j:128 * j + 128],
                                           zT[:, 8 + 4 * g + j, 128 * i:128 * i + n], ident)
                    last.then_inc(sem("kv_t"), 1)

            pe.wait_ge(sem("kt_ev"), 10)
            pe.wait_ge(sem("vt_ev"), 10)
            pe.wait_ge(*done_at("lf_rows"))

            def sb_scores(h):
                for kt in range(4):
                    if h:
                        pe.wait_ge(sem("sbz_read"), 4 * (h - 1) + kt + 1)
                    o = 64 * (h % 2)
                    mm(banks[kt][:, 128 * kt:SEQ], zT[o:o + 64, 8 + h // 2, 128 * kt:128 * kt + 128],
                       zT[o:o + 64, h // 2, 128 * kt:SEQ]).then_inc(sem("sbz_mm"), 1)

            sb_scores(0)
            for h in range(4):
                if h < 3:
                    sb_scores(h + 1)
                pe.wait_ge(sem("sbsp"), h + 1)
                for n, kt in enumerate((3, 2, 1, 0)):
                    if 4 * h + n >= 2:
                        pe.wait_ge(sem("sba_read"), 4 * h + n - 1)
                    bk = banks[4 + n % 2]
                    last = mm(bk[:, 128 * kt:SEQ], later_key, sb_sp[h % 2][:, kt, 128 * kt:SEQ], True, kt == 3)
                    for k2 in range(kt + 1, 4):
                        last = mm(bk[:, 128 * k2:SEQ], ones, sb_sp[h % 2][:, k2, 128 * k2:SEQ], False, k2 == 3)
                    last.then_inc(sem("sba_mm"), 1)
                pe.wait_ge(sem("sbw"), h + 1)
                if h >= 2:
                    pe.wait_ge(sem("sbo_ev"), h - 1)
                o = 64 * (h % 2)
                for kt in range(4):
                    last = mm(banks[6 + h % 2][o:o + 64, 128 * kt:SEQ], vtok[:, kt, 64 * h:64 * h + 64],
                              sb_zm[h % 2][:, kt, 128 * kt:SEQ], kt == 0, kt == 3)
                last.then_inc(sem("sbo_mm"), 1)

            pe.wait_ge(sem("sbo_ev"), 4)
            pe.wait_ge(sem("sba_read"), 16)
            pe.wait_ge(sem("sbz_read"), 16)
            pe.wait_ge(sem("ld_dt"), 16 * 7)

            def fox_rows(h):
                if h >= 2:
                    pe.wait_ge(sem("nck_ev"), h - 1)
                mm(banks[6 + h % 2], pick_head[0:NFOX, 128 * h:128 * h + 128], ncumT[0:NFOX, 0:SEQ]
                   ).then_inc(sem("nck_mm"), 1)

            def scores(n):
                u = units[n]
                o, i = u["off"], u["i"]
                for s, (tile, k0, cols, _) in enumerate(u["subs"]):
                    c = u["sub0"] + s
                    if c >= 2:
                        pe.wait_ge(sem("sc_ev"), c - 1)
                    mm(banks[c % 2][:, 0:cols], zT[o:o + 64, tile, 128 * i:128 * i + 128],
                       zT[o:o + 64, 8 + tile, k0:k0 + cols]).then_inc(sem("sc_mm"), 1)

            def turn_weights(n):
                u = units[n]
                pe.wait_ge(sem("nrm"), n + 1)
                for tg in range(u["tg0"], u["tg1"]):
                    if tg >= 2:
                        d, a = evs(tg - 2)
                        pe.wait_ge(sem("tg_evA" if tg % 2 else "tg_evD"), a if tg % 2 else d)
                    b0 = 4 * (tg - u["tg0"])
                    for b in range(b0, min(b0 + 4, u["nblk"])):
                        last = T.transpose(banks[2 + tg % 2][:, 128 * (b - b0):128 * (b - b0) + 128],
                                           sc_sb[:, n % 3, 128 * b:128 * b + 128], ident)
                    last.then_inc(sem("tg_mm"), 1)

            def weigh(n):
                u = units[n]
                d, a = evs(u["tg1"] - 1)
                pe.wait_ge(sem("tg_evD"), d)
                if a:
                    pe.wait_ge(sem("tg_evA"), a)
                if u["i"] == 0 and u["head"] >= 2:
                    pe.wait_ge(sem("o_ev"), u["head"] - 1)
                o, i = u["off"], u["i"]
                for b, (kt, vc) in enumerate(u["blk"]):
                    last = mm(banks[4 + u["head"] % 2][o:o + 64, 128 * i:128 * i + 128], vtok[:, kt, vc:vc + 64],
                              pT(n % 2, b), b == 0, b == u["nblk"] - 1)
                last.then_inc(sem("pv_mm"), 1)

            fox_rows(0)
            scores(0)
            scores(1)
            for n in range(NU):
                if n % 4 == 0 and n // 4 + 1 < NFOX:
                    fox_rows(n // 4 + 1)
                if n + 2 < NU:
                    scores(n + 2)
                turn_weights(n)
                if n:
                    weigh(n - 1)
            weigh(NU - 1)

            pe.wait_ge(sem("qbd_ready"), 1)
            pe.wait_ge(sem("sc_ev"), nsub)
            for b in range(NB):
                for j in range(8):
                    tile = PAIR_TILES[j] if j < 5 else j - 3
                    last = mm(banks[0][0:NT, 64 * b + 8 * j:64 * b + 8 * j + 8],
                              zT[:, 8 + tile, SEQ + NT * b:SEQ + NT * b + NT], qbd[:, b, 8 * j:8 * j + 8])
            last.then_inc(sem("own_keys"), 1)
            pe.wait_ge(*done_at("spn_ready"))
            mm(banks[1][0:NT, 0:128], later_key[0:NT, 0:NT], spnew[:, :, :].rearrange("p b n -> p (b n)")
               ).then_inc(sem("own_keys"), 1)

            pe.wait_ge(*done_at("new_ready"))
            pe.wait_ge(sem("o_ev"), 8)
            pe.wait_ge(sem("nck_ev"), NFOX)

            def turn_keys(i, b0, p):
                pe.wait_ge(sem("kT_evA" if p % 2 else "kT_evD"), i * 18 + (9 * b0 + p // 2))
                if p % 4 == 0 and p < PAGES or p == PAGES + 1:
                    pe.wait_ge(sem("kT5_ev"), i * 10 + (5 * b0 + p // 4))
                par = b0 % 2
                if p < PAGES:
                    pe.wait_ge(sem(f"ld_k{p % 4}"), i * 128 + 16 * (4 * b0 + p // 4 + 1))
                    srcs = [kring[:, p % 4, 128 * j:128 * j + 128] for j in range(5)]
                    dsts = [banks[p % 2][:, 128 * j:128 * j + 128] for j in range(4)]
                    dsts.append(banks[2][:, 128 * (p % 4):128 * (p % 4) + 128])
                else:
                    if p == PAGES:
                        pe.wait_ge(sem(f"ld_db{par}"), i * 48 + 48 * (b0 // 2 + 1))
                    lo = 4 * (p - PAGES)
                    starts = [0] + [256 + 256 * t for t in range(2 * NT)]
                    srcs = [dbuf[:, par, a:a + 128] for a in starts[lo:lo + 4 + p - PAGES]]
                    dsts = [banks[p % 2][:, 128 * j:128 * j + 128] for j in range(4)] + [banks[2][:, 0:128]]
                for a, d in zip(srcs, dsts):
                    last = T.transpose(d, a, ident)
                last.then_inc(sem("kT_mm"), 1)

            def score_keys(i, b0, q):
                par = b0 % 2
                n = 2 * q + 2 if q < 4 else 9
                pe.wait_ge(sem("kT_evA"), i * 18 + (9 * b0 + n))
                pe.wait_ge(sem("kT_evD"), i * 18 + (9 * b0 + n))
                pe.wait_ge(sem("kT5_ev"), i * 10 + (5 * b0 + q + 1))
                pe.wait_ge(sem("row_a"), i * 10 + (5 * b0 + q))
                if q == 0:
                    pe.wait_ge(sem("qcur"), i * 2 + (b0 + 1))
                    pe.wait_ge(sem("row_b"), i * 2 + b0)
                if q < 4:
                    jobs = [(j, kT5[:, j, :]) for j in range(4)]
                    mm(banks[4][32 * q:32 * q + 32, :], qcur[:, par, 4, :], kT5[:, 4, :], skip_group_check=True)
                else:
                    flat = kT5.rearrange("p j n -> p (j n)")
                    jobs = [(j, flat[:, a:a + 512]) for j, a in ((5, 0), (6, 128), (7, 640), (5, 0))]
                for n, (j, keys) in enumerate(jobs):
                    last = mm(banks[3][32 * n:32 * n + 32, :], qcur[:, par, j, :], keys, skip_group_check=True)
                last.then_inc(sem("qk_mm"), 1)

            def turn_scores(i, b0, n):
                if n == 4:
                    pe.wait_ge(sem("row_b"), i * 2 + (b0 + 1))
                else:
                    pe.wait_ge(sem("row_a"), i * 10 + (5 * b0 + min(n, 4) + 1))
                pe.wait_ge(sem("s_read"), i * 12 + (6 * b0 + n))
                if n == 0 and b0:
                    pe.wait_ge(sem("seq_out"), i * 2 + (b0 - 1))
                src = row_b if n == 4 else row_a
                for b in range(4):
                    last = T.transpose(banks[5][:, 128 * b:128 * b + 128], src[:, 128 * b:128 * b + 128], ident)
                last.then_inc(sem("sT_mm"), 1)

            def column_max(i, b0):
                pe.wait_ge(sem("m_ready"), i * 2 + (b0 + 1))
                T.transpose(banks[6][0:32, 0:128], s_m[:, b0 % 2, :], ident).then_inc(sem("m_t"), 1)

            def column_max_back(i, b0):
                pe.wait_ge(sem("dg_ready"), i * 2 + (b0 + 1))
                mm(banks[6][:, 128:160], ones[0:32, :], s_dg[0:32, b0 % 2, :]).then_inc(sem("m_b"), 1)

            def sticks(i, b0):
                pe.wait_ge(sem("y_ready"), i * 2 + (b0 + 1))
                pe.wait_ge(sem("f_sub"), i * 2 + (b0 + 1))
                a = banks[6][:, 192:448]
                mm(a, later_key, s_sp[:, 0:256], True, False)
                mm(a, ones, s_y[:, 16:272], False, False)
                mm(a.rearrange("p (a b) -> p a b", b=16), ones[0:NT, :],
                   s_sn[0:NT, b0 % 2, :].unsqueeze(1).to_broadcast([NT, PAGES, 16]), False, True).then_inc(sem("a_mm"), 1)

            def sums(i, b0):
                pe.wait_ge(sem("r_ready"), i * 2 + (b0 + 1))
                mm(banks[6][:, 160:192], ones, s_r[:, b0 % 2, :], True, False)
                mm(banks[6][:, 160:192], ones[0:NT, :], s_rn[0:NT, b0 % 2, :], False, True).then_inc(sem("l_mm"), 1)

            def add_value(q, col, w, v, start=False):
                return mm(banks[7][32 * q:32 * q + 8, 128 * col:128 * col + 128], w, v, start, False,
                          skip_group_check=True)

            def weigh_values(i, b0, lo, hi):
                par = b0 % 2
                if lo == 0:
                    pe.wait_ge(sem("w_ready"), i * 2 + (b0 + 1))
                    pe.wait_ge(sem("r_ready"), i * 2 + (b0 + 1))
                    pe.wait_ge(sem(f"ld_v{par}"), i * 256 + 256 * (b0 // 2 + 1))
                    pe.wait_ge(sem("o_rows"), i * 2 + b0)
                for p in range(lo, hi):
                    for j in range(5):
                        w = s_w[:, par, 16 * p + 8 * j:16 * p + 8 * j + 8] if j < 2 else \
                            s_f[:, par, 24 * p + 8 * (j - 2):24 * p + 8 * (j - 2) + 8]
                        v = vpast[par][:, p, 128 * j:128 * j + 128]
                        if j < 4:
                            add_value(j, 0, w, v, p == 0)
                        else:
                            last = add_value(p % 4, 1, w, v)
                if hi < PAGES:
                    last.then_inc(sem("v_used"), 1)
                    return
                pe.wait_ge(sem("ld_vn"), i * 32 + 16 * (b0 + 1))
                add_value(0, 2, s_dl[:, par, 0:8], dbuf[:, par, 128:256])
                for g in range(2):
                    for t in range(NT):
                        a = 1024 * g + 256 + 256 * t + 128
                        last = add_value(t, 2, s_dx[:, 2 * par + g, 8 * t:8 * t + 8], dbuf[:, par, a:a + 128])
                last.then_inc(sem("v_used"), 1)
                for j in range(8):
                    tile = PAIR_TILES[j] if j < 5 else j - 3
                    q, col = (j, 0) if j < 4 else (0, 1) if j == 4 else (j - 4, 2)
                    last = add_value(q, col, s_wn[0:NT, par, 8 * j:8 * j + 8], vncur[0:NT, 128 * tile:128 * tile + 128])
                last.then_inc(sem("seq_pv"), 1)

            def turn_outputs(i, b0, read):
                pe.wait_ge(sem("o_rows"), i * 2 + (b0 + 1))
                pe.wait_ge(sem("s_read"), i * 12 + 6 * read)
                T.transpose(banks[5][:, 0:128], s_o[:, 0:128], ident)
                for n in range(2):
                    last = mm(banks[5][:, 128 + 8 * n:136 + 8 * n], s_o[:, 128 + 128 * n:256 + 128 * n], cs["fold4"])
                last.then_inc(sem("oT_mm"), 1)

            def read_keys(i, b0, before):
                between = {3: (column_max,), 6: (column_max_back,), 9: (sticks,), 13: (sums,)} if before else {}
                for p in range(18):
                    turn_keys(i, b0, p)
                    if p >= 5 and p % 4 == 1:
                        score_keys(i, b0, (p - 5) // 4)
                    if p in (7, 11, 15):
                        turn_scores(i, b0, (p - 7) // 4)
                    for stage in between.get(p, ()):
                        stage(i, b0 - 1)
                    if before and p >= 13:
                        weigh_values(i, b0 - 1, 2 * (p - 13), 2 * (p - 12))
                turn_scores(i, b0, 3)
                score_keys(i, b0, 4)
                if before:
                    weigh_values(i, b0 - 1, 10, PAGES)
                turn_scores(i, b0, 4)
                turn_scores(i, b0, 5)
                if before:
                    turn_outputs(i, b0 - 1, b0 + 1)

            pe.wait_ge(sem("o_zero"), 1)
            read_keys(0, 0, False)
            with pe.Fori(0, NB // 2 - 1) as i:
                read_keys(i, 1, True)
                read_keys(i, 2, True)
            read_keys(0, NB - 1, True)
            for stage in (column_max, column_max_back, sticks, sums):
                stage(0, NB - 1)
            weigh_values(0, NB - 1, 0, PAGES)
            turn_outputs(0, NB - 1, NB)

            pe.wait_ge(sem("seq_out"), NB)
            pe.wait_ge(sem("s_read"), 6 * NB)
            pe.wait_ge(sem("ld_br"), 16 * 6)
            n, c = 0, 18
            for half in range(2):
                for b in range(3):
                    pe.wait_ge(sem(f"ld_w{c % 3}"), 16 * (c // 3 + 1))
                    for j in range(4):
                        m = 4 * half + j
                        if n >= 2:
                            pe.wait_ge(sem("gate_ev"), n - 1)
                            pe.wait_ge(sem("br_ev"), n - 1)
                        kts = ((0, 1), (2,), (3, 4, 5))[b]
                        for k in kts:
                            w = wbr[:, k, 128 * m:128 * m + 128]
                            mm_tokens(4 + 2 * (n % 2), w, oT[:, k, :], k == kts[0], k == kts[-1])
                        for k in range(KD):
                            w = wring[:, c % 3, 512 * k + 128 * j:512 * k + 128 * j + 128]
                            last = mm_tokens(2 * (n % 2), w, hT[:, k, :], k == 0, k == KD - 1)
                        last.then_inc(sem("gate_mm"), 1)
                        n += 1
                    c += 1

            for half in range(2):
                pe.wait_ge(sem(f"ld_w{c % 3}"), 16 * (c // 3 + 1))
                pe.wait_ge(sem("br_ev"), 24)
                for j in range(4):
                    m = 4 * half + j
                    if m >= 2:
                        pe.wait_ge(sem("xo_ev"), m - 1)
                    for k in range(KD):
                        w = wring[:, c % 3, 512 * k + 128 * j:512 * k + 128 * j + 128]
                        last = mm_tokens(2 * (m % 2), w, merged[:, k, :], k == 0, k == KD - 1)
                    last.then_inc(sem("xo_mm"), 1)
                c += 1
            norm_sums(1)

            pe.wait_ge(sem("h_ready"), 4)
            pe.wait_ge(sem("xo_ev"), 8)
            pe.wait_ge(sem("ld_r"), 64)
            for r in range(2):
                for q in range(4):
                    k = 2 * q + r
                    for half in range(2):
                        last = mm(psum[32 * q:32 * q + 32, half, 0:HALF], wr_sb[:, k, :],
                                  hT[:, k, HALF * half:HALF * half + HALF], r == 0, r == 1, skip_group_check=True)
            last.then_inc(sem("routing"), 1)
            pe.wait_ge(*done_at("lg_rows"))
            for i in range(5):
                n = P if i < 4 else 32
                dst = banks[2][:, 128 * i:128 * i + 128] if i < 4 else banks[5][0:32, 0:128]
                last = T.transpose(dst, lg_rows[:, 128 * i:128 * i + n], ident)
            last.then_inc(sem("routing"), 1)
            for i in range(5):
                n = P if i < 4 else 32
                for g in range(2):
                    if i:
                        pe.wait_ge(sem("row_ev"), 2 * i + g - 1)
                    for j in range(4):
                        last = T.transpose(banks[3 + g][0:n, 128 * j:128 * j + 128],
                                           hT[:, 4 * g + j, 128 * i:128 * i + n], ident)
                    last.then_inc(sem("row_t"), 1)
            pe.wait_ge(*done_at("comb_ready"))
            rb = r_b.rearrange("p i e -> p (i e)")
            mm(banks[1][:, 0:80], cs["strict_mul"], rb)
            last = mm(banks[1][:, 80:160], ones, rb)
            last.then_inc(sem("routing"), 1)

            pe.wait_ge(sem("row_ev"), 10)

            def turn_rows(i, c0, slot):
                pe.wait_ge(sem(f"ld_g{slot}"), i * 16 + 16 * (c0 // RING + 1))
                if c0:
                    pe.wait_ge(sem("xg_evA"), i * RING + c0)
                    pe.wait_ge(sem("xg_evD"), i * RING + c0)
                for k in range(KD):
                    last = T.transpose(banks[k // 4][:, 128 * (k % 4):128 * (k % 4) + 128],
                                       xrow[:, slot, 128 * k:128 * k + 128], ident)
                last.then_inc(sem("xg_t"), 1)

            def hidden(i, c0, slot):
                pe.wait_ge(sem("xg_evA"), i * RING + (c0 + 1))
                pe.wait_ge(sem("xg_evD"), i * RING + (c0 + 1))
                pe.wait_ge(sem(f"ld_w{slot}"), i * 32 + (W_LOADS[slot] + 32 * (c0 // RING + 1)))
                for k in range(KD):
                    last = mm(banks[2 + slot], xg[:, slot, 128 * k:128 * k + 128],
                              wring[:, slot, 512 * k:512 * k + 512], k == 0, k == KD - 1)
                last.then_inc(sem("h_mm"), 1)

            def turn_hidden(i, c0, slot):
                pe.wait_ge(sem("hid_ready"), i * RING + (c0 + 1))
                if c0:
                    pe.wait_ge(sem("hidT_ev"), i * RING + c0)
                for k in range(2):
                    last = T.transpose(banks[5][:, 128 * k:128 * k + 128], hidr[:, slot, 128 * k:128 * k + 128], ident)
                last.then_inc(sem("hid_t"), 1)

            def outputs(i, c0, slot, before=True):
                pe.wait_ge(sem("hidT_ev"), i * RING + (c0 + 1))
                pe.wait_ge(sem(f"ld_e{slot}"), i * 16 + 16 * (c0 // RING + 1))
                for half in range(2):
                    if before:
                        pe.wait_ge(sem("yc_evD" if half else "yc_evA"), i * RING + c0)
                    for k in range(2):
                        last = mm(banks[6 + half], hidT[:, slot, 128 * k:128 * k + 128],
                                  wdown[:, slot, 1024 * k + 512 * half:1024 * k + 512 * half + 512], k == 0, k == 1)
                    last.then_inc(sem("y_mm"), 1)

            turn_rows(0, 0, 0)
            hidden(0, 0, 0)
            turn_rows(0, 1, 1)
            turn_hidden(0, 0, 0)
            with pe.Fori(0, CHUNKS // RING - 1) as i:
                for c0 in range(1, 1 + RING):
                    hidden(i, c0, c0 % RING)
                    outputs(i, c0 - 1, (c0 - 1) % RING, True)
                    turn_rows(i, c0 + 1, (c0 + 1) % RING)
                    turn_hidden(i, c0, c0 % RING)
            for c in (CHUNKS - 2, CHUNKS - 1):
                hidden(0, c, c % RING)
                outputs(0, c - 1, (c - 1) % RING)
                if c < CHUNKS - 1:
                    turn_rows(0, c + 1, (c + 1) % RING)
                turn_hidden(0, c, c % RING)
            outputs(0, CHUNKS - 1, (CHUNKS - 1) % RING)

            pe.wait_ge(sem("yc_evA"), CHUNKS)
            for m in range(KD):
                if m >= 2:
                    pe.wait_ge(sem("x2_ev"), m - 1)
                for i in range(5):
                    if m == 0:
                        pe.wait_ge(sem("ysum"), i + 1)
                    n = P if i < 4 else 32
                    bk = banks[2 * (m % 2)][:, 128 * i:128 * i + 128] if i < 4 else banks[2 * (m % 2) + 1][:, 0:32]
                    last = T.transpose(bk, yrow[0:n, i, 128 * m:128 * m + 128], ident[0:n, 0:n])
                last.then_inc(sem("yt_t"), 1)
            norm_sums(2)
            pe.wait_ge(sem("h_ready"), 5)
            for i in range(5):
                n = P if i < 4 else 32
                for g in range(2):
                    if i:
                        pe.wait_ge(sem("yo_evA" if g else "yo_evD"), i)
                    for j in range(4):
                        last = T.transpose(banks[g][0:n, 128 * j:128 * j + 128],
                                           hT[:, 4 * g + j, 128 * i:128 * i + n], ident)
                    last.then_inc(sem("yo_t"), 1)

        @block.scalar
        def _(act):
            link = Chain(act, sem("act_own"))

            def f(out, in_, fn, **k):
                return A.activation(out, in_, fn, **k)

            act.wait_ge(sem("ld_c"), 16 * 6)
            f(c_tmp[0:9, :], c_raw[0:9, :], ACT.Exp, scale=-1.0).then_inc(sem("c_steps"), 1)
            for k in range(0, KD, 2):
                act.wait_ge(sem("x_t"), k + 1)
                A.copy(xT[:, k, 0:SEQ], banks[k % 4]).then_inc(sem("x_evA"), 1)

            def squares(updated=None):
                for k in range(KD):
                    if updated:
                        act.wait_ge(updated, k + 1)
                    f(hT[:, k, :], xT[:, k, :], ACT.Square).then_inc(sem("sq"), 1)

            def gain_and_shift(n, shift):
                for k in range(KD):
                    act.wait_ge(sem("x_normed"), KD * n + k + 1)
                    last = f(hT[:, k, 0:SEQ], hT[:, k, 0:SEQ], ACT.Identity, scale=gainA[:, k, 0:1],
                             bias=modT[:, shift + k, 0:1])
                last.then_inc(sem("h_ready"), 1)

            def norm_root(n):
                act.wait_ge(sem("ss"), n + 1)
                link(f(as_halves(rstd[:, :]), halves(5), ACT.Ln, scale=1.0 / D, bias=eps_sb[:, 0:1]))
                f(rstd[:, :], rstd[:, :], ACT.Exp, scale=-0.5).then_inc(sem("rs"), 1)

            act.wait_ge(sem("x_evD"), 4)
            act.wait_ge(sem("x_evD"), 5)
            act.wait_ge(sem("x_evA"), 4)
            squares()
            for c in range(6):
                act.wait_ge(sem("w_used"), c + 1)
                if c >= 3:
                    act.wait_ge(sem("mod_t"), c - 2)
                A.copy(mod_rows[:, c % 3, :], banks[c % 3]).then_inc(sem("mod_rows"), 1)
            norm_root(0)
            gain_and_shift(0, 0)

            with act.Fori(0, 2) as i:
                for n in range(12):
                    act.wait_ge(sem("z_mm"), i * 12 + (n + 1))
                    A.copy(zT[:, bass.ds(i * 12 + n, 1), :].rearrange("p o (a b) -> p (o a) b", a=2),
                           halves(2 * (n % 2))).then_inc(sem("z_ev"), 1)
                    if n % 4 == 3:
                        u = n // 4
                        act.wait_ge(sem("w_used"), i * 3 + (7 + u))
                        act.wait_ge(sem("mod_t"), i * 3 + (4 + u))
                        A.copy(mod_rows[:, u, :], banks[4 + u]).then_inc(sem("mod_rows"), 1)

            act.wait_ge(*done_at("f_abs"))
            link(f(fscr[0:NFOX, 2, :], fscr[0:NFOX, 1, :], ACT.Exp))
            f(fscr[0:NFOX, 3, :], fscr[0:NFOX, 2, :], ACT.Ln, bias=1.0).then_inc(sem("f_steps"), 1)

            for i in range(5):
                n = P if i < 4 else 32
                for g in range(2):
                    act.wait_ge(sem("kv_t"), 4 * i + g + 1)
                    A.copy(ktok[i][0:n, 512 * g:512 * g + 512], banks[g][0:n, :]).then_inc(sem("kt_ev"), 1)

            def stick_logs(h):
                tmp = sb_tmp[h % 2]
                for kt in range(4):
                    c = slice(128 * kt, SEQ)
                    act.wait_ge(sem("sb_abs"), 4 * h + kt + 1)
                    link(f(tmp[:, kt, c], tmp[:, kt, c], ACT.Exp))
                    f(tmp[:, kt, c], tmp[:, kt, c], ACT.Ln, bias=1.0).then_inc(sem("sb_ln"), 1)

            stick_logs(0)
            for h in range(4):
                if h < 3:
                    stick_logs(h + 1)
                for n, kt in enumerate((3, 2, 1, 0)):
                    zm = sb_zm[h % 2][:, kt, 128 * kt:SEQ]
                    act.wait_ge(sem("sba_read"), 4 * h + n + 1)
                    f(zm, zm, ACT.Exp).then_inc(sem("sb_exp"), 1)
                act.wait_ge(sem("sbo_mm"), h + 1)
                o = 64 * (h % 2)
                A.copy(oT[o:o + 64, h // 2, 0:SEQ], banks[6 + h % 2][o:o + 64, :]).then_inc(sem("sbo_ev"), 1)

            def fox_rows(h):
                act.wait_ge(sem("nck_mm"), h + 1)
                if h >= 2:
                    act.wait_ge(sem("sc_ev"), 4 * (h - 1))
                A.copy(nck[:, h % 2, :], banks[6 + h % 2]).then_inc(sem("nck_ev"), 1)

            def weights(n):
                act.wait_ge(sem("mx_ready"), n + 1)
                s = sc_sb[:, n % 3, 0:units[n]["cols"]]
                f(s, s, ACT.Exp, bias=rowst[:, 1, n % 3:n % 3 + 1],
                  accum_out=rowst[:, 2, n % 3:n % 3 + 1]).then_inc(sem("ex"), 1)

            fox_rows(0)
            weights(0)
            weights(1)
            for n, u in enumerate(units):
                if n % 4 == 0 and n // 4 + 1 < NFOX:
                    fox_rows(n // 4 + 1)
                if n + 2 < NU:
                    weights(n + 2)
                for tg in range(u["tg0"], u["tg1"]):
                    if tg % 2:
                        group_out(act, n, tg, A.copy, "tg_evA")
                done = [n - 1] if n < NU - 1 else [n - 1, n]
                for m in done:
                    if m >= 0 and units[m]["i"] == 3:
                        v = units[m]
                        act.wait_ge(sem("pv_mm"), m + 1)
                        A.copy(oT[v["off"]:v["off"] + 64, v["tile"], 0:SEQ],
                               banks[4 + v["head"] % 2][v["off"]:v["off"] + 64, :]).then_inc(sem("o_ev"), 1)

            act.wait_ge(*done_at("new_abs"))
            link(f(s_lng[0:NT, :, 0:16], s_lng[0:NT, :, 0:16], ACT.Exp))
            f(s_lng[0:NT, :, 0:16], s_lng[0:NT, :, 0:16], ACT.Ln, bias=1.0).then_inc(sem("own_keys"), 1)
            act.wait_ge(*done_at("new_t"))
            f(wnew[:, :, 0:16], wnew[:, :, 0:16], ACT.Exp).then_inc(sem("own_keys"), 1)

            def stick_logs(i, b0):
                act.wait_ge(sem("z_abs"), i * 2 + (b0 + 1))
                link(f(s_y[:, 0:256], s_y[:, 0:256], ACT.Exp))
                f(s_y[:, 0:256], s_y[:, 0:256], ACT.Ln, bias=1.0).then_inc(sem("z_ln"), 1)

            def softmax_weights(i, b0):
                par = b0 % 2
                act.wait_ge(sem("f_sub"), i * 2 + (b0 + 1))
                f(s_f[:, par, :], s_f[:, par, :], ACT.Exp)
                f(s_dl[:, par, :], s_dl[:, par, :], ACT.Exp)
                f(s_wn[0:NT, par, 16:64], s_wn[0:NT, par, 16:64], ACT.Exp).then_inc(sem("f_exp"), 1)

            def stick_weights(i, b0):
                act.wait_ge(sem("t_ready"), i * 2 + (b0 + 1))
                f(s_w[:, b0 % 2, 0:256], s_z, ACT.Exp).then_inc(sem("w_ready"), 1)

            def rows_out(i, b0, q):
                act.wait_ge(sem("qk_mm"), i * 10 + (5 * b0 + q + 1))
                act.wait_ge(sem("sT_mm"), i * 12 + (6 * b0 + q))
                if q == 3:
                    A.copy(row_b, banks[4]).then_inc(sem("row_b"), 1)
                A.copy(row_a, banks[3]).then_inc(sem("row_a"), 1)

            def copy_out(i, b0, before):
                steps = {1: (stick_logs,), 9: (softmax_weights,), 11: (stick_weights,)} if before else {}
                for p in range(1, 18, 2):
                    keys_out(act, i, b0, p, A.copy)
                    if p in (5, 9, 13):
                        rows_out(i, b0, (p - 5) // 4)
                    for stage in steps.get(p, ()):
                        stage(i, b0 - 1)
                rows_out(i, b0, 3)
                rows_out(i, b0, 4)

            copy_out(0, 0, False)
            with act.Fori(0, NB // 2 - 1) as i:
                link.enter(i, 2)
                copy_out(i, 1, True)
                copy_out(i, 2, True)
                link.leave(NB // 2 - 1)
            copy_out(0, NB - 1, True)
            for stage in (stick_logs, softmax_weights, stick_weights):
                stage(0, NB - 1)

            for n in range(24):
                act.wait_ge(sem("gate_mm"), n + 1)
                if n >= 2:
                    act.wait_ge(sem("br_ev"), n - 1)
                f(as_halves(gsig[:, n % 2, :]), halves(2 * (n % 2)), ACT.Sigmoid).then_inc(sem("gate_ev"), 1)

            squares(sem("xo_ev"))
            norm_root(1)
            gain_and_shift(1, 24)

            def rows_out(i):
                n = P if i < 4 else 32
                if i >= 2:
                    act.wait_ge(sem(f"st_h{i % 2}"), 16 * (i // 2))
                for g in range(2):
                    act.wait_ge(sem("row_t"), 2 * i + g + 1)
                    A.copy(hrow[0:n, i % 2, 512 * g:512 * g + 512], banks[3 + g][0:n, :]).then_inc(sem("row_ev"), 1)

            rows_out(0)
            act.wait_ge(*done_at("rt_sub"))
            f(r_ge, r_ge, ACT.Exp).then_inc(sem("rt_act"), 1)
            rows_out(1)
            act.wait_ge(*done_at("rt_d"))
            f(r_w2, r_w2, ACT.Exp).then_inc(sem("rt_act"), 1)
            for i in range(2, 5):
                rows_out(i)

            def features_out(i, c0, slot):
                act.wait_ge(sem("xg_t"), i * RING + (c0 + 1))
                A.copy(xg[:, slot, 0:512], banks[0]).then_inc(sem("xg_evA"), 1)

            def gate_half(i, c0, slot):
                act.wait_ge(sem("h_mm"), i * RING + (c0 + 1))
                f(sil[:, slot, :], banks[2 + slot][:, 0:DE], ACT.Silu).then_inc(sem("sil_ready"), 1)

            def hidden_out(i, c0, slot):
                act.wait_ge(sem("hid_t"), i * RING + (c0 + 1))
                A.copy(hidT[:, slot, :], banks[5][:, 0:DE]).then_inc(sem("hidT_ev"), 1)

            def outputs_out(i, c0, slot):
                act.wait_ge(sem("y_mm"), i * 2 * RING + (2 * c0 + 1))
                act.wait_ge(sem(f"st_yc{slot}"), i * 16 + 16 * (c0 // RING))
                A.copy(ychunk[:, slot, 0:512], banks[6]).then_inc(sem("yc_evA"), 1)

            features_out(0, 0, 0)
            gate_half(0, 0, 0)
            features_out(0, 1, 1)
            hidden_out(0, 0, 0)
            with act.Fori(0, CHUNKS // RING - 1) as i:
                for c0 in range(1, 1 + RING):
                    gate_half(i, c0, c0 % RING)
                    outputs_out(i, c0 - 1, (c0 - 1) % RING)
                    features_out(i, c0 + 1, (c0 + 1) % RING)
                    hidden_out(i, c0, c0 % RING)
            for c in (CHUNKS - 2, CHUNKS - 1):
                gate_half(0, c, c % RING)
                outputs_out(0, c - 1, (c - 1) % RING)
                if c < CHUNKS - 1:
                    features_out(0, c + 1, (c + 1) % RING)
                hidden_out(0, c, c % RING)
            outputs_out(0, CHUNKS - 1, (CHUNKS - 1) % RING)

            squares(sem("x2_ev"))
            norm_root(2)
            for k in range(KD):
                act.wait_ge(sem("x_normed"), KD * 2 + k + 1)
                last = f(hT[:, k, :], hT[:, k, :], ACT.Copy, scale=vecT[:, 64 + k:65 + k])
            last.then_inc(sem("h_ready"), 1)
            for i in range(5):
                n = P if i < 4 else 32
                act.wait_ge(sem("yo_t"), 2 * i + 2)
                if i >= 2:
                    act.wait_ge(sem(f"st_y{i % 2}"), 16 * (i // 2))
                A.copy(ystage[0:n, i % 2, 512:1024], banks[1][0:n, :]).then_inc(sem("yo_evA"), 1)
                act.wait_ge(sem("yo_evA"), i + 1)
                act.wait_ge(sem("yo_evD"), i + 1)
                if i < 4:
                    dst = O["y_prompt"][0, 128 * i:128 * i + 128, :]
                else:
                    dst = O["y_sample"].rearrange("b t d -> (b t) d")
                act.dma_start(dst, ystage[0:n, i % 2, :]).then_inc(sem(f"st_y{i % 2}"), 16)

        @block.vector
        def _(dve):
            link = Chain(dve, sem("dve_own"))

            def tt(out, a, b, op):
                return V.tensor_tensor(out, a, b, op)

            def ts(out, a, s1, s2, op0, op1=None):
                if op1 is None:
                    return V.tensor_scalar(out, a, s1, None, op0)
                return V.tensor_scalar(out, a, s1, s2, op0, op1)

            def stt(out, a, s, b, op0, op1):
                return V.scalar_tensor_tensor(out=out, in0=a, scalar=s, in1=b, op0=op0, op1=op1)

            V.memset(eps_sb[:, :], EPS)
            V.memset(wr_sb[:, :, 20:32], 0.0)
            V.memset(cT, 0.0)
            V.memset(lf_one, 1.0)
            link(V.memset(qbd[:, :, :], 0.0))
            dve.wait_ge(*done_at("c_e"))
            link(ts(c_tmp[0:9, :], c_tmp[0:9, :], 1.0, None, ALU.add))
            link(V.reciprocal(c_tmp[0:9, :], c_tmp[0:9, :]))
            tt(c_tmp[0:9, :], c_tmp[0:9, :], c_raw[0:9, :], ALU.mult).then_inc(sem("c_steps"), 1)
            dve.wait_ge(*done_at("c_t"))
            V.tensor_copy(vecT[:, :], banks[7][:, 128:200])
            V.tensor_copy(cT[:, :, 0:9], banks[7][:, 0:72].rearrange("p (k n) -> p k n", n=9)).then_inc(sem("c_steps"), 1)
            dve.wait_ge(*done_at("cT_ready"))
            for k in range(1, KD, 2):
                dve.wait_ge(sem("x_t"), k + 1)
                V.tensor_copy(xT[:, k, 0:SEQ], banks[k % 4]).then_inc(sem("x_evD"), 1)
            dve.wait_ge(sem("x_t"), KD + 1)
            V.tensor_copy(xT[:, :, SEQ:TOK], banks[4][:, 0:256].rearrange("p (k n) -> p k n", n=32)
                          ).then_inc(sem("x_evD"), 1)

            dve.wait_ge(sem("ld_lf"), 16)
            for h in range(NFOX):
                last = V.tensor_tensor_scan(lf_scan[:, h, :], lf_one, lf_page[:, :, h], 0.0, ALU.mult, ALU.add)
            link(last)
            V.tensor_copy(lf_tot[:, 0, :], lf_scan[:, :, P - 1]).then_inc(sem("past_steps"), 1)
            dve.wait_ge(*done_at("lf_tot"))

            def mod_out(bank, j):
                parts4 = banks[bank].rearrange("p (j q n) -> p j n q", q=4, n=32)[:, :, 0:9, :]
                link(V.tensor_reduce(modT[:, j, :], parts4, AX, ALU.add))
                bm = vecT[:, j].unsqueeze(2).to_broadcast([P, 4, 9])
                return tt(modT[:, j, :], modT[:, j, :], bm, ALU.add)

            def gain(n, shift, norm):
                bn = vecT[:, norm:norm + 8].unsqueeze(2).to_broadcast([P, KD, 9])
                link(stt(gainA[:, :, :], modT[:, shift + 8:shift + 16, :], 1.0, bn, ALU.add, ALU.mult))

            def normed(n):
                dve.wait_ge(sem("rs"), n + 1)
                for k in range(KD):
                    tt(hT[:, k, :], xT[:, k, :], rstd[:, :], ALU.mult).then_inc(sem("x_normed"), 1)
                dve.wait_ge(sem("x_normed"), KD * (n + 1))

            def modulate(n, shift):
                normed(n)
                hs = hT[:, :, SEQ:TOK].rearrange("p k (b t) -> p k b t", t=NT)
                link(tt(hs, hs, gainA[:, :, 1:9].unsqueeze(3).to_broadcast([P, KD, NB, NT]), ALU.mult))
                tt(hs, hs, modT[:, shift:shift + 8, 1:9].unsqueeze(3).to_broadcast([P, KD, NB, NT]), ALU.add
                   ).then_inc(sem("h_ready"), 1)

            for c in range(6):
                dve.wait_ge(sem("mod_t"), c + 1)
                mod_out(c % 3, slice(4 * c, 4 * c + 4)).then_inc(sem("mod_ev"), 1)
            dve.wait_ge(sem("mod_ev"), 6)
            gain(0, 0, 48)
            modulate(0, 0)

            with dve.Fori(0, 2) as i:
                link.enter(i, 3)
                for u in range(3):
                    dve.wait_ge(sem("mod_t"), i * 3 + (7 + u))
                    mod_out(4 + u, bass.ds(i * 12 + (24 + 4 * u), 4)).then_inc(sem("mod_ev"), 1)
                link.leave(2)

            dve.wait_ge(*done_at("f_mm"))
            dve.wait_ge(sem("ld_f"), 32)
            y, ya, yl = fscr[0:NFOX, 0, :], fscr[0:NFOX, 1, :], fscr[0:NFOX, 3, :]
            link(ts(as_halves(y), halves(4, NFOX), bf_sb[:, 0:1], None, ALU.add))
            stt(ya, y, -1.0, y, ALU.mult, ALU.min).then_inc(sem("f_steps"), 1)
            dve.wait_ge(*done_at("f_ln"))
            link(stt(logfT[0:NFOX, :], y, 0.0, yl, ALU.min, ALU.subtract))
            link(V.memset(ya, 1.0))
            V.tensor_tensor_scan(ncumT[0:NFOX, 0:SEQ], ya[:, 0:SEQ], logfT[0:NFOX, 0:SEQ], 0.0, ALU.mult, ALU.subtract)
            lfs = logfT[0:NFOX, SEQ:TOK].rearrange("p (b t) -> p b t", t=NT)
            ncs = ncumT[0:NFOX, SEQ:TOK].rearrange("p (b t) -> p b t", t=NT)
            last = link(ts(ncs[:, :, 0], lfs[:, :, 0], -1.0, None, ALU.mult))
            for t in range(1, NT):
                last = tt(ncs[:, :, t], ncs[:, :, t - 1], lfs[:, :, t], ALU.subtract)
                if t < NT - 1:
                    link(last)
            last.then_inc(sem("forget_rows"), 1)
            dve.wait_ge(*done_at("lf_rowT"))

            dve.wait_ge(*done_at("lf_late"))
            link(tt(lf_tot[:, 1, :], lf_tot[:, 0, :], banks[7][:, 0:NFOX], ALU.add))
            for h in range(NFOX):
                last = ts(lf_scan[:, h, :], lf_scan[:, h, :], -1.0, lf_tot[:, 1, h:h + 1], ALU.mult, ALU.add)
            last.then_inc(sem("past_steps"), 1)

            dve.wait_ge(*done_at("lf_tr"))
            V.tensor_copy(fox_past[:, :, 0:4].rearrange("p a h -> p h a"),
                          banks[0].rearrange("p (h a) -> p h a", h=4))
            V.tensor_copy(fox_past[:, :, 4:6].rearrange("p a h -> p h a"),
                          banks[1][:, 0:256].rearrange("p (h a) -> p h a", h=2)).then_inc(sem("past_steps"), 1)
            dve.wait_ge(*done_at("lf_rowt"))
            V.tensor_copy(lf_tok[:, 0:4, :], banks[6][:, 0:24].rearrange("p (i h) -> p i h", h=6))
            V.tensor_copy(lf_tok[0:32, 4, :], banks[6][0:32, 24:30])
            V.tensor_copy(ncn[:, :], banks[6][0:32, 32:38]).then_inc(sem("forget_rows"), 1)

            dve.wait_ge(sem("z_ev"), 24)
            for j, tile in enumerate(PAIR_TILES):
                for hh in range(2):
                    r = slice(64 * hh, 64 * hh + 64)
                    V.tensor_copy(qbd[r, :, 8 * j + 4 * hh:8 * j + 4 * hh + 4],
                                  zT[r, tile, SEQ:TOK].rearrange("p (b t) -> p b t", t=NT))
            for g in range(3):
                for hh in range(2):
                    r = slice(64 * hh, 64 * hh + 64)
                    last = V.tensor_copy(qbd[r, :, 40 + 8 * g + hh:48 + 8 * g:2],
                                         zT[r, 2 + g, SEQ:TOK].rearrange("p (b t) -> p b t", t=NT))
            last.then_inc(sem("qbd_ready"), 1)

            for i in range(5):
                n = P if i < 4 else 32
                for g in range(2):
                    dve.wait_ge(sem("kv_t"), 4 * i + g + 3)
                    V.tensor_copy(vtok[0:n, i, 512 * g:512 * g + 512], banks[2 + g][0:n, :]
                                  ).then_inc(sem("vt_ev"), 1)

            def stick_scores(h):
                zm, tmp = sb_zm[h % 2], sb_tmp[h % 2]
                if h >= 2:
                    dve.wait_ge(sem("sbo_mm"), h - 1)
                for kt in range(4):
                    c = slice(128 * kt, SEQ)
                    dve.wait_ge(sem("sbz_mm"), 4 * h + kt + 1)
                    ts(zm[:, kt, c], banks[kt][:, c], SCALE, None, ALU.mult).then_inc(sem("sbz_read"), 1)
                    dve.wait_ge(sem("sbz_read"), 4 * h + kt + 1)
                    stt(tmp[:, kt, c], zm[:, kt, c], -1.0, zm[:, kt, c], ALU.mult, ALU.min
                        ).then_inc(sem("sb_abs"), 1)

            stick_scores(0)
            for h in range(4):
                if h < 3:
                    stick_scores(h + 1)
                spl, zm, tmp = sb_sp[h % 2], sb_zm[h % 2], sb_tmp[h % 2]
                for kt in range(4):
                    c, dg = slice(128 * kt, SEQ), slice(128 * kt, 128 * kt + 128)
                    dve.wait_ge(sem("sb_ln"), 4 * h + kt + 1)
                    link(stt(spl[:, kt, c], zm[:, kt, c], 0.0, tmp[:, kt, c], ALU.max, ALU.add))
                    link(tt(zm[:, kt, c], zm[:, kt, c], spl[:, kt, c], ALU.subtract))
                    last = tt(spl[:, kt, dg], spl[:, kt, dg], cs["strict_mul"], ALU.mult)
                last.then_inc(sem("sbsp"), 1)
                for n, kt in enumerate((3, 2, 1, 0)):
                    c = slice(128 * kt, SEQ)
                    dve.wait_ge(sem("sba_mm"), 4 * h + n + 1)
                    tt(zm[:, kt, c], zm[:, kt, c], banks[4 + n % 2][:, c], ALU.subtract
                       ).then_inc(sem("sba_read"), 1)
                for n, kt in enumerate((3, 2, 1, 0)):
                    dg = slice(128 * kt, 128 * kt + 128)
                    dve.wait_ge(sem("sb_exp"), 4 * h + n + 1)
                    last = tt(zm[:, kt, dg], zm[:, kt, dg], cs["strict_mul"], ALU.mult)
                last.then_inc(sem("sbw"), 1)

            dve.wait_ge(sem("ld_dt"), 16 * 7)
            dve.wait_ge(sem("sbo_mm"), 4)
            tab_at = {}
            k = 0
            for hh in range(2):
                for g in range(3):
                    tab_at[g, hh] = (k, DIL_COLS[g])
                    k += DIL_COLS[g]

            def logits(n):
                u = units[n]
                sc = sc_sb[:, n % 3, :]
                if n >= 3:
                    dve.wait_ge(sem("tg_mm"), units[n - 3]["tg1"])
                for s, (tile, k0, cols, at) in enumerate(u["subs"]):
                    c = u["sub0"] + s
                    dve.wait_ge(sem("sc_mm"), c + 1)
                    if u["kind"] == "fox":
                        dve.wait_ge(sem("nck_ev"), u["h"] + 1)
                        bias = nck[:, u["h"] % 2, 0:cols]
                    else:
                        t0, tn = tab_at[s, u["h"]]
                        bias = dil_tab[:, t0 + tn - cols:t0 + tn]
                    stt(sc[:, at:at + cols], banks[c % 2][:, 0:cols], SCALE, bias, ALU.mult, ALU.add
                        ).then_inc(sem("sc_ev"), 1)
                dve.wait_ge(sem("sc_ev"), u["sub1"])
                n_ = u["cols"]
                if u["kind"] == "fox":
                    link(tt(sc[:, n_ - 128:n_], sc[:, n_ - 128:n_], cs["causal_add"], ALU.add))
                V.tensor_reduce(rowst[:, 1, n % 3:n % 3 + 1], sc[:, 0:n_], AX, ALU.max, negate=True
                                ).then_inc(sem("mx_ready"), 1)

            logits(0)
            logits(1)
            for n, u in enumerate(units):
                dve.wait_ge(sem("ex"), n + 1)
                if n >= 3:
                    dve.wait_ge(sem("nrm"), n - 2)
                V.reciprocal(rowst[:, 3, n % 3:n % 3 + 1], rowst[:, 2, n % 3:n % 3 + 1]).then_inc(sem("rs_ready"), 1)
                if n + 2 < NU:
                    logits(n + 2)
                for tg in range(u["tg0"], u["tg1"]):
                    if tg % 2 == 0:
                        group_out(dve, n, tg, V.tensor_copy, "tg_evD")

            dve.wait_ge(*done_at("new_mm"))
            dve.wait_ge(sem("ld_nc"), 16)
            dve.wait_ge(sem("pv_mm"), NU)
            nv = banks[0][0:NT, :].rearrange("p (b n) -> p b n", n=64)
            link(ts(wnew[:, :, 0:16], nv[:, :, 0:16], SCALE, None, ALU.mult))
            stt(s_lng[0:NT, :, 0:16], wnew[:, :, 0:16], -1.0, wnew[:, :, 0:16], ALU.mult, ALU.min
                ).then_inc(sem("own_keys"), 1)
            link(stt(wnew[:, :, 16:64], nv[:, :, 16:64], SCALE,
                     cs["new_add"][0:NT, 16:64].unsqueeze(1).to_broadcast([NT, NB, 48]), ALU.mult, ALU.add))
            fx = wnew[:, :, 16:40].rearrange("p b (h t) -> p b h t", t=NT)
            link(tt(fx, fx, lfnew[:, :, :].unsqueeze(3).to_broadcast([NT, NB, NFOX, NT]), ALU.add))
            V.tensor_copy(mnew[:, :, 0:24], wnew[:, :, 16:40])
            V.tensor_reduce(mnew[:, :, 24:32], wnew[:, :, 40:64].rearrange("p b (g c) -> p b c g", g=3), AX, ALU.max)
            dve.wait_ge(*done_at("new_ln"))
            link(stt(spnew[:, :, :], wnew[:, :, 0:16], 0.0, s_lng[0:NT, :, 0:16], ALU.max, ALU.add))
            link(tt(wnew[:, :, 0:16], wnew[:, :, 0:16], spnew[:, :, :], ALU.subtract))
            strict = cs["new_strict"][0:NT, :].unsqueeze(1).to_broadcast([NT, NB, 16])
            tt(spnew[:, :, :], spnew[:, :, :], strict, ALU.mult).then_inc(sem("own_keys"), 1)
            dve.wait_ge(*done_at("new_a"))
            tt(wnew[:, :, 0:16], wnew[:, :, 0:16], banks[1][0:NT, 0:128].rearrange("p (b n) -> p b n", n=16),
               ALU.subtract).then_inc(sem("own_keys"), 1)
            dve.wait_ge(*done_at("new_exp"))
            tt(wnew[:, :, 0:16], wnew[:, :, 0:16], strict, ALU.mult).then_inc(sem("own_keys"), 1)
            dve.wait_ge(*done_at("new_ready"))

            def take(i, b0):
                par = b0 % 2
                b = i * 2 + b0
                V.tensor_copy(qcur[:, par, :, 0:8], qbd[:, bass.ds(b, 1), :].rearrange("p o (j n) -> p (o j) n", n=8)
                              ).then_inc(sem("qcur"), 1)
                V.tensor_copy(s_sn[0:NT, par, :], spnew[:, bass.ds(b, 1), :].rearrange("p o n -> p (o n)"))
                link(V.tensor_copy(s_wn[0:NT, par, :], wnew[:, bass.ds(b, 1), :].rearrange("p o n -> p (o n)")))

            def read_scores(i, b0, n):
                par = b0 % 2
                dve.wait_ge(sem("sT_mm"), i * 12 + (6 * b0 + n + 1))
                v = banks[5].rearrange("p (b j c) -> p b j c", j=4, c=32)
                if n < 4:
                    ts(s_w[:, par, 64 * n:64 * n + 64].rearrange("p (b j c) -> p b j c", j=2, c=8),
                       v[:, :, 0:2, 0:8], SCALE, None, ALU.mult)
                    last = ts(s_f[:, par, 96 * n:96 * n + 96].rearrange("p (b j c) -> p b j c", j=3, c=8)[:, :, 0:2],
                              v[:, :, 2:4, 0:8], SCALE, None, ALU.mult)
                elif n == 4:
                    f4 = s_f[:, par, :].rearrange("p (q b c) -> p b q c", q=4, c=24)
                    last = ts(f4[:, :, :, 16:24], v[:, :, :, 0:8], SCALE, None, ALU.mult)
                else:
                    bias = cs["dil_past"]
                    last = stt(s_dl[:, par, 0:8], banks[5][:, 0:8], SCALE, bias[:, 0:8], ALU.mult, ALU.add)
                    for g in (1, 2):
                        for hh in range(2):
                            a = 32 * g + hh
                            c = slice(8 * g + hh, 8 * g + 8, 2)
                            last = stt(s_dl[:, par, c], banks[5][:, a:a + 391:130], SCALE, bias[:, c],
                                       ALU.mult, ALU.add)
                last.then_inc(sem("s_read"), 1)

            def start_softmax(i, b0):
                par = b0 % 2
                dve.wait_ge(sem("s_read"), i * 12 + (6 * b0 + 6))
                z = s_w[:, par, 0:256]
                stt(s_y[:, 0:256], z, -1.0, z, ALU.mult, ALU.min).then_inc(sem("z_abs"), 1)
                f4 = s_f[:, par, :].rearrange("p (a h t) -> p a h t", h=NFOX, t=NT)
                past = fox_past[:, bass.ds(i * 32 + 16 * b0, 16), :].unsqueeze(3).to_broadcast([P, PAGES, NFOX, NT])
                link(tt(f4, f4, past, ALU.add))
                V.tensor_reduce(s_m[:, par, 0:24], s_f[:, par, :].rearrange("p (a c) -> p c a", c=24), AX, ALU.max)
                link(V.tensor_reduce(s_m[:, par, 24:32], s_dl[:, par, :].rearrange("p (g c) -> p c g", g=3),
                                     AX, ALU.max))
                tt(s_m[0:NT, par, :], s_m[0:NT, par, :],
                   mnew[:, bass.ds(i * 2 + b0, 1), :].rearrange("p o n -> p (o n)"), ALU.max
                   ).then_inc(sem("m_ready"), 1)

            def softplus(i, b0):
                z = s_w[:, b0 % 2, 0:256]
                dve.wait_ge(sem("z_ln"), i * 2 + (b0 + 1))
                link(stt(s_sp[:, 0:256], z, 0.0, s_y[:, 0:256], ALU.max, ALU.add))
                tt(s_z, z, s_sp[:, 0:256], ALU.subtract).then_inc(sem("sp_ready"), 1)

            def top(i, b0):
                par = b0 % 2
                dve.wait_ge(sem("m_t"), i * 2 + (b0 + 1))
                link(V.tensor_reduce(s_mx[0:32, par, :], banks[6][0:32, 0:128], AX, ALU.max))
                ts(s_dg[0:32, par, :], ident[0:32, 0:32], s_mx[0:32, par, 0:1], None, ALU.mult
                   ).then_inc(sem("dg_ready"), 1)

            def less_top(i, b0):
                par = b0 % 2
                dve.wait_ge(sem("m_b"), i * 2 + (b0 + 1))
                f = s_f[:, par, :].rearrange("p (a c) -> p a c", c=24)
                tt(f, f, banks[6][:, 128:152].unsqueeze(1).to_broadcast([P, PAGES, 24]), ALU.subtract)
                d = s_dl[:, par, :].rearrange("p (g c) -> p g c", g=3)
                tt(d, d, banks[6][:, 152:160].unsqueeze(1).to_broadcast([P, 3, 8]), ALU.subtract)
                w = s_wn[0:NT, par, :]
                tt(w[:, 16:40], w[:, 16:40], banks[6][0:NT, 128:152], ALU.subtract)
                w = w[:, 40:64].rearrange("p (g c) -> p g c", g=3)
                tt(w, w, banks[6][0:NT, 152:160].unsqueeze(1).to_broadcast([NT, 3, 8]), ALU.subtract
                   ).then_inc(sem("f_sub"), 1)

            def row_sums(i, b0):
                par = b0 % 2
                dve.wait_ge(sem("f_exp"), i * 2 + (b0 + 1))
                V.tensor_copy(s_dx[:, 2 * par:2 * par + 2, :].rearrange("p g (t c) -> p g t c", c=10)[:, :, :, 0:2],
                              s_dl[:, par, 8:24].rearrange("p (g t h) -> p g t h", g=2, h=2))
                V.tensor_reduce(s_r[:, par, 0:24], s_f[:, par, :].rearrange("p (a c) -> p c a", c=24), AX, ALU.add)
                V.tensor_reduce(s_r[:, par, 24:32], s_dl[:, par, :].rearrange("p (g c) -> p c g", g=3), AX, ALU.add)
                V.tensor_copy(s_rn[0:NT, par, 0:24], s_wn[0:NT, par, 16:40])
                V.tensor_reduce(s_rn[0:NT, par, 24:32], s_wn[0:NT, par, 40:64].rearrange("p (g c) -> p c g", g=3),
                                AX, ALU.add).then_inc(sem("r_ready"), 1)

            def less_sticks(i, b0):
                dve.wait_ge(sem("a_mm"), i * 2 + (b0 + 1))
                tt(s_z, s_z, banks[6][:, 192:448], ALU.subtract).then_inc(sem("t_ready"), 1)

            def inverse(i, b0):
                dve.wait_ge(sem("l_mm"), i * 2 + (b0 + 1))
                link(V.reciprocal(s_li[:, b0 % 2, :], banks[6][:, 160:192]))

            def output_rows(i, b0):
                dve.wait_ge(sem("seq_pv"), i * 2 + (b0 + 1))
                V.tensor_copy(s_o, banks[7][:, 0:384]).then_inc(sem("o_rows"), 1)

            def write_out(i, b0):
                par = b0 % 2
                dve.wait_ge(sem("oT_mm"), i * 2 + (b0 + 1))
                c = bass.ds(i * 8 + (SEQ + 4 * b0), NT)
                for hh in range(2):
                    r = slice(64 * hh, 64 * hh + 64)
                    pair = banks[5][r, 0:128].rearrange("p (j n) -> p j n", n=32)[:, :, 4 * hh:4 * hh + 4]
                    V.tensor_copy(oT[r, 0:2, c], pair[:, 0:2])
                    li = s_li[r, par, 0:24].rearrange("p (j n) -> p j n", n=8)[:, :, 4 * hh:4 * hh + 4]
                    tt(oT[r, 3:5, c], pair[:, 2:4], li[:, 0:2], ALU.mult)
                    tt(oT[r, 5, c], banks[5][r, 128 + 4 * hh:132 + 4 * hh], li[:, 2], ALU.mult)
                    last = tt(oT[r, 2, c], banks[5][r, 136 + hh:144:2], s_li[r, par, 24 + hh:32:2], ALU.mult)
                last.then_inc(sem("seq_out"), 1)

            def fifth_out(i, b0, g):
                dve.wait_ge(sem("kT_mm"), i * 36 + (18 * b0 + min(4 * g + 4, 18)))
                dve.wait_ge(sem("qk_mm"), i * 10 + (5 * b0 + g))
                if g < 4:
                    V.tensor_copy(kT5[:, 4, :], banks[2]).then_inc(sem("kT5_ev"), 1)
                else:
                    V.tensor_copy(kT5[:, 2, 0:128], banks[2][:, 0:128]).then_inc(sem("kT5_ev"), 1)

            def sequence(i, b0, before):
                steps = {2: (softplus,), 4: (top,), 8: (less_top,), 10: (less_sticks, row_sums),
                         14: (inverse,)} if before else {}
                for p in range(0, 18, 2):
                    keys_out(dve, i, b0, p, V.tensor_copy)
                    if p == 0:
                        take(i, b0)
                        if before:
                            start_softmax(i, b0 - 1)
                    if p in (2, 6, 10, 14):
                        fifth_out(i, b0, p // 4)
                    if p in (6, 10, 14):
                        read_scores(i, b0, (p - 6) // 4)
                    for stage in steps.get(p, ()):
                        stage(i, b0 - 1)
                fifth_out(i, b0, 4)
                read_scores(i, b0, 3)
                if before:
                    output_rows(i, b0 - 1)
                read_scores(i, b0, 4)
                read_scores(i, b0, 5)
                if before:
                    write_out(i, b0 - 1)

            dve.wait_ge(sem("nck_ev"), NFOX)
            dve.wait_ge(sem("st_k"), 16 * KV_STORES)
            dve.wait_ge(sem("st_smp"), 16 * SAMPLE_STORES)
            V.memset(qcur, 0.0)
            V.memset(s_dx, 0.0)
            link(V.memset(banks[7], 0.0))
            V.memset(s_o[0:1, 0:1], 0.0).then_inc(sem("o_zero"), 1)
            sequence(0, 0, False)
            with dve.Fori(0, NB // 2 - 1) as i:
                link.enter(i, 12)
                sequence(i, 1, True)
                sequence(i, 2, True)
                link.leave(NB // 2 - 1)
            sequence(0, NB - 1, True)
            for stage in (start_softmax, softplus, top, less_top, less_sticks, row_sums, inverse, output_rows, write_out):
                stage(0, NB - 1)

            for n in range(24):
                half, b, j = n // 12, (n // 4) % 3, n % 4
                m = 4 * half + j
                dve.wait_ge(sem("gate_ev"), n + 1)
                out = merged[:, m, :] if b == 0 else btmp[:, n % 2, :]
                last = tt(as_halves(out), as_halves(gsig[:, n % 2, :]), halves(4 + 2 * (n % 2)), ALU.mult)
                if b:
                    link(last)
                    last = tt(merged[:, m, :], merged[:, m, :], btmp[:, n % 2, :], ALU.add)
                last.then_inc(sem("br_ev"), 1)

            def add_gated(m, gate, prompt, smp):
                lo = 0
                for part in prompt:
                    c = slice(lo, lo + part.shape[-1])
                    stt(xT[:, m, c], part, modT[:, gate + m, 0:1], xT[:, m, c], ALU.mult, ALU.add)
                    lo = c.stop
                g = modT[:, gate + m, 1:9].unsqueeze(2).to_broadcast([P, NB, NT])
                link(tt(upd_s[:, m, :].rearrange("p (b t) -> p b t", t=NT),
                        smp.rearrange("p (b t) -> p b t", t=NT), g, ALU.mult))
                return tt(xT[:, m, SEQ:TOK], xT[:, m, SEQ:TOK], upd_s[:, m, :], ALU.add)

            for m in range(KD):
                dve.wait_ge(sem("xo_mm"), m + 1)
                b = 2 * (m % 2)
                add_gated(m, 16, (banks[b][:, 0:HALF], banks[b + 1][:, 0:SEQ - HALF]), banks[b + 1][:, SEQ - HALF:HALF]
                          ).then_inc(sem("xo_ev"), 1)
            dve.wait_ge(sem("xo_ev"), 8)
            gain(1, 24, 56)
            modulate(1, 24)

            dve.wait_ge(sem("ld_r"), 64)
            link(V.memset(r_lg, 0.0))
            dve.wait_ge(*done_at("rt_part"))
            V.tensor_copy(as_halves(lg_rows), halves(0)).then_inc(sem("routing"), 1)
            dve.wait_ge(*done_at("rt_mm"))
            v = banks[2].rearrange("p (i q n) -> p i n q", q=4, n=32)[:, :, 0:20, :]
            link(V.tensor_reduce(r_lg[:, 0:4, :], v, AX, ALU.add))
            v = banks[5][0:32, 0:128].rearrange("p (q n) -> p n q", q=4)[:, 0:20, :]
            link(V.tensor_reduce(r_lg[0:32, 4, :], v, AX, ALU.add))
            link(tt(r_lg, r_lg, br_sb[:, :].unsqueeze(1).to_broadcast([P, 5, 20]), ALU.add))

            def wide(a):
                return a.unsqueeze(2).to_broadcast([P, 5, 4])

            count4 = cs["count4"].rearrange("p (i n) -> p i n", n=4)

            def first_max(val, mx, oh):
                link(V.tensor_reduce(mx, val, AX, ALU.max))
                link(tt(r_t, val, wide(mx), ALU.is_ge))
                link(stt(r_t, r_t, -100.0, count4, ALU.mult, ALU.add))
                link(V.tensor_reduce(r_g1, r_t, AX, ALU.min))
                link(tt(oh, r_t, wide(r_g1), ALU.is_equal))

            gl = r_lg[:, :, 0:4]
            first_max(gl, r_m, r_oh)
            tt(r_ge, gl, wide(r_m), ALU.subtract).then_inc(sem("rt_dve"), 1)
            ohe = r_oh.unsqueeze(2).to_broadcast([P, 5, 4, 4])
            link(tt(r_pr, r_lg[:, :, 4:20].rearrange("p i (g e) -> p i e g", g=4), ohe, ALU.mult))
            link(V.tensor_reduce(r_es, r_pr, AX, ALU.add))
            first_max(r_es, r_m1, r_oh1)
            link(stt(r_es, r_oh1, NEG, r_es, ALU.mult, ALU.add))
            first_max(r_es, r_m2, r_oh2)
            tt(r_w2, r_m2, r_m1, ALU.subtract).then_inc(sem("rt_dve"), 1)
            for k, oh in enumerate((r_oh1, r_oh2)):
                last = tt(r_a[:, k].rearrange("p i (g e) -> p i g e", g=4),
                          r_oh.unsqueeze(3).to_broadcast([P, 5, 4, 4]),
                          oh.unsqueeze(2).to_broadcast([P, 5, 4, 4]), ALU.mult)
            link(last)
            link(tt(r_b, r_a[:, 0], r_a[:, 1], ALU.add))
            V.memset(r_b[32:64, 4, :], 0.0)
            V.memset(r_b[64:128, 4, :], 0.0).then_inc(sem("routing"), 1)
            dve.wait_ge(*done_at("rt_exp"))
            link(V.tensor_reduce(r_gg, r_ge, AX, ALU.add))
            dve.wait_ge(*done_at("rt_dexp"))
            link(stt(r_gg, r_w2, 1.0, r_gg, ALU.add, ALU.mult))
            link(V.reciprocal(r_g1, r_gg))
            link(tt(r_w2, r_w2, r_g1, ALU.mult))
            dve.wait_ge(sem("ld_mi"), 16)
            V.memset(slot_t, 0.0)
            link(V.memset(pay, 0.0))
            py = pay.rearrange("p (i k) n -> p i k n", k=TOP)
            for k, g in enumerate((r_g1, r_w2)):
                V.tensor_copy(py[:, :, k, 0], moe_ids[:, 0:5])
                ts(py[:, :, k, 1], moe_ids[:, 0:5], 2.0, float(k), ALU.mult, ALU.add)
                last = V.tensor_copy(py[:, :, k, 2], g)
            dve.wait_ge(*done_at("rank_mm"))
            V.memset(r_tot[:, 0, :], 0.0)
            link(V.memset(r_n, 0.0))
            for i in range(5):
                link(tt(r_tot[:, i + 1, :], r_tot[:, i, :], banks[1][:, 80 + 16 * i:96 + 16 * i], ALU.add))
            for j in range(-(-TOK // P)):
                link(stt(r_n, r_tot[:, 5, :], float(P * j), r_n, ALU.is_gt, ALU.add))
            link(V.tensor_tensor_scan(r_end, ones[:, 0:NEXP], r_n, 0.0, ALU.mult, ALU.add))
            link(tt(r_st, r_end, r_n, ALU.subtract))
            link(stt(r_sb, r_st.unsqueeze(1).to_broadcast([P, 5, NEXP]), float(P), r_tot[:, 0:5, :],
                     ALU.mult, ALU.add))
            link(tt(r_sb, r_sb, banks[1][:, 0:80].rearrange("p (i e) -> p i e", e=NEXP), ALU.add))
            for k in range(TOP):
                link(tt(r_sel, r_a[:, k], r_sb, ALU.mult))
                link(V.tensor_reduce(r_dest[:, :, k], r_sel, AX, ALU.add))
            V.tensor_copy(dest_i, r_dest.rearrange("p i k -> p (i k)")).then_inc(sem("routing"), 1)
            link(tt(r_cmp[0:1], r_end[0:1].unsqueeze(1).to_broadcast([1, CHUNKS, NEXP]),
                    moe_ids[0:1, 5:].unsqueeze(2).to_broadcast([1, CHUNKS, NEXP]), ALU.is_le))
            link(V.tensor_reduce(r_eid[0:1], r_cmp[0:1], AX, ALU.add))
            link(ts(r_eid[0:1], r_eid[0:1], float(NEXP - 1), None, ALU.min))
            V.tensor_copy(exp_id[0:1], r_eid[0:1]).then_inc(sem("routing"), 1)
            dve.wait_ge(sem("ld_slot"), 16)

            def tokens(i, c0, slot):
                V.tensor_copy(tok_now[:, slot:slot + 1], slot_t[:, bass.ds(i * RING + c0, 1), 0]
                              ).then_inc(sem("tok_ready"), 1)

            def features_out(i, c0, slot):
                dve.wait_ge(sem("xg_t"), i * RING + (c0 + 1))
                V.tensor_copy(xg[:, slot, 512:1024], banks[1]).then_inc(sem("xg_evD"), 1)

            def gated(i, c0, slot):
                link(V.tensor_copy(gate_now[:, slot:slot + 1],
                                   slot_t[:, bass.ds(i * RING + c0, 1), 2]))
                dve.wait_ge(sem("sil_ready"), i * RING + (c0 + 1))
                stt(hidr[:, slot, :], banks[2 + slot][:, DE:2 * DE], gate_now[:, slot:slot + 1], sil[:, slot, :],
                    ALU.mult, ALU.mult).then_inc(sem("hid_ready"), 1)

            def outputs_out(i, c0, slot):
                dve.wait_ge(sem("y_mm"), i * 2 * RING + (2 * c0 + 2))
                dve.wait_ge(sem(f"st_yc{slot}"), i * 16 + 16 * (c0 // RING))
                link(V.tensor_copy(row_now[:, slot:slot + 1], slot_t[:, bass.ds(i * RING + c0, 1), 1]))
                V.tensor_copy(ychunk[:, slot, 512:1024], banks[7]).then_inc(sem("yc_evD"), 1)

            for c in range(RING):
                tokens(0, c, c)
            features_out(0, 0, 0)
            tokens(0, 3, 0)
            gated(0, 0, 0)
            features_out(0, 1, 1)
            tokens(0, 4, 1)
            with dve.Fori(0, CHUNKS // RING - 1) as i:
                link.enter(i, 2 * RING)
                for c0 in range(1, 1 + RING):
                    gated(i, c0, c0 % RING)
                    outputs_out(i, c0 - 1, (c0 - 1) % RING)
                    features_out(i, c0 + 1, (c0 + 1) % RING)
                    tokens(i, c0 + 4, (c0 + 1) % RING)
                link.leave(CHUNKS // RING - 1)
            for c in (CHUNKS - 2, CHUNKS - 1):
                gated(0, c, c % RING)
                outputs_out(0, c - 1, (c - 1) % RING)
                if c < CHUNKS - 1:
                    features_out(0, c + 1, (c + 1) % RING)
            outputs_out(0, CHUNKS - 1, (CHUNKS - 1) % RING)

            for i in range(5):
                n = P if i < 4 else 32
                dve.wait_ge(sem(f"ld_y{i % RING}"), 16 * (i // RING + 1))
                tt(yrow[0:n, i, 0:D], yrow[0:n, i, 0:D], yrow[0:n, i, D:2 * D], ALU.add).then_inc(sem("ysum"), 1)
            for m in range(KD):
                dve.wait_ge(sem("yt_t"), m + 1)
                b = 2 * (m % 2)
                add_gated(m, 40, (banks[b],), banks[b + 1][:, 0:32]).then_inc(sem("x2_ev"), 1)
            dve.wait_ge(sem("x2_ev"), KD)

            normed(2)
            for i in range(5):
                n = P if i < 4 else 32
                dve.wait_ge(sem("yo_t"), 2 * i + 1)
                if i >= 2:
                    dve.wait_ge(sem(f"st_y{i % 2}"), 16 * (i // 2))
                V.tensor_copy(ystage[0:n, i % 2, 0:512], banks[0][0:n, :]).then_inc(sem("yo_evD"), 1)


_OUTS = [("y_prompt", (1, SEQ, D)), ("y_sample", (NB, NT, D)),
         ("kv_prompt", (1, 1, SEQ, 2, 10, HD)), ("logf_prompt", (1, 1, SEQ, NFOX)),
         ("dil1_prompt", (1, 1, 128, 2, 2, HD)), ("dil2_prompt", (1, 1, 512, 2, 2, HD)),
         ("dil3_prompt", (1, 1, 512, 2, 2, HD)),
         ("kv_sample", (NB, 1, NT, 2, 10, HD)), ("logf_sample", (NB, 1, NT, NFOX)),
         ("dil1_sample", (NB, 1, 128, 2, 2, HD)), ("dil2_sample", (NB, 1, 512, 2, 2, HD)),
         ("dil3_sample", (NB, 1, 2048, 2, 2, HD))]


def program(nc, arrays):
    ins = {n: nc.dram_tensor(f"in_{n}", a.shape, mybir.dt.from_np(a.dtype), kind="ExternalInput").ap()
           for n, a in arrays.items()}
    outs = {n: nc.dram_tensor(f"out_{n}", s, F32, kind="ExternalOutput").ap() for n, s in _OUTS}
    trunk_kernel(nc, ins, outs)


def kernel(**inputs):
    import concourse.bacc as _bacc
    from concourse.bass_utils import run_bass_kernel_spmd as _run

    nc = _bacc.Bacc("TRN2", target_bir_lowering=False, num_devices=1)
    arrays = {n: np.ascontiguousarray(a) for n, a in inputs.items()}
    arrays["const"] = const_table()[1]
    program(nc, arrays)
    r = _run(nc, [{f"in_{n}": a for n, a in arrays.items()}], core_ids=[0])
    return tuple(r.results[0][f"out_{n}"] for n, _ in _OUTS)
```
